# Optimizing a Trainium2 kernel written in Bass

```python
import jax, jax.numpy as jnp
from jax import lax
import numpy as np

D_MODEL = 1024
BATCH = 1
SEQ = 512
DEPTH = 2

N_A_LAYERS = DEPTH // 2
N_B_LAYERS = DEPTH - N_A_LAYERS
HEAD_DIM = 64
RWKV_HEADS = D_MODEL // HEAD_DIM
D_DECAY_LORA = max(32, int(round(1.8 * D_MODEL ** 0.5 / 32)) * 32)
D_AAA_LORA = max(32, int(round(1.8 * D_MODEL ** 0.5 / 32)) * 32)
D_MV_LORA = max(32, int(round(1.3 * D_MODEL ** 0.5 / 32)) * 32)
D_GATE_LORA = max(32, int(round(0.6 * D_MODEL ** 0.8 / 32)) * 32)
GN_EPS = 64e-5
N_Q_HEADS = D_MODEL // HEAD_DIM
N_KV_HEADS = 2
GROUP = N_Q_HEADS // N_KV_HEADS
WINDOW = 128
BLOCK = WINDOW
FFN_DIM = 4 * D_MODEL
RMS_EPS = 1e-6


def rms_norm(x, g):
    xf = x.astype(jnp.float32)
    y = xf * lax.rsqrt(jnp.mean(xf * xf, axis=-1, keepdims=True) + RMS_EPS)
    return (y * g.astype(jnp.float32)).astype(x.dtype)

def squared_relu_mlp(h, w1, w2):
    return jnp.square(jax.nn.relu(h @ w1)) @ w2

def token_shift(x):
    return jnp.pad(x, ((0, 0), (1, 0), (0, 0)))[:, :-1]

def wkv7(r, w, k, v, a, b):
    B, T, H, N = r.shape
    s0 = jnp.zeros((B, H, N, N), jnp.float32)

    def step(S, inp):
        r_t, w_t, k_t, v_t, a_t, b_t = inp
        sa = jnp.einsum('bhvk,bhk->bhv', S, a_t)
        S = S * w_t[:, :, None, :] + sa[..., None] * b_t[:, :, None, :] + v_t[..., None] * k_t[:, :, None, :]
        y = jnp.einsum('bhvk,bhk->bhv', S, r_t)
        return S, y

    xs = tuple(jnp.moveaxis(t, 1, 0) for t in (r, w, k, v, a, b))
    _, ys = lax.scan(step, s0, xs)
    return jnp.moveaxis(ys, 0, 1)

def rwkv7_time_mix(h, v_first, vres, mu, w_rkv, w0, w1, w2, a0, a1, a2, g1, g2, k_k, k_a, r_k, gn_g, gn_b, wo):
    f32 = jnp.float32
    B, T, C = h.shape
    H, N = RWKV_HEADS, HEAD_DIM
    xx = token_shift(h) - h
    xs = h[None] + xx[None] * mu[:, None, None, :]
    r, k, v = jnp.einsum('nbtc,ncd->nbtd', xs[:3], w_rkv)
    xv, xw, xa, xg = xs[2], xs[3], xs[4], xs[5]
    w_log = -jax.nn.softplus(-(w0 + jnp.tanh(xw @ w1) @ w2).astype(f32)) - 0.5
    decay = jnp.exp(-jnp.exp(w_log))
    if vres is None:
        v_first = v
    else:
        v0, v1, v2 = vres
        v = v + (v_first - v) * jax.nn.sigmoid(v0 + (xv @ v1) @ v2)
    a = jax.nn.sigmoid(a0 + (xa @ a1) @ a2)
    g = jax.nn.sigmoid(xg @ g1) @ g2

    def split(t):
        return t.reshape(B, T, H, N).astype(f32)

    kk = split(k * k_k)
    kk = kk / jnp.maximum(jnp.sqrt(jnp.sum(kk * kk, axis=-1, keepdims=True)), 1e-12)
    k_mod = k * (1.0 + (a - 1.0) * k_a)
    rh, kh, vh, ah, wh = split(r), split(k_mod), split(v), split(a), split(decay)
    y = wkv7(rh, wh, kh, vh, -kk, kk * ah)
    mean = jnp.mean(y, axis=-1, keepdims=True)
    var = jnp.mean(jnp.square(y - mean), axis=-1, keepdims=True)
    y = (y - mean) * lax.rsqrt(var + GN_EPS) * gn_g.reshape(H, N).astype(f32) + gn_b.reshape(H, N).astype(f32)
    y = y + jnp.sum(rh * kh * r_k.astype(f32), axis=-1, keepdims=True) * vh
    out = (y.reshape(B, T, C).astype(h.dtype) * g) @ wo
    return out, v_first

def shared_kv(x, kv_norm, w_kv, k_gain):
    B, T, _ = x.shape
    kv = (rms_norm(x, kv_norm) @ w_kv).reshape(B, T, 2, N_KV_HEADS, HEAD_DIM)
    k = rms_norm(kv[:, :, 0], k_gain)
    v = kv[:, :, 1]
    return k, v

def swa_sink_attention(q, k, v, sinks):
    B, T, _, D = q.shape
    nb = T // BLOCK
    qb = q.reshape(B, nb, BLOCK, N_KV_HEADS, GROUP, D)
    kb = k.reshape(B, nb, BLOCK, N_KV_HEADS, D)
    vb = v.reshape(B, nb, BLOCK, N_KV_HEADS, D)
    pad = ((0, 0), (1, 0), (0, 0), (0, 0), (0, 0))
    kcat = jnp.concatenate([jnp.pad(kb, pad)[:, :-1], kb], axis=2)
    vcat = jnp.concatenate([jnp.pad(vb, pad)[:, :-1], vb], axis=2)
    s = jnp.einsum('bnqhgd,bnshd->bnhgqs', qb, kcat, preferred_element_type=jnp.float32)
    qi = jnp.arange(BLOCK)[:, None]
    kj = jnp.arange(2 * BLOCK)[None, :]
    dist = qi + BLOCK - kj
    blk = jnp.arange(nb)[:, None, None]
    valid = (dist >= 0)[None] & (dist < WINDOW)[None] & ((blk > 0) | (kj >= BLOCK)[None])
    slopes = jnp.exp2(-8.0 * jnp.arange(1, N_Q_HEADS + 1, dtype=jnp.float32) / N_Q_HEADS)
    alibi = slopes.reshape(N_KV_HEADS, GROUP)[:, :, None, None] * dist.astype(jnp.float32)
    s = jnp.where(valid[None, :, None, None], s - alibi, -jnp.inf)
    sink = sinks.astype(jnp.float32).reshape(N_KV_HEADS, GROUP)[None, None, :, :, None, None]
    m = jnp.maximum(jnp.max(s, axis=-1, keepdims=True), sink)
    p = jnp.exp(s - m)
    p = p / (jnp.sum(p, axis=-1, keepdims=True) + jnp.exp(sink - m))
    o = jnp.einsum('bnhgqs,bnshd->bnqhgd', p.astype(v.dtype), vcat)
    return o.reshape(B, T, N_Q_HEADS * D)

def swa_layer(h, k_sh, v_sh, wq, q_gain, sinks, wo):
    B, T, _ = h.shape
    q = (h @ wq).reshape(B, T, N_Q_HEADS, HEAD_DIM)
    q = rms_norm(q, q_gain) * (HEAD_DIM ** -0.5)
    return swa_sink_attention(q, k_sh, v_sh, sinks) @ wo

def first_inputs(seed: int = 0) -> dict:
    key = jax.random.key(seed)
    ks = iter(jax.random.split(key, 40))
    f32 = jnp.float32
    C, F, NA, NB = D_MODEL, FFN_DIM, N_A_LAYERS, N_B_LAYERS

    def nrm(shape, scale):
        return jax.random.normal(next(ks), shape, f32) * scale

    def gain(shape):
        return 1.0 + nrm(shape, 0.02)

    return {
        'x': nrm((BATCH, SEQ, C), 1.0),
        'ln_mix': gain((DEPTH, C)),
        'ln_mlp': gain((DEPTH, C)),
        'mlp_w1': nrm((DEPTH, C, F), C ** -0.5),
        'mlp_w2': nrm((DEPTH, F, C), F ** -0.5),
        'a_mu': jax.random.uniform(next(ks), (NA, 6, C), f32),
        'a_w_rkv': nrm((NA, 3, C, C), C ** -0.5),
        'a_w0': jax.random.uniform(next(ks), (NA, C), f32, -6.0, -0.5),
        'a_w1': nrm((NA, C, D_DECAY_LORA), C ** -0.5),
        'a_w2': nrm((NA, D_DECAY_LORA, C), 0.1 * D_DECAY_LORA ** -0.5),
        'a_a0': nrm((NA, C), 0.5),
        'a_a1': nrm((NA, C, D_AAA_LORA), C ** -0.5),
        'a_a2': nrm((NA, D_AAA_LORA, C), 0.1 * D_AAA_LORA ** -0.5),
        'a_g1': nrm((NA, C, D_GATE_LORA), C ** -0.5),
        'a_g2': nrm((NA, D_GATE_LORA, C), D_GATE_LORA ** -0.5),
        'a_k_k': 0.85 + nrm((NA, C), 0.05),
        'a_k_a': 1.0 + nrm((NA, C), 0.05),
        'a_r_k': nrm((NA, RWKV_HEADS, HEAD_DIM), 0.1),
        'a_gn_g': gain((NA, C)),
        'a_gn_b': nrm((NA, C), 0.02),
        'a_wo': nrm((NA, C, C), C ** -0.5),
        'a_v0': 1.0 + nrm((NA - 1, C), 0.1),
        'a_v1': nrm((NA - 1, C, D_MV_LORA), C ** -0.5),
        'a_v2': nrm((NA - 1, D_MV_LORA, C), 0.1 * D_MV_LORA ** -0.5),
        'kv_norm': gain((C,)),
        'w_kv': nrm((C, 2 * N_KV_HEADS * HEAD_DIM), C ** -0.5),
        'k_gain': gain((HEAD_DIM,)),
        'b_wq': nrm((NB, C, N_Q_HEADS * HEAD_DIM), C ** -0.5),
        'b_q_gain': gain((NB, HEAD_DIM)),
        'b_sinks': nrm((NB, N_Q_HEADS), 0.5),
        'b_wo': nrm((NB, N_Q_HEADS * HEAD_DIM, C), (N_Q_HEADS * HEAD_DIM) ** -0.5),
    }

def first_block(x, ln_mix, ln_mlp, mlp_w1, mlp_w2, a_mu, a_w_rkv, a_w0, a_w1, a_w2, a_a0, a_a1, a_a2, a_g1, a_g2, a_k_k, a_k_a, a_r_k, a_gn_g, a_gn_b, a_wo, a_v0, a_v1, a_v2, kv_norm, w_kv, k_gain, b_wq, b_q_gain, b_sinks, b_wo):
    v_first = None
    k_sh = None
    v_sh = None
    for i in range(DEPTH):
        h = rms_norm(x, ln_mix[i])
        if i < N_A_LAYERS:
            j = i
            vres = None if j == 0 else (a_v0[j - 1], a_v1[j - 1], a_v2[j - 1])
            out, v_first = rwkv7_time_mix(h, v_first, vres, a_mu[j], a_w_rkv[j], a_w0[j], a_w1[j], a_w2[j], a_a0[j], a_a1[j], a_a2[j], a_g1[j], a_g2[j], a_k_k[j], a_k_a[j], a_r_k[j], a_gn_g[j], a_gn_b[j], a_wo[j])
        else:
            j = i - N_A_LAYERS
            out = swa_layer(h, k_sh, v_sh, b_wq[j], b_q_gain[j], b_sinks[j], b_wo[j])
        x = x + out
        x = x + squared_relu_mlp(rms_norm(x, ln_mlp[i]), mlp_w1[i], mlp_w2[i])
        if i == N_A_LAYERS - 1:
            k_sh, v_sh = shared_kv(x, kv_norm, w_kv, k_gain)
    return x


DEPTH_2 = 1

CTX_LEN = 256
GRID_W = 64
RET_W = D_MODEL // 2
RET_HEADS = 4
RET_HEAD_DIM = RET_W // RET_HEADS
FOURIER_W = D_MODEL - RET_W
FOURIER_GROUPS = 4
FOURIER_GROUP_DIM = FOURIER_W // FOURIER_GROUPS
MIX_W = RET_W + FOURIER_W
IN_W = 4 * RET_W + FOURIER_W
D_FF = ((8 * D_MODEL // 3 + 127) // 128) * 128
CONV_WIDTH = 3
CHUNK = 128
ROPE_BASE = 10000.0
NORM_EPS = 1e-6
N_MOD = 6


def rms_norm_2(x, g):
    xf = x.astype(jnp.float32)
    xf = xf * lax.rsqrt(jnp.mean(xf * xf, axis=-1, keepdims=True) + NORM_EPS)
    return xf.astype(x.dtype) * g

def modulate(h, shift, scale):
    return h * (1 + scale) + shift

def adaln(cond, w, b):
    return jnp.split(jax.nn.silu(cond) @ w + b, N_MOD, axis=-1)

def split_heads(t):
    bsz, length, _ = t.shape
    return t.reshape(bsz, length, RET_HEADS, RET_HEAD_DIM).transpose(0, 2, 1, 3).astype(jnp.float32)

def axial_rope(length):
    t = jnp.arange(length)
    row = (t // GRID_W).astype(jnp.float32)
    col = (t % GRID_W).astype(jnp.float32)
    n_freq = RET_HEAD_DIM // 4
    freqs = ROPE_BASE ** (-jnp.arange(n_freq, dtype=jnp.float32) / n_freq)
    ang = jnp.concatenate([row[:, None] * freqs, col[:, None] * freqs], axis=-1)
    return jnp.cos(ang), jnp.sin(ang)

def apply_rope(t, cos, sin):
    half = RET_HEAD_DIM // 2
    t1, t2 = t[..., :half], t[..., half:]
    return jnp.concatenate([t1 * cos - t2 * sin, t1 * sin + t2 * cos], axis=-1)

def retention_scan(q, k, v, log_gamma, init_state, strict):
    bsz, heads, length, dk = q.shape
    dv = v.shape[-1]
    n_chunks = length // CHUNK
    pos = jnp.arange(CHUNK, dtype=jnp.float32)
    diff = pos[:, None] - pos[None, :]
    mask = diff > 0 if strict else diff >= 0
    dmask = jnp.where(mask[None], jnp.exp(jnp.where(mask, diff, 0.0)[None] * log_gamma[:, None, None]), 0.0)
    qc = q.reshape(bsz, heads, n_chunks, CHUNK, dk)
    kc = k.reshape(bsz, heads, n_chunks, CHUNK, dk)
    vc = v.reshape(bsz, heads, n_chunks, CHUNK, dv)
    scores = jnp.einsum('bhncd,bhnmd->bhncm', qc, kc) * dmask[:, None]
    intra = jnp.einsum('bhncm,bhnme->bhnce', scores, vc)
    zeta = jnp.exp((CHUNK - 1 - pos)[None, :] * log_gamma[:, None])
    xi = jnp.exp((pos + 1)[None, :] * log_gamma[:, None])
    kv = jnp.einsum('bhnmd,bhnme->nbhde', kc * zeta[None, :, None, :, None], vc)
    chunk_decay = jnp.exp(CHUNK * log_gamma)[None, :, None, None]

    def step(state, kv_i):
        return state * chunk_decay + kv_i, state

    _, prev = lax.scan(step, init_state, kv)
    cross = jnp.einsum('bhncd,nbhde->bhnce', qc * xi[None, :, None, :, None], prev)
    return (intra + cross).reshape(bsz, heads, length, dv)

def context_states(h_ctx, w_in, lg_f, lg_b):
    kv = h_ctx @ w_in[:, RET_W:3 * RET_W]
    k, v = jnp.split(kv, 2, axis=-1)
    k = split_heads(k) * RET_HEAD_DIM ** -0.5
    v = split_heads(v)
    length = k.shape[2]
    m = jnp.arange(length, dtype=jnp.float32)
    w_f = jnp.exp((length - 1 - m)[None, :] * lg_f[:, None])
    w_b = jnp.exp(m[None, :] * lg_b[:, None])
    s_f = jnp.einsum('bhld,hl,bhle->bhde', k, w_f, v)
    s_b = jnp.einsum('bhld,hl,bhle->bhde', k, w_b, v)
    return s_f, s_b

def fourier_mix(f):
    bsz, length, _ = f.shape
    fg = f.reshape(bsz, length, FOURIER_GROUPS, FOURIER_GROUP_DIM).astype(jnp.float32)
    out = jnp.fft.fft2(fg, axes=(1, 3), norm="ortho").real
    return out.reshape(bsz, length, FOURIER_W).astype(f.dtype)

def token_mixer(h, w_in, w_out, lg_f, lg_b, init_f, init_b, rope):
    proj = h @ w_in
    q, k, v, g, f = jnp.split(proj, [RET_W, 2 * RET_W, 3 * RET_W, 4 * RET_W], axis=-1)
    q = split_heads(q)
    k = split_heads(k) * RET_HEAD_DIM ** -0.5
    v = split_heads(v)
    if rope is not None:
        q = apply_rope(q, *rope)
        k = apply_rope(k, *rope)
    o_f = retention_scan(q, k, v, lg_f, init_f, strict=False)
    flip = lambda t: jnp.flip(t, axis=2)
    o_b = flip(retention_scan(flip(q), flip(k), flip(v), lg_b, init_b, strict=True))
    o = o_f + o_b
    o = o * lax.rsqrt(jnp.mean(o * o, axis=-1, keepdims=True) + NORM_EPS)
    bsz, length = h.shape[0], h.shape[1]
    o = o.transpose(0, 2, 1, 3).reshape(bsz, length, RET_W).astype(h.dtype)
    ret = o * jax.nn.silu(g)
    return jnp.concatenate([ret, fourier_mix(f)], axis=-1) @ w_out

def conv_ffn(h, w_up, conv_w, conv_b, w_down, rows):
    bsz, length, _ = h.shape
    u = (h @ w_up).reshape(bsz, rows, length // rows, 2 * D_FF)
    up = jnp.pad(u, ((0, 0), (0, 0), (1, 1), (0, 0)))
    u = up[:, :, :-2] * conv_w[0] + up[:, :, 1:-1] * conv_w[1] + up[:, :, 2:] * conv_w[2] + conv_b
    a, b = jnp.split(u.reshape(bsz, length, 2 * D_FF), 2, axis=-1)
    return (jax.nn.silu(a) * b) @ w_down

def second_inputs(seed: int = 0) -> dict:
    key = jax.random.key(seed)
    ks = jax.random.split(key, 20)
    nrm = lambda k, shape, s: jax.random.normal(k, shape, jnp.float32) * s
    base = 1.0 - 2.0 ** (-5.0 - jnp.arange(RET_HEADS, dtype=jnp.float32))
    logit = jnp.log(base / (1.0 - base))
    return {
        "x": nrm(ks[0], (BATCH, SEQ, D_MODEL), 1.0),
        "c": nrm(ks[1], (BATCH, D_MODEL), 1.0),
        "ctx": nrm(ks[2], (BATCH, CTX_LEN, D_MODEL), 1.0),
        "c_ctx": nrm(ks[3], (D_MODEL,), 1.0),
        "w_ada": nrm(ks[4], (DEPTH_2, D_MODEL, N_MOD * D_MODEL), D_MODEL ** -0.5),
        "b_ada": nrm(ks[5], (DEPTH_2, N_MOD * D_MODEL), 0.02),
        "g_mix_pre": 1.0 + nrm(ks[6], (DEPTH_2, D_MODEL), 0.05),
        "g_mix_post": 1.0 + nrm(ks[7], (DEPTH_2, D_MODEL), 0.05),
        "g_ffn_pre": 1.0 + nrm(ks[8], (DEPTH_2, D_MODEL), 0.05),
        "g_ffn_post": 1.0 + nrm(ks[9], (DEPTH_2, D_MODEL), 0.05),
        "w_in": nrm(ks[10], (DEPTH_2, D_MODEL, IN_W), D_MODEL ** -0.5),
        "ret_decay_fwd": logit[None] + nrm(ks[11], (DEPTH_2, RET_HEADS), 0.1),
        "ret_decay_bwd": logit[None] + nrm(ks[12], (DEPTH_2, RET_HEADS), 0.1),
        "w_out": nrm(ks[13], (DEPTH_2, MIX_W, D_MODEL), MIX_W ** -0.5),
        "w_up": nrm(ks[14], (DEPTH_2, D_MODEL, 2 * D_FF), D_MODEL ** -0.5),
        "conv_w": nrm(ks[15], (DEPTH_2, CONV_WIDTH, 2 * D_FF), CONV_WIDTH ** -0.5),
        "conv_b": nrm(ks[16], (DEPTH_2, 2 * D_FF), 0.02),
        "w_down": nrm(ks[17], (DEPTH_2, D_FF, D_MODEL), D_FF ** -0.5),
    }

def second_block(x, c, ctx, c_ctx, w_ada, b_ada, g_mix_pre, g_mix_post, g_ffn_pre, g_ffn_post,
              w_in, ret_decay_fwd, ret_decay_bwd, w_out, w_up, conv_w, conv_b, w_down):
    seq_len = x.shape[1]
    rows = seq_len // GRID_W
    rope = axial_rope(seq_len)
    ctx_s = ctx
    for layer in range(DEPTH_2):
        lg_f = jax.nn.log_sigmoid(ret_decay_fwd[layer].astype(jnp.float32))
        lg_b = jax.nn.log_sigmoid(ret_decay_bwd[layer].astype(jnp.float32))
        sh_a, sc_a, gt_a, sh_f, sc_f, gt_f = [m[:, None, :] for m in adaln(c, w_ada[layer], b_ada[layer])]
        csh_a, csc_a, cgt_a, csh_f, csc_f, cgt_f = adaln(c_ctx, w_ada[layer], b_ada[layer])
        h_ctx = modulate(rms_norm_2(ctx_s, g_mix_pre[layer]), csh_a, csc_a)
        s_f, s_b = context_states(h_ctx, w_in[layer], lg_f, lg_b)
        h_lat = modulate(rms_norm_2(x, g_mix_pre[layer]), sh_a, sc_a)
        mix = token_mixer(h_lat, w_in[layer], w_out[layer], lg_f, lg_b, s_f, s_b, rope)
        x = x + gt_a * rms_norm_2(mix, g_mix_post[layer])
        h_ffn = modulate(rms_norm_2(x, g_ffn_pre[layer]), sh_f, sc_f)
        ffn = conv_ffn(h_ffn, w_up[layer], conv_w[layer], conv_b[layer], w_down[layer], rows)
        x = x + gt_f * rms_norm_2(ffn, g_ffn_post[layer])
        if layer + 1 < DEPTH_2:
            zero = jnp.zeros_like(s_f)
            mix_c = token_mixer(h_ctx, w_in[layer], w_out[layer], lg_f, lg_b, zero, zero, None)
            ctx_s = ctx_s + cgt_a * rms_norm_2(mix_c, g_mix_post[layer])
            h_cffn = modulate(rms_norm_2(ctx_s, g_ffn_pre[layer]), csh_f, csc_f)
            ffn_c = conv_ffn(h_cffn, w_up[layer], conv_w[layer], conv_b[layer], w_down[layer], 1)
            ctx_s = ctx_s + cgt_f * rms_norm_2(ffn_c, g_ffn_post[layer])
    return x


def setup_inputs(seed=0):
    out = dict(first_inputs(seed))
    for name, value in second_inputs(seed + 1).items():
        if name != "x":
            out[name + "_2"] = value
    return out


def reference(
    x, ln_mix, ln_mlp, mlp_w1, mlp_w2, a_mu, a_w_rkv, a_w0, a_w1, a_w2, a_a0, a_a1, a_a2, a_g1,
    a_g2, a_k_k, a_k_a, a_r_k, a_gn_g, a_gn_b, a_wo, a_v0, a_v1, a_v2, kv_norm, w_kv, k_gain,
    b_wq, b_q_gain, b_sinks, b_wo, c_2, ctx_2, c_ctx_2, w_ada_2, b_ada_2, g_mix_pre_2,
    g_mix_post_2, g_ffn_pre_2, g_ffn_post_2, w_in_2, ret_decay_fwd_2, ret_decay_bwd_2, w_out_2,
    w_up_2, conv_w_2, conv_b_2, w_down_2,
):
    x = first_block(
        x, ln_mix, ln_mlp, mlp_w1, mlp_w2, a_mu, a_w_rkv, a_w0, a_w1, a_w2, a_a0, a_a1, a_a2,
        a_g1, a_g2, a_k_k, a_k_a, a_r_k, a_gn_g, a_gn_b, a_wo, a_v0, a_v1, a_v2, kv_norm, w_kv,
        k_gain, b_wq, b_q_gain, b_sinks, b_wo,
    )
    return second_block(
        x, c_2, ctx_2, c_ctx_2, w_ada_2, b_ada_2, g_mix_pre_2, g_mix_post_2, g_ffn_pre_2,
        g_ffn_post_2, w_in_2, ret_decay_fwd_2, ret_decay_bwd_2, w_out_2, w_up_2, conv_w_2,
        conv_b_2, w_down_2,
    )


_drawn_inputs = setup_inputs


def setup_inputs(seed=0):
    import zlib

    import numpy as np

    out = dict(_drawn_inputs(seed))
    spreads = {}
    factors = {'a_w1': 8.0,
     'a_w2': 8.0,
     'a_gn_g': 5.183,
     'a_gn_b': 4.317,
     'kv_norm': 8.0,
     'k_gain': 8.0,
     'b_q_gain': 8.0,
     'b_sinks': 96.64,
     'b_ada_2': 2.683,
     'g_mix_pre_2': 2.745,
     'g_mix_post_2': 17.422,
     'g_ffn_pre_2': 3.058,
     'g_ffn_post_2': 17.031,
     'conv_b_2': 25.625}
    for name, (base, spread) in spreads.items():
        noise = np.random.default_rng([zlib.crc32(name.encode()), seed]).standard_normal(out[name].shape)
        drawn = base * np.exp(spread * noise) if base else spread * noise
        out[name] = __import__('jax').numpy.asarray(drawn.astype(out[name].dtype))
    for name, factor in factors.items():
        out[name] = (out[name] * factor).astype(out[name].dtype)
    return out
```

```python
import math
from contextlib import ExitStack, contextmanager

import numpy as np
import concourse.bass as bass
from concourse import mybir

F32 = mybir.dt.float32
F32R = mybir.dt.float32r
ALU = mybir.AluOpType
ACT = mybir.ActivationFunctionType
AX = mybir.AxisListType

P = 128
C = 1024
CB = C // P
T = 512
TB = T // P
HEADS = 16
HD = 64
FF = 4 * C
DFF = 2816
NFB = DFF // P
CTX = 256
RH = 4
LORA_W, LORA_A, LORA_G = 64, 64, 160
LAM = math.exp(-0.5)
RMS_EPS = 1e-6
GN_EPS = 64e-5
GRID = 64
LEVELS = 6

COLS = {}


def _columns():
    at = 0
    for name, n in (
        ("ln_mix0", 8), ("ln_mix1", 8), ("ln_mlp0", 8), ("ln_mlp1", 8), ("mu", 48), ("w0", 8), ("a0", 8),
        ("k_k", 8), ("k_a", 8), ("r_k", 8), ("gn_g", 8), ("gn_b", 8), ("kv_norm", 8), ("k_gain", 1),
        ("q_gain", 1), ("sinks", 16), ("c", 8), ("c_ctx", 8), ("b_ada", 48), ("g_mix_pre", 8),
        ("g_mix_post", 8), ("g_ffn_pre", 8), ("g_ffn_post", 8), ("decay", 8), ("conv_w", 132),
        ("conv_b", 44),
    ):
        COLS[name] = at
        at += n
    return at


N_COLS = _columns()

SQUARES = ["ident", "ones", "blk", "blk64", "upper", "upper_in", "lower", "rot", "m0", "m0t"] + [
    f"lvl{i}" for i in range(LEVELS)]
SQ_AT = {n: i for i, n in enumerate(SQUARES)}
N_SQ = len(SQUARES)


def constants():
    i = np.arange(P)
    t, s = i[:, None], i[None, :]
    sq = {
        "ident": t == s, "ones": np.ones((P, P)), "blk": t // 64 == s // 64,
        "blk64": (t // 64 == s // 64) / 64.0,
        "upper": t < s, "upper_in": t <= s, "lower": t > s,
        "m0": (t // 2 == s // 2) & (t > s), "m0t": (t // 2 == s // 2) & (t < s),
        "rot": (t == s - 64) * 1.0 - (t == s + 64) * 1.0,
    }
    for n in range(LEVELS):
        b = 2 << n
        sq[f"lvl{n}"] = (t // (2 * b) == s // (2 * b)) & (t // b != s // b) & (t > s)
    squares = np.concatenate([np.asarray(sq[n], np.float32) for n in SQUARES], 1)
    sel = np.zeros((P, CB, HEADS), np.float32)
    for cb in range(CB):
        sel[i, cb, 2 * cb + i // 64] = 1.0
    selt = np.ascontiguousarray(sel.transpose(2, 1, 0)).reshape(HEADS, CB * P)
    d = t + P - np.arange(2 * P)[None, :]
    band = np.where((d >= 0) & (d < P), d, 1e32)
    first = np.where(np.arange(2 * P)[None, :] < P, 1e32, band)
    band = np.stack([first, band, band], 1)
    e = np.arange(896)[None, :] - 384 - i[:, None]
    after = np.maximum(e, 0).astype(np.float32)
    before = np.maximum(-e, 0).astype(np.float32)
    pos = np.arange(T, dtype=np.float64)
    n_freq = P // 4
    freqs = 10000.0 ** (-np.arange(n_freq, dtype=np.float32) / n_freq)
    ang = np.concatenate([(pos // GRID)[:, None] * freqs, (pos % GRID)[:, None] * freqs], 1)
    cos = np.tile(np.cos(ang).T, (2, 1)).astype(np.float32)
    sin = np.tile(np.sin(ang).T, (2, 1)).astype(np.float32)
    ramp = np.stack([np.broadcast_to(pos + 1, (P, T)), np.broadcast_to(T - pos, (P, T))], 1)
    cpos = np.stack([CTX - 1 - (i[:, None] + P * np.arange(2)[None, :]), i[:, None] + P * np.arange(2)[None, :]], 2)
    kd = 2 * np.pi * np.outer(i, i) / P
    dft_c = np.concatenate([np.cos(kd), np.sin(kd)], 1) / math.sqrt(P)
    kl = 2 * np.pi * (np.outer(pos, pos) % T) / T
    dl = np.stack([np.cos(kl), -np.sin(kl)]) / math.sqrt(T)
    dft_l = dl.reshape(2, TB, P, T).transpose(2, 0, 1, 3)
    f = lambda a: np.ascontiguousarray(a, np.float32)
    return {
        "k_sq": f(squares), "k_sel": f(sel.reshape(P, CB * HEADS)), "k_selt": f(selt), "k_band": f(band),
        "k_after": f(after), "k_before": f(before), "k_cos": f(cos), "k_sin": f(sin), "k_ramp": f(ramp),
        "k_cpos": f(cpos.reshape(P, 4)), "k_sum2": f(np.tile(np.eye(2), (2, 1))), "k_dftc": f(dft_c), "k_dftl": f(dft_l),
    }


class Steps:

    def __init__(self, sem, name, book):
        self.sem, self.name, self.book, self.n = sem, name, book, 0
        self.first, self.marks = 0, None

    def step(self, *marks):
        self.n += 1
        for m in marks:
            self.book[self.name, m] = self.n
            if self.marks is not None:
                self.marks.append(m)
        return 1

    def at(self, what, loop=None, ago=0):
        v = what if isinstance(what, int) else self.book[self.name, what] if "built" in self.book else self.book.get((self.name, what), 1)
        if loop is None:
            return v
        per = self.book.get((self.name, "per turn", loop.name), 1)
        return loop.i * per + (v - ago * per if (self.name, what) in self.book or isinstance(what, int) else 1)

    def begin(self):
        self.first, self.marks = self.n, []

    def end(self, name, turns, units):
        per = self.n - self.first
        self.book[self.name, "per turn", name] = per
        for m in self.marks:
            last = self.book[self.name, m] + per * (turns - 1)
            self.book[self.name, ("last", m)] = last
            if m[0] == "used":
                self.book[self.name, ("used", m[1] + units * (turns - 1))] = last
        self.n += per * (turns - 1)
        self.marks = None


class Loop:
    def __init__(self, name, i, units):
        self.name, self.i, self.units = name, i, units


def program(nc, t, out, book):
    ctx = ExitStack()
    with ctx:
        KB = 1024
        base = 16640

        def at(name, kb, shape, dt=F32):
            return nc.alloc_sbuf_tensor_at(name, [P] + list(shape), dt, offset=base + int(kb * KB))

        slab = ctx.enter_context(nc.sbuf_tensor("slab", [P, (229368 - base) // 4 - 8], F32))

        vec = at("vec", 0, [N_COLS])
        sqs = at("sqs", 2, [N_SQ * P])
        sel = at("sel", 10, [CB, HEADS])
        selt = at("selt", 10.5, [CB * P])
        adac = at("adac", 14.5, [48, 2])
        small = at("small", 14.875, [96])
        SLOTS = 4
        raw = [at(f"raw{s}", 16 + 4 * s, [1024]) for s in range(SLOTS)]
        whi = [at(f"whi{s}", 32 + 4 * s, [1024], F32R) for s in range(SLOTS)]
        wlo = [at(f"wlo{s}", 48 + 4 * s, [1024], F32R) for s in range(SLOTS)]
        A0 = 64

        def sq(name):
            return sqs[:, SQ_AT[name] * P:(SQ_AT[name] + 1) * P]

        def col(name, j=0):
            return vec[:, COLS[name] + j:COLS[name] + j + 1]

        PB = [ctx.enter_context(nc.psum_tensor(f"bank{i}", [P, 512], F32)) for i in range(8)]

        def sem(name):
            return ctx.enter_context(nc.semaphore(name))

        STEP = {}
        for owner, names in (
            ("pe", "pe_lin pe_norm pe_lora pe_prep pe_score pe_inv pe_tok pe_rec pe_gn pe_kv pe_att pe_ada pe_ret pe_four"),
            ("act", "act_norm act_mix act_lora act_prep act_inv act_tok act_rec act_gn act_mlp act_kv act_att act_ada act_ret act_four act_ffn"),
            ("dve", "dve_norm dve_mix dve_lora dve_prep dve_score dve_inv dve_rec dve_gn dve_mlp dve_kv dve_att dve_ada dve_ret dve_four dve_ffn"),
            ("pool", "pool_prep pool_score pool_mlp pool_gn pool_ret"),
        ):
            for n in names.split():
                s = Steps(sem(n), n, book)
                s.owner = owner
                STEP[n] = s

        @contextmanager
        def turns(eng, owner, name, n, units):
            mine = [s for s in STEP.values() if s.owner == owner]
            for s in mine:
                s.begin()
            with eng.Fori(0, n) as i:
                yield Loop(name, i, units)
            for s in mine:
                s.end(name, n, units)

        w_raw = [sem(f"w_raw{s}") for s in range(SLOTS)]
        w_hi, w_lo = sem("w_hi"), sem("w_lo")
        phase = sem("phase")
        in_c, in_x = sem("in_c"), sem("in_x")
        spill, fill = sem("spill"), sem("fill")
        stored = sem("stored")
        phases = {"pe": 0, "act": 0, "dve": 0, "pool": 0, "sp": 0}

        def phase_done(who):
            phases[who] += 1
            return 4 * phases[who]

        def turn(v, loop):
            return v if loop is None else loop.i * loop.units + v

        lin, x_sum = STEP["pe_lin"], STEP["dve_mlp"]

        def used(u, loop):
            if loop is not None and u < loop.first:
                return lin.at(("used", u + loop.units), loop, ago=1)
            return lin.at(("used", u), loop)

        def x_done(stage, m):
            key = ("x", stage, m)
            return x_sum.at(("last", key) if ("dve_mlp", ("last", key)) in book else key)

        kdup, in_a, in_t = sem("kdup"), sem("in_a"), sem("in_t")

        UR, UWO, UM0 = 0, 24, 32
        UKV = UM0 + 64
        UQ = UKV + 4
        UBO = UQ + 8
        UM1 = UBO + 8
        UADA = UM1 + 64
        UCTX = UADA + 48
        UIN = UCTX + 8
        UOUT = UIN + 20
        UF = UOUT + 8
        UEND = UF + 66

        lambda8 = lambda n, kb, dt=F32: at(n, kb, [CB, T], dt)
        XT = lambda8("XT", 64)
        H = lambda8("H", 80)
        XX = lambda8("XX", 96)
        R, K_, V = lambda8("R", 112), lambda8("K", 128), lambda8("V", 144)
        SIG, AA = lambda8("SIG", 160), lambda8("AA", 176)
        NR = 3
        xmh = [at(f"xmh{i}", 192 + 2 * i, [T], F32R) for i in range(NR)]
        xml = [at(f"xml{i}", 192 + 6 + 2 * i, [T], F32R) for i in range(NR)]
        SQT = [at(f"sqt{i}", 192 + 2 * i, [T]) for i in range(2)]
        RS = at("RS", 204, [T])
        xt4 = [at(f"xt4_{i}", 64 + 2 * i, [T]) for i in range(4)]
        lw1 = at("lw1", 112, [CB, LORA_W])
        la1 = at("la1", 114, [CB, LORA_A])
        lg1 = at("lg1", 116, [CB, LORA_G])
        lw2 = at("lw2", 121, [C])
        la2 = at("la2", 125, [C])
        lg2a = at("lg2a", 129, [C])
        lg2b = at("lg2b", 133, [C])
        xl = [at(f"xl{i}", 137 + 2 * i, [T]) for i in range(4)]
        hid1 = [at(f"hid1_{i}", 145 + 2 * i, [T]) for i in range(2)]

        RT, KT, AT, BT = R, K_, SIG, AA
        PREP = {n: [at(f"prep_{n}{p}", 64 + 4 * j + 2 * p, [T]) for p in range(2)]
                for j, n in enumerate(("cs", "csn", "csx", "e1", "e2", "e3", "t1", "km", "rk", "kn", "t2"))}
        KNI, RKS = at("KNI", 108, [T]), at("RKS", 110, [T])
        VT = at("VT", 64, [C])
        ZI, MT, GBm, GKm = (at(n, 68 + 8 * j, [4, 4 * P]) for j, n in enumerate(("ZI", "MT", "GB", "GK")))
        SS = at("SS", 100, [CB, P])
        WB, UB, TS, SM = ([at(f"{n}{p}", 104 + j + 0.5 * p, [P]) for p in range(2)] for j, n in enumerate(("WB", "UB", "TS", "SM")))
        SM += [at(f"SM{i}", 205 + 0.5 * i, [P]) for i in (2, 3)]
        LL = [at(f"LL{p}", 192 + 8 * p, [4 * P]) for p in range(2)]
        LM = [at(f"LM{p}", 194 + 8 * p, [4 * P]) for p in range(2)]
        QS = [at(f"QS{p}", 196 + 8 * p, [4 * P]) for p in range(2)]
        TI = [at("TI0", 198, [4 * P]), at("TI1", 108, [4 * P])]
        DMID = small[:, 2:2 + 32]
        DEND = small[:, 34:34 + 32]
        inh, inl = lambda8("inh", 64, F32R), lambda8("inl", 80, F32R)
        TG = [at(f"TG{p}", 96 + 2 * p, [T]) for p in range(2)]
        TV = [at(f"TV{p}", 100 + 2 * p, [T]) for p in range(2)]
        G2, X = lambda8("G2", 160), lambda8("X", 176)

        hidh, hidl = lambda8("hidh", 96, F32R), lambda8("hidl", 112, F32R)
        HR = [at(f"HR{i}", 128 + 2 * i, [T]) for i in range(4)]
        HS = [at(f"HS{i}", 136 + 2 * i, [T]) for i in range(4)]
        KF, VF, KN, RKN = (at(n, 128 + 2 * j, [T]) for j, n in enumerate(("KF", "VF", "KN", "RKN")))
        KD = [at(f"KD{j}", 196 + 2 * j, [T]) for j in range(2)]
        VK = at("VK", 200, [TB, P])
        QNI = at("QNI", 202, [T])
        QF = lambda8("QF", 144)
        BAND = at("BAND", 160, [3, 2 * P])
        S1 = [at(f"S1_{i}", 128 + 2 * i, [T]) for i in range(3)]
        PTR = [at(f"PTR{i}", 134 + 2 * i, [T]) for i in range(3)]

        CST = at("CST", 15.25, [CB, 4], F32R)
        SUM2 = at("SUM2", 15.375, [2])
        LG = at("LG", 15.4375, [8])
        WC = at("WC", 15.5, [2, 2, RH])
        CPOS = at("CPOS", 15.5625, [4])
        LT = [at(f"LT{i}", 15.625 + 0.0625 * i, [16]) for i in range(5)]
        AR = [at(f"AR{i}", 128 + 4 * i, [1024]) for i in range(2)]
        GA, GAC, GP, GF, GFP = (small[:, 2 + 8 * i:10 + 8 * i] for i in range(5))
        CX = at("CX", 128, [CB, CTX])
        chh, chl = at("chh", 136, [CB, CTX], F32R), at("chl", 144, [CB, CTX], F32R)
        CT = [at(f"CT{i}", 152 + i, [CTX]) for i in range(2)]
        KW = [[at(f"KW{d}{tb}", 96 + 4 * d + 2 * tb, [T]) for tb in range(2)] for d in range(2)]
        VC = [at(f"VC{tb}", 104 + 2 * tb, [T]) for tb in range(2)]
        SFB = at("SFB", 196, [8, P])
        QK = lambda8("QK", 96)
        VL = at("VL", 112, [TB, 512])
        GS = at("GS", 120, [RH, T])
        FQ = at("FQ", 128, [RH, T])
        COS, SIN = at("COS", 136, [T]), at("SIN", 138, [T])
        RAMP = at("RAMP", 140, [2, T])
        AFT, BEF = at("AFT", 144, [896]), at("BEF", 147.5, [896])
        DM = [at(f"DM{i}", 151 + 3.5 * i, [896]) for i in range(2)]
        DFTC = at("DFTC", 158, [256])
        DFTL = at("DFTL", 160, [2, TB, T])
        FAB = at("FAB", 192, [TB, 256])
        PSC = [at(f"PSC{i}", 160 + 2 * i, [T]) for i in range(4)]
        RET = [at(f"RET{i}", 168 + 2 * i, [T]) for i in range(2)]
        RR = at("RR", 172, [T])
        HE = [at("HE0", 174, [T]), at("HE1", 204, [T])]
        QX = [at(f"QX{d}", 192 + 2 * d, [T]) for d in range(2)]
        TQ = [at(f"TQ{i}", 200 + 2 * i, [T]) for i in range(2)]
        MX = lambda8("MX", 96)
        GH, GL = at("GH", 96, [NFB * T], F32R), at("GL", 140, [NFB * T], F32R)
        CV = [at(f"CV{i}", 184 + 2 * i, [T]) for i in range(4)]
        SG = [at(f"SG{i}", 192 + 2 * i, [T]) for i in range(2)]
        HT = [at(f"HT{i}", 196 + 2 * i, [T]) for i in range(2)]
        CWT = [at(f"CWT{i}", 200 + 0.125 * i, [4, 2, 2]) for i in range(2)]
        FO, X2 = lambda8("FO", 64), lambda8("X2", 80)

        class Pass:

            def __init__(self, g, q, name, loop, before, freed):
                self.q, self.name, self.loop, self.before, self.freed = q, name, loop, before, freed
                self.u0 = UF + 4 * g
                self.at = [slice((2 * g + j) * T, (2 * g + j + 1) * T) if loop is None else bass.ds(loop.i * (4 * T) + (2 * g + j) * T, T) for j in range(2)]
                self.blocks = slice(2 * g, 2 * g + 2) if loop is None else bass.ds(loop.i * 4 + 2 * g, 2)

        def prior(steps, what, which, j):
            name, q, loop, ago = which
            key = (what, name, q, j)
            return steps.at(("last", key) if ago == "last" else key, loop, 0 if ago == "last" else ago)

        def up_passes(eng, owner, stream, work):
            stream(UF, 4)
            work(Pass(0, 0, "up0", None, None, None))
            stream(UF + 4, 4)
            work(Pass(1, 1, "up0", None, ("up0", 0, None, 0), None))
            with turns(eng, owner, "up", 4, 8) as lp:
                lp.first = UF + 8
                stream(UF + 8, 4, lp)
                work(Pass(2, 0, "up", lp, ("up", 1, lp, 1), ("up", 0, lp, 1)))
                stream(UF + 12, 4, lp)
                work(Pass(3, 1, "up", lp, ("up", 0, lp, 0), ("up", 1, lp, 1)))
            stream(UF + 40, 4)
            work(Pass(10, 0, "up1", None, ("up", 1, None, "last"), ("up", 0, None, "last")))

        def SM_at(c, cb):
            return SM[cb % 4][:]

        def four(name):
            return sq(name).unsqueeze(1).to_broadcast([P, 4, P])

        def quad(ap):
            return ap.rearrange("p (a b) -> p a b", a=4)

        def chunk(c):
            return slice(c * P, (c + 1) * P)

        xsp = nc.dram_tensor("x_spill", (P, CB * T), F32).ap()
        gsp = nc.dram_tensor("g_spill", (P, CB * T), F32).ap()

        block = ctx.enter_context(nc.Block())

        w_rkv = t["a_w_rkv"]

        @block.sync
        def _(sp):
            def load(u, src, dst=None, loop=None):
                if u >= SLOTS:
                    sp.wait_ge(w_lo, turn(u - SLOTS + 1, loop))
                sp.dma_start(raw[u % SLOTS][:, :] if dst is None else dst(raw[u % SLOTS]), src).then_inc(w_raw[u % SLOTS], 16)


            sp.dma_start(XT[:], t["x"]).then_inc(in_x, 16)
            sp.dma_start(vec[:], t["vec"]).then_inc(in_c, 16)
            sp.dma_start(sqs[:], t["k_sq"]).then_inc(in_c, 16)
            sp.dma_start(sel[:], t["k_sel"].rearrange("p (a b) -> p a b", a=CB)).then_inc(in_c, 16)
            sp.dma_start(selt[0:HEADS, :], t["k_selt"]).then_inc(in_c, 16)
            for dst, name in ((lg1, "a_g1"), (lw1, "a_w1"), (la1, "a_a1")):
                sp.dma_start(dst[:], t[name].rearrange("(a p) n -> p a n", p=P)).then_inc(in_c, 16)
            sp.dma_start(lg2a[:], t["a_g2"][0:P, :]).then_inc(in_c, 16)
            sp.dma_start(lg2b[0:LORA_G - P, :], t["a_g2"][P:LORA_G, :]).then_inc(in_c, 16)
            sp.dma_start(lw2[0:LORA_W, :], t["a_w2"]).then_inc(in_c, 16)
            sp.dma_start(la2[0:LORA_A, :], t["a_a2"]).then_inc(in_c, 16)
            rows = lambda w, k, n0=0: w[k * P:(k + 1) * P, n0:n0 + 1024]
            for u in range(4):
                load(u, rows(w_rkv[0], u))
            sp.wait_ge(STEP["dve_norm"].sem, STEP["dve_norm"].at("h0"))
            sp.dma_start(xsp, XT[:]).then_inc(spill, 16)
            sp.wait_ge(STEP["act_lora"].sem, STEP["act_lora"].at(("out", "g", CB - 1)))
            sp.dma_start(gsp, XT[:]).then_inc(spill, 16)
            for u in range(4, 24):
                load(u, rows(w_rkv[u // 8], u % 8))
            for u in range(7):
                load(UWO + u, rows(t["a_wo"], u))
            sp.wait_ge(STEP["pe_rec"].sem, STEP["pe_rec"].at(("sy", TB - 1, CB - 1)))
            sp.dma_start(G2[:], gsp.rearrange("p (a b) -> p a b", a=CB)).then_inc(fill, 16)
            sp.dma_start(X[:], xsp.rearrange("p (a b) -> p a b", a=CB)).then_inc(fill, 16)
            load(UWO + 7, rows(t["a_wo"], 7))

            def load_mlp(layer, u0, name):
                with turns(sp, "sp", name, 4, 16) as lp:
                    lp.first = u0
                    for j in range(8):
                        load(u0 + j, t["mlp_w1"][layer, j * P:(j + 1) * P, bass.ds(lp.i * 1024, 1024)], loop=lp)
                    for j in range(8):
                        load(u0 + 8 + j, t["mlp_w2"][layer, bass.ds(lp.i * 1024 + j * P, P), :], loop=lp)

            load_mlp(0, UM0, "mlp0")
            for j in range(4):
                load(UKV + j, t["w_kv"][2 * j * P:(2 * j + 2) * P, :].rearrange("(a p) n -> p a n", p=P),
                     dst=lambda r: r[:, 0:512].rearrange("p (a n) -> p a n", a=2))
            sp.dma_start(BAND[:], t["k_band"]).then_inc(in_c, 16)
            for j in range(8):
                load(UQ + j, rows(t["b_wq"], j))
            for j in range(8):
                load(UBO + j, rows(t["b_wo"], j))
            load_mlp(1, UM1, "mlp1")
            sp.dma_start(SUM2[0:4, :], t["k_sum2"]).then_inc(in_a, 16)
            sp.dma_start(CPOS[:], t["k_cpos"]).then_inc(in_a, 16)
            for n in range(6):
                for j in range(8):
                    load(UADA + 8 * n + j, rows(t["w_ada_2"], j, 1024 * n))
            for j in range(4):
                load(UCTX + j, rows(t["w_in_2"], j, 512))
            sp.wait_ge(phase, 4 * 10)
            sp.dma_start(CX[:], t["ctx"]).then_inc(in_a, 16)
            for j in range(4, 8):
                load(UCTX + j, rows(t["w_in_2"], j, 512))
            for j in range(6):
                load(UIN + j, rows(t["w_in_2"], j))
            sp.wait_ge(phase, 4 * 11)
            for dst, name in ((COS[:], "k_cos"), (SIN[:], "k_sin"), (RAMP[:], "k_ramp"), (AFT[:], "k_after"), (BEF[:], "k_before"),
                              (DFTC[:], "k_dftc"), (DFTL[:], "k_dftl")):
                sp.dma_start(dst, t[name]).then_inc(in_t, 16)
            for j in range(6, 16):
                load(UIN + j, rows(t["w_in_2"], j % 8, 1024 * (j // 8)))
            for j in range(4):
                load(UIN + 16 + j, t["w_in_2"][2 * j * P:(2 * j + 2) * P, 2048:2560].rearrange("(a p) n -> p a n", p=P),
                     dst=lambda r: r[:].rearrange("p (a n) -> p a n", a=2))
            for j in range(8):
                load(UOUT + j, rows(t["w_out_2"], j))
            for j in range(8):
                load(UF + j, t["w_up_2"][j * P:(j + 1) * P, :])
            with turns(sp, "sp", "up", 4, 8) as lp:
                for j in range(8):
                    load(UF + 8 + j, t["w_up_2"][bass.ds(lp.i * 1024 + (8 + j) * P, P), :], loop=lp)
            for j in range(40, 44):
                load(UF + j, t["w_up_2"][j * P:(j + 1) * P, :])
            for j in range(NFB):
                load(UF + 44 + j, rows(t["w_down_2"], j))
            for m in range(CB):
                sp.wait_ge(STEP["dve_ffn"].sem, STEP["dve_ffn"].at(("out", m)))
                sp.dma_start(out[:, m, :], X2[:, m, :]).then_inc(stored, 16)
            sp.wait_ge(stored, 16 * CB)

        @block.scalar
        def _(act):
            an, am, al = STEP["act_norm"], STEP["act_mix"], STEP["act_lora"]
            pn, pl = STEP["pe_norm"], STEP["pe_lora"]

            def split_hi(u, loop=None):
                act.wait_ge(w_raw[u % SLOTS], 16 * (u // SLOTS + 1) if loop is None else loop.i * (4 * loop.units) + 16 * (u // SLOTS + 1))
                if u >= SLOTS:
                    act.wait_ge(lin.sem, used(u - SLOTS, loop))
                act.activation(whi[u % SLOTS][:, :], raw[u % SLOTS][:, :], ACT.Copy).then_inc(w_hi, 1)

            def norm_stats(name, xb, n=T, root=None):
                for kb in range(CB):
                    if kb >= 2:
                        act.wait_ge(pn.sem, pn.at(("sum", name, kb - 2)))
                    act.activation(SQT[kb % 2][:, :n], xb(kb), ACT.Square).then_inc(an.sem, an.step(("sq", name, kb)))
                act.wait_ge(pn.sem, pn.at(("sum", name, CB - 1)))
                act.activation(RS[:, :n], PB[0][:, :n], ACT.Sqrt, scale=1.0 / C, bias=small[:, 0:1]).then_inc(an.sem, an.step(("root", name)))

            act.wait_ge(in_x, 16)
            act.wait_ge(STEP["dve_norm"].sem, STEP["dve_norm"].at("eps"))
            norm_stats("n0", lambda kb: XT[:, kb, :])

            act.wait_ge(spill, 16)
            q = 0
            for j, (name, width) in enumerate((("g", LORA_G), ("w", LORA_W), ("a", LORA_A))):
                act.wait_ge(pl.sem, pl.at(("hid", name)))
                fn = {"g": ACT.Sigmoid, "w": ACT.Tanh, "a": ACT.Copy}[name]
                if j > 0:
                    act.wait_ge(pl.sem, pl.at(("outs", "gwa"[j - 1])))
                act.activation(hid1[0][0:min(width, P), :], PB[0][0:min(width, P), :], fn).then_inc(al.sem, al.step(("hid", name, 0)))
                if width > P:
                    act.activation(hid1[1][0:width - P, :], PB[1][0:width - P, :], fn).then_inc(al.sem, al.step(("hid", name, 1)))
                for m in range(CB):
                    act.wait_ge(pl.sem, pl.at(("out", name, m)))
                    b = PB[2 + q % 6]
                    if name == "g":
                        act.activation(XT[:, m, :], b[:], ACT.Copy).then_inc(al.sem, al.step(("out", name, m)))
                    elif name == "w":
                        act.activation(SIG[:, m, :], b[:], ACT.Sigmoid, bias=col("w0", m)).then_inc(al.sem, al.step(("out", name, m)))
                    else:
                        act.activation(AA[:, m, :], b[:], ACT.Sigmoid, bias=col("a0", m)).then_inc(al.sem, al.step(("out", name, m)))
                    q += 1
            for u in range(3):
                split_hi(u)
            act.drain().then_inc(phase, 1)
            act.wait_ge(phase, phase_done("act"))
            act.wait_ge(spill, 32)

            def mix_hi(u):
                act.wait_ge(STEP["dve_mix"].sem, STEP["dve_mix"].at(("mix", u)))
                if u >= NR:
                    act.wait_ge(lin.sem, lin.at(("used", u - NR)))
                act.activation(xmh[u % NR][:], xt4[u % 4][:], ACT.Copy).then_inc(am.sem, am.step(("hi", u)))

            for u in range(2):
                mix_hi(u)
            for u in range(24):
                split_hi(u + 3)
                if u + 2 < 24:
                    mix_hi(u + 2)
            act.drain().then_inc(phase, 1)
            act.wait_ge(phase, phase_done("act"))

            ap_, ai, at_, ar, ag = (STEP["act_" + n] for n in ("prep", "inv", "tok", "rec", "gn"))
            pp, pr = STEP["pe_prep"], STEP["pe_rec"]
            dp = STEP["dve_prep"]
            for cb in range(CB):
                if cb >= 2:
                    act.wait_ge(pp.sem, pp.at(("ksum", cb - 2)))
                act.activation(PREP["e1"][cb % 2][:], K_[:, cb, :], ACT.Square, scale=col("k_k", cb)).then_inc(ap_.sem, ap_.step(("ksq", cb)))
            act.wait_ge(pp.sem, pp.at(("ksum", CB - 1)))
            act.activation(KNI[0:HEADS, :], PB[0][0:HEADS, :], ACT.Sqrt).then_inc(ap_.sem, ap_.step("kroot"))
            for cb in range(CB):
                p = cb % 2
                if cb >= 2:
                    act.wait_ge(dp.sem, dp.at(("at", cb - 2)))
                    act.wait_ge(STEP["pool_prep"].sem, STEP["pool_prep"].at(("done", cb - 2)))
                act.wait_ge(dp.sem, dp.at(("csn", cb)))
                act.activation(PREP["e2"][p][:], PREP["csn"][p][:], ACT.Exp, scale=LAM).then_inc(ap_.sem, ap_.step(("e2", cb)))
                act.activation(PREP["e1"][p][:], PREP["csn"][p][:], ACT.Exp, scale=-LAM).then_inc(ap_.sem, ap_.step(("e1", cb)))
                act.wait_ge(dp.sem, dp.at(("csx", cb)))
                act.activation(PREP["e3"][p][:], PREP["csx"][p][:], ACT.Exp, scale=-LAM).then_inc(ap_.sem, ap_.step(("e3", cb)))
                act.activation(DMID[:, 4 * cb:4 * cb + 4].unsqueeze(2), quad(PREP["cs"][p][:])[:, :, 63:64], ACT.Exp, scale=-LAM).then_inc(ap_.sem, ap_.step())
                act.activation(DEND[:, 4 * cb:4 * cb + 4].unsqueeze(2), quad(PREP["csn"][p][:])[:, :, 127:128], ACT.Exp, scale=-LAM).then_inc(ap_.sem, ap_.step(("exps", cb)))
            act.drain().then_inc(phase, 1)
            act.wait_ge(phase, phase_done("act"))

            def inverse_copies(c, half):
                for lv in range(LEVELS):
                    for p in range(2):
                        if lv > 0:
                            act.wait_ge(STEP["pe_inv"].sem, STEP["pe_inv"].at(("tz", c, half, lv - 1, p)))
                        act.wait_ge(STEP["pe_inv"].sem, STEP["pe_inv"].at(("q", c, half, lv, p)))
                        act.activation(QS[p][:], PB[2 + p][:], ACT.Copy).then_inc(ai.sem, ai.step(("q", c, half, lv, p)))

            for c in range(TB):
                for half in range(2):
                    inverse_copies(c, half)
                if c > 0:
                    act.wait_ge(pr.sem, pr.at(("sy", c - 1, CB - 1)))
                for j, which in enumerate("vkb"):
                    for half in range(2):
                        act.wait_ge(STEP["pe_tok"].sem, STEP["pe_tok"].at(("tr", c, which, half)))
                        b = PB[half]
                        if which == "v":
                            dst = quad(VT[:, half * 512:(half + 1) * 512])
                        else:
                            dst = (KT if which == "k" else BT)[:, 4 * half:4 * half + 4, chunk(c)]
                        act.activation(dst, quad(b[:]), ACT.Copy).then_inc(at_.sem, at_.step(("tr", c, which, half)))
                for i in range(CB + 2):
                    if i < CB:
                        act.wait_ge(pr.sem, pr.at(("w", c, i)))
                        if i >= 2:
                            act.wait_ge(pr.sem, pr.at(("u", c, i - 2)))
                        act.activation(WB[i % 2][:], PB[2 + i % 2][:, 0:P], ACT.Copy).then_inc(ar.sem, ar.step(("w", c, i)))
                    if i >= 2:
                        cb = i - 2
                        act.wait_ge(pr.sem, pr.at(("sy", c, cb)))
                        act.activation(RT[:, cb, chunk(c)], PB[cb % 2][:, 0:P], ACT.Copy).then_inc(ar.sem, ar.step(("y", c, cb)))
            act.drain().then_inc(phase, 1)
            act.wait_ge(phase, phase_done("act"))
            dg, pg = STEP["dve_gn"], STEP["pe_gn"]
            for cb in range(CB):
                act.wait_ge(dg.sem, dg.at(("yc", cb)))
                if cb >= 2:
                    act.wait_ge(pg.sem, pg.at(("var", cb - 2)))
                act.activation(SQT[cb % 2][:], RT[:, cb, :], ACT.Square).then_inc(ag.sem, ag.step(("sq", cb)))
            act.wait_ge(pg.sem, pg.at(("var", CB - 1)))
            act.activation(KNI[0:HEADS, :], PB[4][0:HEADS, :], ACT.Sqrt, scale=1.0 / HD, bias=small[0:HEADS, 1:2]).then_inc(ag.sem, ag.step("root"))
            for cb in range(CB):
                act.wait_ge(STEP["pool_gn"].sem, STEP["pool_gn"].at(("o", cb)))
                act.activation(inh[:, cb, :], TV[cb % 2][:], ACT.Copy).then_inc(ag.sem, ag.step(("hi", cb)))
            act.drain().then_inc(phase, 1)
            act.wait_ge(phase, phase_done("act"))
            amlp, akv, aat = STEP["act_mlp"], STEP["act_kv"], STEP["act_att"]
            dmlp = STEP["dve_mlp"]

            def split_run(u0, n, loop=None):
                for u in range(u0, u0 + n):
                    split_hi(u + 3, loop)

            def x_stats(name, prev):
                for kb in range(CB):
                    act.wait_ge(x_sum.sem, x_done(prev, kb))
                    if kb >= 2:
                        act.wait_ge(pn.sem, pn.at(("sum", name, kb - 2)))
                    act.activation(SQT[kb % 2][:], X[:, kb, :], ACT.Square).then_inc(an.sem, an.step(("sq", name, kb)))
                act.wait_ge(pn.sem, pn.at(("sum", name, CB - 1)))
                act.activation(RS[:], PB[0][:], ACT.Sqrt, scale=1.0 / C, bias=small[:, 0:1]).then_inc(an.sem, an.step(("root", name)))

            def gained_hi(name, dst, gain, last_unit):
                act.wait_ge(lin.sem, used(last_unit, None))
                for kb in range(CB):
                    act.activation(dst[:, kb, :], X[:, kb, :], ACT.Copy, scale=col(gain, kb)).then_inc(an.sem, an.step(("hi", name, kb)))

            def mlp(layer, u0, name, prev, last_unit):
                x_stats(name, prev)
                gained_hi(name, inh, f"ln_mlp{layer}", last_unit)
                with turns(act, "act", name, 4, 16) as lp:
                    lp.first = u0
                    split_run(u0, 8, lp)
                    for m in range(CB):
                        act.wait_ge(dmlp.sem, dmlp.at(("r", name, m), lp))
                        act.activation(hidh[:, m, :], HR[m % 4][:], ACT.Square).then_inc(amlp.sem, amlp.step(("hh", name, m)))
                    split_run(u0 + 8, 8, lp)

            split_run(UWO, 8)
            mlp(0, UM0, "mlp0", "wo", UWO + 7)
            act.drain().then_inc(phase, 1)
            act.wait_ge(phase, phase_done("act"))
            x_stats("kv", "mlp0")
            gained_hi("kv", inh, "kv_norm", UM0 + 63)
            gained_hi("q", hidh, "ln_mix1", UM0 + 63)
            split_run(UKV, 4)
            dk = STEP["dve_kv"]
            act.wait_ge(dk.sem, dk.at("kf"))
            act.activation(HS[2][:], KF[:], ACT.Square).then_inc(akv.sem, akv.step("ksq"))
            act.wait_ge(STEP["pe_kv"].sem, STEP["pe_kv"].at("kmean"))
            act.activation(RKN[:], PB[3][:], ACT.Sqrt, bias=small[:, 0:1]).then_inc(akv.sem, akv.step("kroot"))
            act.wait_ge(STEP["pe_kv"].sem, STEP["pe_kv"].at("vt"))
            act.activation(VK[:].rearrange("p a b -> p (a b)"), PB[4][:], ACT.Copy).then_inc(akv.sem, akv.step("vk"))
            act.wait_ge(dk.sem, dk.at("kn"))
            for j in range(2):
                for half in range(2):
                    act.dma_start(KD[j][64 * half:64 * half + 64, :], KN[64 * j:64 * j + 64, :]).then_inc(kdup, 16)
            split_run(UQ, 8)
            for cb in range(CB):
                act.wait_ge(dk.sem, dk.at(("q", cb)))
                if cb >= 2:
                    act.wait_ge(STEP["pe_kv"].sem, STEP["pe_kv"].at(("qsum", cb - 2)))
                act.activation(SQT[cb % 2][:], QF[:, cb, :], ACT.Square).then_inc(akv.sem, akv.step(("qsq", cb)))
            act.wait_ge(STEP["pe_kv"].sem, STEP["pe_kv"].at(("qsum", CB - 1)))
            act.activation(QNI[0:HEADS, :], PB[0][0:HEADS, :], ACT.Sqrt, bias=small[0:HEADS, 66:67]).then_inc(akv.sem, akv.step("qroot"))
            act.drain().then_inc(phase, 1)
            act.wait_ge(phase, phase_done("act"))
            pa, da = STEP["pe_att"], STEP["dve_att"]
            NT = 32
            for i in range(NT + 5):
                if i < NT:
                    act.wait_ge(da.sem, da.at(("nm", i)))
                    st = small[:, 2 + 16 * (i % 4):]
                    h = 2 * (i // 4) + i % 2
                    for b in range(2):
                        pb = S1[i % 3][:, b * 256:(b + 1) * 256]
                        act.activation(pb, pb, ACT.Exp, bias=st[:, b:b + 1], accum_out=st[:, 2 + b:3 + b]).then_inc(aat.sem, aat.step())
                    act.activation(st[:, 4:6], st[:, 0:2], ACT.Exp, bias=col("sinks", h)).then_inc(aat.sem, aat.step(("exp", i)))
                if 2 <= i < NT + 2:
                    k = i - 2
                    act.wait_ge(pa.sem, pa.at(("tr", k)))
                    if k >= 3:
                        act.wait_ge(pa.sem, pa.at(("pv", k - 3)))
                    act.activation(PTR[k % 3][:], PB[4 + k % 2][:], ACT.Copy).then_inc(aat.sem, aat.step(("ptr", k)))
                if i >= 4 and (i - 4) % 2 == 1 and i - 4 < NT:
                    k = i - 4
                    pr_ = k // 2
                    cb, nn = divmod(pr_, 2)
                    act.wait_ge(pa.sem, pa.at(("pv", k)))
                    act.activation(inh[:, cb, nn * 256:(nn + 1) * 256], PB[6 + pr_ % 2][:, 0:256], ACT.Copy).then_inc(aat.sem, aat.step(("oh", pr_)))
            act.drain().then_inc(phase, 1)
            act.wait_ge(phase, phase_done("act"))
            split_run(UBO, 8)
            mlp(1, UM1, "mlp1", "bo", UBO + 7)
            act.drain().then_inc(phase, 1)
            act.wait_ge(phase, phase_done("act"))
            aad, art, af, affn = (STEP["act_" + n] for n in ("ada", "ret", "four", "ffn"))
            dad, drt, dff = (STEP["dve_" + n] for n in ("ada", "ret", "ffn"))
            pad, prt, pf = (STEP["pe_" + n] for n in ("ada", "ret", "four"))
            act.activation(LT[0][:], vec[:, COLS["c"]:COLS["c"] + 16], ACT.Sigmoid).then_inc(aad.sem, aad.step("sig"))
            act.wait_ge(dad.sem, dad.at("abs"))
            act.activation(LT[1][:, 0:8], LT[1][:, 0:8], ACT.Exp, scale=-1.0).then_inc(aad.sem, aad.step("eabs"))
            act.wait_ge(dad.sem, dad.at("silu"))
            act.activation(CST[:, :, 0:2], LT[0][:].rearrange("p (b k) -> p k b", b=2), ACT.Copy).then_inc(aad.sem, aad.step("ch"))
            act.wait_ge(dad.sem, dad.at("cpos"))
            wc = WC[:].rearrange("p a b c -> p (a b c)")
            act.activation(wc, wc, ACT.Exp).then_inc(aad.sem, aad.step("wc"))
            for n in range(6):
                split_run(UADA + 8 * n, 8)
                if n >= 2:
                    act.wait_ge(pad.sem, pad.at(("turned", n - 2)))
                for hf in range(2):
                    act.wait_ge(lin.sem, lin.at(("row", n, hf)))
                    act.activation(AR[n % 2][0:4, hf * 512:(hf + 1) * 512], PB[2 * (n % 2) + hf][0:4, :], ACT.Copy).then_inc(aad.sem, aad.step(("row", n, hf)))
            act.drain().then_inc(phase, 1)
            act.wait_ge(phase, phase_done("act"))

            def modulated_hi(name, dst, tmp, shift, n=T):
                for kb in range(CB):
                    act.wait_ge(dad.sem, dad.at(("t", name, kb)))
                    act.activation(dst[:, kb, :n], tmp[kb % 2][:, :n], ACT.Identity, bias=shift(kb)).then_inc(aad.sem, aad.step(("hi", name, kb)))

            def stats_of(name, block_, ready=None, n=T):
                for kb in range(CB):
                    if ready is not None:
                        ready(kb)
                    if kb >= 2:
                        act.wait_ge(pn.sem, pn.at(("sum", name, kb - 2)))
                    act.activation(SQT[kb % 2][:, :n], block_(kb), ACT.Square).then_inc(an.sem, an.step(("sq", name, kb)))
                act.wait_ge(pn.sem, pn.at(("sum", name, CB - 1)))
                act.activation(RS[:, :n], PB[0][:, :n], ACT.Sqrt, scale=1.0 / C, bias=small[:, 0:1]).then_inc(an.sem, an.step(("root", name)))

            act.wait_ge(in_a, 48)
            stats_of("ctx", lambda kb: CX[:, kb, :], n=CTX)
            modulated_hi("ctx", chh, CT, lambda kb: adac[:, kb, 1:2], CTX)
            split_run(UCTX, 8)
            for tb in range(2):
                act.wait_ge(lin.sem, lin.at(("bank", "ctx", 2 * tb + 1)))
                for d in range(2):
                    for h in range(RH):
                        act.activation(KW[d][tb][:, h * P:(h + 1) * P], PB[2 * tb][:, h * P:(h + 1) * P], ACT.Copy, scale=WC[:, tb, d, h:h + 1]).then_inc(art.sem, art.step())
                act.activation(VC[tb][:], PB[2 * tb + 1][:], ACT.Copy).then_inc(art.sem, art.step(("kv", tb)))
            for d in range(2):
                act.wait_ge(prt.sem, prt.at(("state", d)))
                act.activation(SFB[:, 4 * d:4 * d + 4, :].rearrange("p a b -> p (a b)"), PB[4 + d][:], ACT.Copy).then_inc(art.sem, art.step(("state", d)))
            act.drain().then_inc(phase, 1)
            act.wait_ge(phase, phase_done("act"))
            stats_of("lat", lambda kb: X[:, kb, :])
            modulated_hi("lat", inh, TQ, lambda kb: adac[:, kb, 0:1])
            split_run(UIN, 16)
            for m in range(RH):
                act.wait_ge(lin.sem, lin.at(("bank", "g", m)))
                if m >= 2:
                    act.wait_ge(drt.sem, drt.at(("g", m - 2)))
                act.activation(TQ[m % 2][:], PB[4 + m][:], ACT.Sigmoid).then_inc(art.sem, art.step(("sig", m)))
            split_run(UIN + 16, 4)
            act.drain().then_inc(phase, 1)
            act.wait_ge(phase, phase_done("act"))
            for g in range(4):
                for j in range(2):
                    act.wait_ge(pf.sem, pf.at(("ab", g, j)))
                    if g >= 1 and j == 0:
                        act.wait_ge(pf.sem, pf.at(("f", g - 1)))
                    act.activation(FAB[:, 2 * j:2 * j + 2, :].rearrange("p a b -> p (a b)"), PB[j][:], ACT.Copy).then_inc(af.sem, af.step(("ab", g, j)))
                act.wait_ge(pf.sem, pf.at(("f", g)))
                act.activation(inh[:, 4 + g, :], PB[2 + g % 2][:], ACT.Copy).then_inc(af.sem, af.step(("hi", g)))
            act.drain().then_inc(phase, 1)
            act.wait_ge(phase, phase_done("act"))
            act.wait_ge(in_t, 112)

            def decays(h):
                act.wait_ge(drt.sem, drt.at(("dm", h)))
                act.activation(DM[h % 2][:], DM[h % 2][:], ACT.Exp).then_inc(art.sem, art.step(("dm", h)))
                for d in range(2):
                    if h > 0:
                        act.wait_ge(drt.sem, drt.at(("qx", h - 1, d)))
                    act.activation(HE[d][:], RAMP[:, d, :], ACT.Exp, scale=LG[:, 4 * d + h:4 * d + h + 1]).then_inc(art.sem, art.step(("xi", h, d)))

            decays(0)
            for h in range(RH):
                if h + 1 < RH:
                    decays(h + 1)
                act.wait_ge(prt.sem, prt.at(("out", h)))
                if h >= 1:
                    act.wait_ge(prt.sem, prt.at(("sum", h - 1)))
                act.activation(TQ[0][:], PB[4 + h % 2][:], ACT.Square).then_inc(art.sem, art.step(("sq", h)))
                if h >= 2:
                    act.wait_ge(drt.sem, drt.at(("lo", h - 2)))
                act.activation(RET[h % 2][:], PB[4 + h % 2][:], ACT.Copy).then_inc(art.sem, art.step(("o", h)))
                act.wait_ge(prt.sem, prt.at(("sum", h)))
                if h >= 1:
                    act.wait_ge(drt.sem, drt.at(("n", h - 1)))
                act.activation(RR[:], PB[6][:], ACT.Sqrt, scale=1.0 / P, bias=small[:, 0:1]).then_inc(art.sem, art.step(("root", h)))
                act.wait_ge(drt.sem, drt.at(("ret", h)))
                act.activation(inh[:, h, :], RET[h % 2][:], ACT.Copy).then_inc(art.sem, art.step(("hi", h)))
            act.drain().then_inc(phase, 1)
            act.wait_ge(phase, phase_done("act"))
            split_run(UOUT, 8)
            stats_of("mx", lambda kb: MX[:, kb, :], lambda kb: act.wait_ge(drt.sem, drt.at(("mx", kb))))
            stats_of("fp", lambda kb: X[:, kb, :], lambda kb: act.wait_ge(drt.sem, drt.at(("x", kb))))
            act.wait_ge(fill, 32)
            act.dma_start(xsp, X[:]).then_inc(spill, 16)
            modulated_hi("fp", inh, TQ, lambda kb: adac[:, 24 + kb, 0:1])
            act.drain().then_inc(phase, 1)
            act.wait_ge(phase, phase_done("act"))
            act.wait_ge(spill, 48)

            def gated(s):
                q, name, loop = s.q, s.name, s.loop
                act.wait_ge(dff.sem, dff.at(("cw", name, q), loop))
                for j in range(2):
                    if s.before is not None:
                        act.wait_ge(dff.sem, prior(dff, "h", s.before, j))
                    for hf in range(2):
                        act.wait_ge(lin.sem, lin.at(("bank", name, q, 2 * j + hf), loop))
                        act.activation(CV[2 * j + hf][:], PB[4 * q + 2 * j + hf][:], ACT.Identity, scale=CWT[q][:, 1, hf, j:j + 1],
                                                bias=CWT[q][:, 3, hf, j:j + 1]).then_inc(affn.sem, affn.step(("cv", name, q, 2 * j + hf)))
                for j in range(2):
                    act.wait_ge(dff.sem, dff.at(("cv", name, q, 2 * j), loop))
                    act.activation(SG[j][:], CV[2 * j][:], ACT.Silu).then_inc(affn.sem, affn.step(("sg", name, q, j)))
                for j in range(2):
                    act.wait_ge(dff.sem, dff.at(("h", name, q, j), loop))
                    act.activation(GH[:, s.at[j]], HT[j][:], ACT.Copy).then_inc(affn.sem, affn.step(("hh", name, q, j)))

            up_passes(act, "act", split_run, gated)
            act.wait_ge(lin.sem, used(UF + 43, None))
            act.dma_start(X2[:], xsp.rearrange("p (a b) -> p a b", a=CB)).then_inc(fill, 16)
            split_run(UF + 44, NFB - 3)
            stats_of("fo", lambda kb: FO[:, kb, :], lambda kb: act.wait_ge(dff.sem, dff.at(("fo", kb))))
        @block.vector
        def _(dve):
            dn, dm, dl = STEP["dve_norm"], STEP["dve_mix"], STEP["dve_lora"]
            an = STEP["act_norm"]

            def split_lo(u, loop=None):
                dve.wait_ge(w_hi, turn(u + 1, loop))
                dve.tensor_tensor(wlo[u % SLOTS][:, :], raw[u % SLOTS][:, :], whi[u % SLOTS][:, :].bitcast(F32), ALU.subtract).then_inc(w_lo, 1)

            def rstd(name, n=T):
                dve.wait_ge(an.sem, an.at(("root", name)))
                dve.reciprocal(RS[:, :n], RS[:, :n]).then_inc(dn.sem, dn.step(("rstd", name)))
                return dn.n

            dve.memset(small[:, 0:1], RMS_EPS).then_inc(dn.sem, dn.step())
            dve.memset(small[:, 1:2], GN_EPS).then_inc(dn.sem, dn.step("eps"))
            dve.wait_ge(in_c, 16 * 11)
            r = rstd("n0")
            dve.wait_ge(dn.sem, r)
            dve.wait_ge(in_x, 16)
            for kb in range(CB):
                dve.scalar_tensor_tensor(H[:, kb, :], XT[:, kb, :], col("ln_mix0", kb), RS[:, :], ALU.mult, ALU.mult).then_inc(dn.sem, dn.step(("h", kb)))
                h = dn.n
            dve.wait_ge(dn.sem, h)
            dve.tensor_tensor(XX[:, :, 1:T], H[:, :, 0:T - 1], H[:, :, 1:T], ALU.subtract).then_inc(dn.sem, dn.step())
            dve.tensor_scalar(XX[:, :, 0:1], H[:, :, 0:1], -1.0, None, ALU.mult).then_inc(dn.sem, dn.step("h0"))
            h = dn.n
            dve.wait_ge(dn.sem, h)
            n = 0
            for name, mu in (("g", 5), ("w", 3), ("a", 4)):
                for kb in range(CB):
                    if n >= 4:
                        dve.wait_ge(STEP["pe_lora"].sem, STEP["pe_lora"].at(("used", n - 4)))
                    dve.scalar_tensor_tensor(xl[n % 4][:], XX[:, kb, :], col("mu", 8 * mu + kb), H[:, kb, :], ALU.mult, ALU.add).then_inc(dl.sem, dl.step(("x", n)))
                    n += 1
            for u in range(3):
                split_lo(u)
            dve.drain().then_inc(phase, 1)
            dve.wait_ge(phase, phase_done("dve"))
            dve.wait_ge(spill, 32)

            def mix(u):
                if u >= 4:
                    dve.wait_ge(STEP["act_mix"].sem, STEP["act_mix"].at(("hi", u - 4)))
                    dve.wait_ge(dm.sem, dm.at(lo_at[u - 4]))
                dve.scalar_tensor_tensor(xt4[u % 4][:], XX[:, u % 8, :], col("mu", 8 * (u // 8) + u % 8), H[:, u % 8, :], ALU.mult, ALU.add).then_inc(dm.sem, dm.step(("mix", u)))

            lo_at = {}

            def mix_lo(u):
                dve.wait_ge(STEP["act_mix"].sem, STEP["act_mix"].at(("hi", u)))
                dve.tensor_tensor(xml[u % NR][:], xt4[u % 4][:], xmh[u % NR][:].bitcast(F32), ALU.subtract).then_inc(dm.sem, dm.step(("lo", u)))
                lo_at[u] = dm.n

            for u in range(3):
                mix(u)
            for u in range(2):
                mix_lo(u)
            for u in range(24):
                split_lo(u + 3)
                if u + 3 < 24:
                    mix(u + 3)
                if u + 2 < 24:
                    mix_lo(u + 2)
                if u % 8 == 7:
                    dst = (R, K_, V)[u // 8]
                    for m in range(CB):
                        dve.wait_ge(lin.sem, lin.at(("bank", u // 8, m)))
                        dve.tensor_copy(dst[:, m, :], PB[m][:]).then_inc(dm.sem, dm.step(("taken", u // 8, m)))
            dve.drain().then_inc(phase, 1)
            dve.wait_ge(phase, phase_done("dve"))

            dp, ds, di, dr, dg = (STEP["dve_" + n] for n in ("prep", "score", "inv", "rec", "gn"))
            ap_, pp, pr = STEP["act_prep"], STEP["pe_prep"], STEP["pe_rec"]
            pre = PREP
            dve.wait_ge(ap_.sem, ap_.at("kroot"))
            dve.tensor_scalar(KNI[0:HEADS, :], KNI[0:HEADS, :], 1e-12, None, ALU.max).then_inc(dp.sem, dp.step())
            k = dp.n
            dve.wait_ge(dp.sem, k)
            dve.reciprocal(KNI[0:HEADS, :], KNI[0:HEADS, :]).then_inc(dp.sem, dp.step("kni"))
            for cb in range(CB):
                p = cb % 2
                if cb >= 2:
                    dve.wait_ge(ap_.sem, ap_.at(("exps", cb - 2)))
                    dve.wait_ge(STEP["pool_prep"].sem, STEP["pool_prep"].at(("done", cb - 2)))
                    dve.wait_ge(pp.sem, pp.at(("rks", cb - 2)))
                    dve.wait_ge(dp.sem, dp.at(("at", cb - 2)))
                for c in range(TB):
                    dve.tensor_tensor_scan(pre["cs"][p][:, chunk(c)], sq("ones"), SIG[:, cb, chunk(c)], 0.0, ALU.mult, ALU.add).then_inc(dp.sem, dp.step())
                    k = dp.n
                dve.wait_ge(dp.sem, k)
                cs = quad(pre["cs"][p][:])
                dve.tensor_tensor(quad(pre["csn"][p][:]), cs, cs[:, :, 63:64].to_broadcast([P, 4, P]), ALU.subtract).then_inc(dp.sem, dp.step(("csn", cb)))
                k = dp.n
                dve.tensor_scalar(pre["t1"][p][:], AA[:, cb, :], 1.0, col("k_a", cb), ALU.subtract, ALU.mult).then_inc(dp.sem, dp.step(("t1", cb)))
                t1 = dp.n
                dve.wait_ge(dp.sem, k)
                dve.tensor_tensor(pre["csx"][p][:], pre["csn"][p][:], SIG[:, cb, :], ALU.subtract).then_inc(dp.sem, dp.step(("csx", cb)))
                dve.wait_ge(dp.sem, t1)
                dve.scalar_tensor_tensor(pre["km"][p][:], pre["t1"][p][:], 1.0, K_[:, cb, :], ALU.add, ALU.mult).then_inc(dp.sem, dp.step())
                km = dp.n
                dve.wait_ge(pp.sem, pp.at(("bc", cb)))
                dve.scalar_tensor_tensor(pre["kn"][p][:], K_[:, cb, :], col("k_k", cb), PB[1 + p][:], ALU.mult, ALU.mult).then_inc(dp.sem, dp.step(("kn", cb)))
                kn = dp.n
                dve.wait_ge(dp.sem, km)
                dve.scalar_tensor_tensor(pre["rk"][p][:], R[:, cb, :], col("r_k", cb), pre["km"][p][:], ALU.mult, ALU.mult).then_inc(dp.sem, dp.step(("rk", cb)))
                dve.wait_ge(dp.sem, kn)
                dve.wait_ge(ap_.sem, ap_.at(("e2", cb)))
                dve.tensor_tensor(KT[:, cb, :], pre["km"][p][:], pre["e2"][p][:], ALU.mult).then_inc(dp.sem, dp.step())
                dve.wait_ge(ap_.sem, ap_.at(("e3", cb)))
                dve.scalar_tensor_tensor(AT[:, cb, :], pre["kn"][p][:], -1.0, pre["e3"][p][:], ALU.mult, ALU.mult).then_inc(dp.sem, dp.step(("at", cb)))
            dve.wait_ge(pp.sem, pp.at(("rks", CB - 1)))
            dve.tensor_copy(RKS[0:HEADS, :], PB[3][0:HEADS, :]).then_inc(dp.sem, dp.step())
            dve.drain().then_inc(phase, 1)
            dve.wait_ge(phase, phase_done("dve"))
            dve.memset(SS[:], 0.0).then_inc(dr.sem, dr.step("s0"))

            def score_masks(c, half):
                for kind in range(5):
                    for p in range(2):
                        g = 2 * half + p
                        dve.wait_ge(STEP["pe_score"].sem, STEP["pe_score"].at((c, half, kind, p)))
                        b = quad(PB[p][:])
                        if kind == 0:
                            dve.tensor_tensor(quad(TI[p][:]), b, four("m0"), ALU.mult).then_inc(ds.sem, ds.step(("ti", c, half, p)))
                            dve.tensor_tensor(quad(LL[p][:]), b, four("lower"), ALU.mult).then_inc(ds.sem, ds.step(("taken", c, half, kind, p)))
                        else:
                            dst, mask = {1: (ZI, "m0t"), 2: (MT, "upper"), 3: (GBm, "upper_in"), 4: (GKm, "upper_in")}[kind]
                            dve.tensor_tensor(quad(dst[:, g, :]), b, four(mask), ALU.mult).then_inc(ds.sem, ds.step(("taken", c, half, kind, p)))

            def inverse_sums(c, half):
                for lv in range(LEVELS):
                    for p in range(2):
                        g = 2 * half + p
                        dve.wait_ge(STEP["pe_inv"].sem, STEP["pe_inv"].at(("tz", c, half, lv, p)))
                        if lv < LEVELS - 1:
                            dve.tensor_tensor(TI[p][:], TI[p][:], PB[4 + p][:], ALU.add).then_inc(di.sem, di.step())
                        dve.tensor_tensor(ZI[:, g, :], ZI[:, g, :], PB[6 + p][:], ALU.add).then_inc(di.sem, di.step(("z", c, half, lv, p)))

            for c in range(TB):
                if c > 0:
                    dve.wait_ge(pr.sem, pr.at(("sy", c - 1, CB - 1)))
                for half in range(2):
                    score_masks(c, half)
                    inverse_sums(c, half)
                for i in range(CB + 2):
                    p = i % 2
                    if i < CB:
                        if i >= 4:
                            dve.wait_ge(pr.sem, pr.at(("sy", c, i - 4)))
                            dve.wait_ge(dr.sem, dr.at(("s", c, i - 4)))
                        if c == 0:
                            dve.wait_ge(dr.sem, dr.at("s0"))
                        else:
                            dve.wait_ge(dr.sem, dr.at(("s", c - 1, i)))
                        dve.tensor_scalar(SM[i % 4][:], SS[:, i, :], DMID[:, 4 * i + c:4 * i + c + 1], None, ALU.mult).then_inc(dr.sem, dr.step(("sm", c, i)))
                    if 1 <= i <= CB:
                        dve.wait_ge(pr.sem, pr.at(("u", c, i - 1)))
                        if i >= 3:
                            dve.wait_ge(pr.sem, pr.at(("sy", c, i - 3)))
                        dve.tensor_copy(UB[(i - 1) % 2][:], PB[4 + (i - 1) % 2][:, 0:P]).then_inc(dr.sem, dr.step(("u", c, i - 1)))
                    if i >= 2:
                        cb = i - 2
                        q = cb % 2
                        dve.wait_ge(pr.sem, pr.at(("s", c, cb)))
                        if c > 0 or cb >= 2:
                            dve.wait_ge(dr.sem, dr.at(("s", c, cb - 2) if cb >= 2 else ("s", c - 1, CB - 2 + cb)))
                        dve.tensor_tensor(TS[q][:], PB[6 + q][:, 0:P], sq("blk"), ALU.mult).then_inc(dr.sem, dr.step())
                        k = dr.n
                        dve.wait_ge(dr.sem, k)
                        dve.tensor_tensor(TS[q][:], TS[q][:], SM_at(c, cb), ALU.add).then_inc(dr.sem, dr.step())
                        k = dr.n
                        dve.wait_ge(dr.sem, k)
                        dve.tensor_scalar(SS[:, cb, :], TS[q][:], DEND[:, 4 * cb + c:4 * cb + c + 1], None, ALU.mult).then_inc(dr.sem, dr.step(("s", c, cb)))
            dve.drain().then_inc(phase, 1)
            dve.wait_ge(phase, phase_done("dve"))
            pg, ag = STEP["pe_gn"], STEP["act_gn"]
            for cb in range(CB):
                dve.wait_ge(pg.sem, pg.at(("mean", cb)))
                dve.tensor_tensor(RT[:, cb, :], RT[:, cb, :], PB[cb % 4][:], ALU.subtract).then_inc(dg.sem, dg.step(("yc", cb)))
            dve.wait_ge(ag.sem, ag.at("root"))
            dve.reciprocal(KNI[0:HEADS, :], KNI[0:HEADS, :]).then_inc(dg.sem, dg.step("gni"))
            dve.wait_ge(fill, 32)
            def gn_lo(cb):
                dve.wait_ge(ag.sem, ag.at(("hi", cb)))
                dve.tensor_tensor(inl[:, cb, :], TV[cb % 2][:], inh[:, cb, :].bitcast(F32), ALU.subtract).then_inc(dg.sem, dg.step(("lo", cb)))
            for cb in range(CB):
                p = cb % 2
                if cb >= 2:
                    dve.wait_ge(STEP["pool_gn"].sem, STEP["pool_gn"].at(("o", cb - 2)))
                    dve.wait_ge(dg.sem, dg.at(("lo", cb - 2)))
                dve.wait_ge(pg.sem, pg.at(("bc1", cb)))
                dve.scalar_tensor_tensor(TG[p][:], RT[:, cb, :], col("gn_g", cb), PB[5 + p][:], ALU.mult, ALU.mult).then_inc(dg.sem, dg.step(("t1", cb)))
                k = dg.n
                dve.wait_ge(pg.sem, pg.at(("bc2", cb)))
                dve.tensor_tensor(TV[p][:], V[:, cb, :], PB[p][:], ALU.mult).then_inc(dg.sem, dg.step(("t2", cb)))
                k = dg.n
                dve.wait_ge(dg.sem, k)
                dve.scalar_tensor_tensor(TG[p][:], TG[p][:], col("gn_b", cb), TV[p][:], ALU.add, ALU.add).then_inc(dg.sem, dg.step(("t3", cb)))
                if cb >= 1:
                    gn_lo(cb - 1)
            gn_lo(CB - 1)
            dve.drain().then_inc(phase, 1)
            dve.wait_ge(phase, phase_done("dve"))
            dmlp, dk, da = STEP["dve_mlp"], STEP["dve_kv"], STEP["dve_att"]
            amlp, akv, aat, pkv = STEP["act_mlp"], STEP["act_kv"], STEP["act_att"], STEP["pe_kv"]
            dve.memset(small[:, 66:67], 64 * RMS_EPS).then_inc(dn.sem, dn.step("eps64"))

            def split_run(u0, n, loop=None):
                for u in range(u0, u0 + n):
                    split_lo(u + 3, loop)

            def add_x(stage, loop=None):
                for m in range(CB):
                    dve.wait_ge(lin.sem, lin.at(("bank", stage, m), loop))
                    dve.tensor_tensor(X[:, m, :], X[:, m, :], PB[m][:], ALU.add).then_inc(dmlp.sem, dmlp.step(("x", stage, m)))

            def gained_lo(name, dst_h, dst_l, gain):
                for kb in range(CB):
                    dve.wait_ge(an.sem, an.at(("hi", name, kb)))
                    dve.scalar_tensor_tensor(dst_l[:, kb, :], X[:, kb, :], col(gain, kb), dst_h[:, kb, :].bitcast(F32), ALU.mult, ALU.subtract).then_inc(dn.sem, dn.step(("lo", name, kb)))

            def mlp(layer, u0, name):
                k = rstd(name)
                gained_lo(name, inh, inl, f"ln_mlp{layer}")
                dve.wait_ge(dn.sem, k)
                with turns(dve, "dve", name, 4, 16) as lp:
                    lp.first = u0

                    def hidden_lo(m):
                        dve.wait_ge(amlp.sem, amlp.at(("hh", name, m), lp))
                        dve.wait_ge(STEP["pool_mlp"].sem, STEP["pool_mlp"].at(("hs", name, m), lp))
                        dve.tensor_tensor(hidl[:, m, :], HS[m % 4][:], hidh[:, m, :].bitcast(F32), ALU.subtract).then_inc(dmlp.sem, dmlp.step(("hl", name, m)))

                    split_run(u0, 8, lp)
                    for m in range(CB):
                        dve.wait_ge(lin.sem, lin.at(("bank", name + "up", m), lp))
                        if m >= 4:
                            dve.wait_ge(amlp.sem, amlp.at(("hh", name, m - 4), lp))
                            dve.wait_ge(STEP["pool_mlp"].sem, STEP["pool_mlp"].at(("hs", name, m - 4), lp))
                        dve.scalar_tensor_tensor(HR[m % 4][:], PB[m][:], 0.0, RS[:], ALU.max, ALU.mult).then_inc(dmlp.sem, dmlp.step(("r", name, m)))
                        if m >= 2:
                            hidden_lo(m - 2)
                    hidden_lo(6)
                    hidden_lo(7)
                    split_run(u0 + 8, 8, lp)
                    add_x(name, lp)

            split_run(UWO, 8)
            add_x("wo")
            mlp(0, UM0, "mlp0")
            dve.drain().then_inc(phase, 1)
            dve.wait_ge(phase, phase_done("dve"))
            k = rstd("kv")
            gained_lo("kv", inh, inl, "kv_norm")
            gained_lo("q", hidh, hidl, "ln_mix1")
            split_run(UKV, 4)
            dve.wait_ge(dn.sem, k)
            dve.wait_ge(lin.sem, lin.at(("bank", "kv", 0)))
            dve.tensor_tensor(KF[:], PB[1][:], RS[:], ALU.mult).then_inc(dk.sem, dk.step("kf"))
            dve.wait_ge(lin.sem, lin.at(("bank", "kv", 1)))
            dve.tensor_tensor(VF[:], PB[2][:], RS[:], ALU.mult).then_inc(dk.sem, dk.step("vf"))
            dve.wait_ge(akv.sem, akv.at("kroot"))
            dve.reciprocal(RKN[:], RKN[:]).then_inc(dk.sem, dk.step())
            k = dk.n
            dve.wait_ge(dk.sem, k)
            dve.scalar_tensor_tensor(KN[:], KF[:], col("k_gain"), RKN[:], ALU.mult, ALU.mult).then_inc(dk.sem, dk.step("kn"))
            split_run(UQ, 8)
            for m in range(CB):
                dve.wait_ge(lin.sem, lin.at(("bank", "q", m)))
                dve.tensor_tensor(QF[:, m, :], PB[m][:], RS[:], ALU.mult).then_inc(dk.sem, dk.step(("q", m)))
            dve.wait_ge(akv.sem, akv.at("qroot"))
            dve.reciprocal(QNI[0:HEADS, :], QNI[0:HEADS, :]).then_inc(dk.sem, dk.step("qni"))
            for cb in range(CB):
                dve.wait_ge(pkv.sem, pkv.at(("qbc", cb)))
                dve.scalar_tensor_tensor(QF[:, cb, :], QF[:, cb, :], col("q_gain"), PB[1 + cb % 2][:], ALU.mult, ALU.mult).then_inc(dk.sem, dk.step(("qn", cb)))
            dve.wait_ge(in_c, 16 * 12)
            dve.drain().then_inc(phase, 1)
            dve.wait_ge(phase, phase_done("dve"))
            pa = STEP["pe_att"]
            NT = 32
            for i in range(NT + 5):
                if i < NT:
                    h, nn = 2 * (i // 4) + i % 2, (i // 2) % 2
                    st = small[:, 2 + 16 * (i % 4):]
                    dve.wait_ge(pa.sem, pa.at(("s", i)))
                    if i >= 3:
                        dve.wait_ge(pa.sem, pa.at(("tr", i - 3)))
                    dve.scalar_tensor_tensor(S1[i % 3][:].rearrange("p (a b) -> p a b", a=2), BAND[:, nn:nn + 2, :],
                                                        -(2.0 ** (-8.0 * (h + 1) / HEADS)),
                                                        PB[i % 4][:].rearrange("p (a b) -> p a b", a=2), ALU.mult, ALU.add).then_inc(da.sem, da.step(("taken", i)))
                    k = da.n
                    dve.wait_ge(da.sem, k)
                    if i >= 4:
                        dve.wait_ge(da.sem, da.at(("den", i - 4)))
                    dve.tensor_reduce(st[:, 8:10], S1[i % 3][:].rearrange("p (a b) -> p a b", a=2), AX.X, ALU.max).then_inc(da.sem, da.step())
                    k = da.n
                    dve.wait_ge(da.sem, k)
                    dve.tensor_scalar(st[:, 0:2], st[:, 8:10], col("sinks", h), -1.0, ALU.max, ALU.mult).then_inc(da.sem, da.step(("nm", i)))
                if 1 <= i <= NT:
                    k = i - 1
                    st = small[:, 2 + 16 * (k % 4):]
                    dve.wait_ge(aat.sem, aat.at(("exp", k)))
                    dve.tensor_tensor(st[:, 6:8], st[:, 2:4], st[:, 4:6], ALU.add).then_inc(da.sem, da.step())
                    w = da.n
                    dve.wait_ge(da.sem, w)
                    dve.reciprocal(st[:, 6:8], st[:, 6:8]).then_inc(da.sem, da.step())
                    w = da.n
                    dve.wait_ge(da.sem, w)
                    for b in range(2):
                        pb = S1[k % 3][:, b * 256:(b + 1) * 256]
                        dve.tensor_scalar(pb, pb, st[:, 6 + b:7 + b], None, ALU.mult).then_inc(da.sem, da.step(*([("den", k)] if b else [])))
                        w = da.n
                if i >= 4 and (i - 4) % 2 == 1 and i - 4 < NT:
                    pr_ = (i - 4) // 2
                    cb, nn = divmod(pr_, 2)
                    dve.wait_ge(aat.sem, aat.at(("oh", pr_)))
                    cs = slice(nn * 256, (nn + 1) * 256)
                    dve.tensor_tensor(inl[:, cb, cs], PB[6 + pr_ % 2][:, 0:256], inh[:, cb, cs].bitcast(F32), ALU.subtract).then_inc(da.sem, da.step(("ol", pr_)))
            dve.drain().then_inc(phase, 1)
            dve.wait_ge(phase, phase_done("dve"))
            split_run(UBO, 8)
            add_x("bo")
            mlp(1, UM1, "mlp1")
            dve.drain().then_inc(phase, 1)
            dve.wait_ge(phase, phase_done("dve"))
            dad, drt, df, dff = (STEP["dve_" + n] for n in ("ada", "ret", "four", "ffn"))
            aad, art, af, affn = (STEP["act_" + n] for n in ("ada", "ret", "four", "ffn"))
            pad, prt, pf = (STEP["pe_" + n] for n in ("ada", "ret", "four"))
            y = vec[:, COLS["decay"]:COLS["decay"] + 8]
            neg, e, s_, s2, low = LT[2][:, 0:8], LT[1][:, 0:8], LT[3][:, 0:8], LT[4][:, 0:8], LT[3][:, 8:16]

            dve.tensor_scalar(neg, y, -1.0, None, ALU.mult).then_inc(dad.sem, dad.step())
            dve.wait_ge(dad.sem, dad.n)
            dve.tensor_tensor(e, neg, y, ALU.max).then_inc(dad.sem, dad.step("abs"))
            dve.wait_ge(dad.sem, dad.n)
            dve.tensor_scalar(low, neg, 0.0, None, ALU.max).then_inc(dad.sem, dad.step())
            dve.wait_ge(dad.sem, dad.n)
            dve.wait_ge(aad.sem, aad.at("sig"))
            dve.tensor_tensor(LT[0][:], LT[0][:], vec[:, COLS["c"]:COLS["c"] + 16], ALU.mult).then_inc(dad.sem, dad.step("silu"))
            dve.wait_ge(dad.sem, dad.n)
            dve.wait_ge(aad.sem, aad.at("eabs"))
            dve.tensor_scalar(s_, e, 2.0, None, ALU.add).then_inc(dad.sem, dad.step())
            dve.wait_ge(dad.sem, dad.n)
            dve.reciprocal(s_, s_).then_inc(dad.sem, dad.step())
            dve.wait_ge(dad.sem, dad.n)
            dve.tensor_tensor(s_, s_, e, ALU.mult).then_inc(dad.sem, dad.step())
            dve.wait_ge(dad.sem, dad.n)
            dve.tensor_tensor(s2, s_, s_, ALU.mult).then_inc(dad.sem, dad.step())
            dve.wait_ge(dad.sem, dad.n)
            dve.tensor_scalar(e, s2, 1.0 / 19, None, ALU.mult).then_inc(dad.sem, dad.step())
            dve.wait_ge(dad.sem, dad.n)
            for n in range(8, 0, -1):
                dve.scalar_tensor_tensor(e, e, 1.0 / (2 * n + 1), s2, ALU.add, ALU.mult).then_inc(dad.sem, dad.step())
                dve.wait_ge(dad.sem, dad.n)
            dve.scalar_tensor_tensor(e, e, 1.0, s_, ALU.add, ALU.mult).then_inc(dad.sem, dad.step())
            dve.wait_ge(dad.sem, dad.n)
            dve.scalar_tensor_tensor(LG[:], e, -2.0, low, ALU.mult, ALU.subtract).then_inc(dad.sem, dad.step())
            dve.wait_ge(dad.sem, dad.n)
            dve.wait_ge(in_a, 32)
            for tb in range(2):
                for d in range(2):
                    dve.tensor_scalar(WC[:, tb, d, :], LG[:, 4 * d:4 * d + 4], CPOS[:, 2 * tb + d:2 * tb + d + 1], None, ALU.mult).then_inc(dad.sem, dad.step("cpos"))
                    dve.wait_ge(dad.sem, dad.n)
            dve.wait_ge(aad.sem, aad.at("ch"))
            dve.tensor_tensor(CST[:, :, 2:4], LT[0][:].rearrange("p (b k) -> p k b", b=2), CST[:, :, 0:2].bitcast(F32), ALU.subtract).then_inc(dad.sem, dad.step("cl"))
            dve.wait_ge(aad.sem, aad.at("wc"))
            dve.tensor_scalar(WC[:], WC[:], 1.0 / math.sqrt(P), None, ALU.mult).then_inc(dad.sem, dad.step("wcs"))
            split_run(UADA, 48)
            dve.wait_ge(pad.sem, pad.at(("turned", 5)))
            b_ada = vec[:, COLS["b_ada"]:COLS["b_ada"] + 48]
            dve.tensor_tensor(adac[:], PB[4][:, 0:96].rearrange("p (a b) -> p a b", b=2), b_ada.unsqueeze(2).to_broadcast([P, 48, 2]), ALU.add).then_inc(dad.sem, dad.step())
            dve.wait_ge(dad.sem, dad.n)
            gains = lambda name: vec[:, COLS[name]:COLS[name] + 8]
            dve.scalar_tensor_tensor(GA, adac[:, 8:16, 0], 1.0, gains("g_mix_pre"), ALU.add, ALU.mult).then_inc(dad.sem, dad.step())
            dve.scalar_tensor_tensor(GAC, adac[:, 8:16, 1], 1.0, gains("g_mix_pre"), ALU.add, ALU.mult).then_inc(dad.sem, dad.step())
            dve.tensor_tensor(GP, adac[:, 16:24, 0], gains("g_mix_post"), ALU.mult).then_inc(dad.sem, dad.step())
            dve.scalar_tensor_tensor(GF, adac[:, 32:40, 0], 1.0, gains("g_ffn_pre"), ALU.add, ALU.mult).then_inc(dad.sem, dad.step())
            dve.tensor_tensor(GFP, adac[:, 40:48, 0], gains("g_ffn_post"), ALU.mult).then_inc(dad.sem, dad.step())
            dve.drain().then_inc(phase, 1)
            dve.wait_ge(phase, phase_done("dve"))

            def modulated(name, src, gain, tmp, dst_h, dst_l, shift, n=T):
                dve.wait_ge(dn.sem, rstd(name, n))

                def lo(kb):
                    dve.wait_ge(aad.sem, aad.at(("hi", name, kb)))
                    dve.scalar_tensor_tensor(dst_l[:, kb, :n], tmp[kb % 2][:, :n], shift(kb), dst_h[:, kb, :n].bitcast(F32), ALU.add, ALU.subtract).then_inc(dad.sem, dad.step(("lo", name, kb)))

                for kb in range(CB):
                    if kb >= 2:
                        dve.wait_ge(dad.sem, dad.at(("lo", name, kb - 2)))
                    dve.scalar_tensor_tensor(tmp[kb % 2][:, :n], src[:, kb, :n], gain[:, kb:kb + 1], RS[:, :n], ALU.mult, ALU.mult).then_inc(dad.sem, dad.step(("t", name, kb)))
                    if kb >= 1:
                        lo(kb - 1)
                lo(CB - 1)

            dve.wait_ge(in_a, 48)
            modulated("ctx", CX, GAC, CT, chh, chl, lambda kb: adac[:, kb, 1:2], CTX)
            split_run(UCTX, 8)
            dve.drain().then_inc(phase, 1)
            dve.wait_ge(phase, phase_done("dve"))
            modulated("lat", X, GA, TQ, inh, inl, lambda kb: adac[:, kb, 0:1])
            split_run(UIN, 8)
            for m in range(CB):
                dve.wait_ge(lin.sem, lin.at(("bank", "qk", m)))
                dve.tensor_copy(QK[:, m, :], PB[m][:]).then_inc(drt.sem, drt.step(("qk", m)))
            split_run(UIN + 8, 8)
            for tb in range(TB):
                dve.wait_ge(lin.sem, lin.at(("bank", "v", tb)))
                dve.tensor_copy(VL[:, tb, :], PB[tb][:]).then_inc(drt.sem, drt.step(("vl", tb)))
            for m in range(RH):
                dve.wait_ge(art.sem, art.at(("sig", m)))
                dve.tensor_tensor(GS[:, m, :], TQ[m % 2][:], PB[4 + m][:], ALU.mult).then_inc(drt.sem, drt.step(("g", m)))
            split_run(UIN + 16, 4)
            for g in range(4):
                dve.wait_ge(lin.sem, lin.at(("bank", "f", g)))
                dve.tensor_copy(FQ[:, g, :], PB[g][:]).then_inc(drt.sem, drt.step(("fq", g)))
            dve.wait_ge(in_t, 112)
            for m in range(CB):
                dve.wait_ge(prt.sem, prt.at(("rot", m)))
                dve.wait_ge(drt.sem, drt.at(("rope", m - 2) if m >= 2 else ("g", RH - 1)))
                dve.tensor_tensor(TQ[m % 2][:], PB[4 + m % 4][:], SIN[:], ALU.mult).then_inc(drt.sem, drt.step())
                dve.tensor_tensor(QK[:, m, :], QK[:, m, :], COS[:], ALU.mult).then_inc(drt.sem, drt.step())
                k = drt.n
                dve.wait_ge(drt.sem, k)
                dve.tensor_tensor(QK[:, m, :], QK[:, m, :], TQ[m % 2][:], ALU.add).then_inc(drt.sem, drt.step(("rope", m)))
            dve.drain().then_inc(phase, 1)
            dve.wait_ge(phase, phase_done("dve"))
            for g in range(4):
                dve.wait_ge(af.sem, af.at(("hi", g)))
                dve.tensor_tensor(inl[:, 4 + g, :], PB[2 + g % 2][:], inh[:, 4 + g, :].bitcast(F32), ALU.subtract).then_inc(df.sem, df.step(("lo", g)))
            dve.drain().then_inc(phase, 1)
            dve.wait_ge(phase, phase_done("dve"))

            def distances(h):
                if h >= 2:
                    dve.wait_ge(drt.sem, drt.at(("p", h - 2, TB - 1)))
                dve.tensor_scalar(DM[h % 2][:], AFT[:], LG[:, h:h + 1], None, ALU.mult).then_inc(drt.sem, drt.step())
                k = drt.n
                dve.wait_ge(drt.sem, k)
                dve.scalar_tensor_tensor(DM[h % 2][:], BEF[:], LG[:, 4 + h:5 + h], DM[h % 2][:], ALU.mult, ALU.add).then_inc(drt.sem, drt.step(("dm", h)))

            def ret_norm(h):
                dve.wait_ge(art.sem, art.at(("root", h)))
                dve.reciprocal(RR[:], RR[:]).then_inc(drt.sem, drt.step())
                k = drt.n
                dve.wait_ge(drt.sem, k)
                dve.tensor_tensor(RET[h % 2][:], RET[h % 2][:], RR[:], ALU.mult).then_inc(drt.sem, drt.step(("n", h)))
                k = drt.n
                dve.wait_ge(drt.sem, k)
                dve.tensor_tensor(RET[h % 2][:], RET[h % 2][:], GS[:, h, :], ALU.mult).then_inc(drt.sem, drt.step(("ret", h)))
                dve.wait_ge(art.sem, art.at(("hi", h)))
                dve.tensor_tensor(inl[:, h, :], RET[h % 2][:], inh[:, h, :].bitcast(F32), ALU.subtract).then_inc(drt.sem, drt.step(("lo", h)))

            distances(0)
            distances(1)
            for h in range(RH):
                if h >= 1:
                    dve.wait_ge(prt.sem, prt.at(("out", h - 1)))
                for d in range(2):
                    dve.wait_ge(art.sem, art.at(("xi", h, d)))
                    dve.tensor_tensor(QX[d][:], QK[:, h, :], HE[d][:], ALU.mult).then_inc(drt.sem, drt.step(("qx", h, d)))
                dve.wait_ge(art.sem, art.at(("dm", h)))
                for sb in range(TB):
                    dve.wait_ge(prt.sem, prt.at(("s", h, sb)))
                    dve.scalar_tensor_tensor(PSC[sb][:], PB[sb][:], 1.0 / math.sqrt(P), DM[h % 2][:, 384 - P * sb:896 - P * sb], ALU.mult, ALU.mult).then_inc(drt.sem, drt.step(("p", h, sb)))
                if h + 2 < RH:
                    distances(h + 2)
                if h >= 1:
                    ret_norm(h - 1)
            ret_norm(RH - 1)
            dve.drain().then_inc(phase, 1)
            dve.wait_ge(phase, phase_done("dve"))
            split_run(UOUT, 8)
            for m in range(CB):
                dve.wait_ge(lin.sem, lin.at(("bank", "mx", m)))
                dve.tensor_copy(MX[:, m, :], PB[m][:]).then_inc(drt.sem, drt.step(("mx", m)))
            dve.wait_ge(dn.sem, rstd("mx"))

            def add_normed(src, gain, dst, steps, mark):
                for kb in range(CB):
                    dve.scalar_tensor_tensor(src[:, kb, :], src[:, kb, :], gain[:, kb:kb + 1], RS[:], ALU.mult, ALU.mult).then_inc(steps.sem, steps.step(("nx", mark, kb)))
                    if kb >= 1:
                        dve.wait_ge(steps.sem, steps.at(("nx", mark, kb - 1)))
                        dve.tensor_tensor(dst[:, kb - 1, :], dst[:, kb - 1, :], src[:, kb - 1, :], ALU.add).then_inc(steps.sem, steps.step((mark, kb - 1)))
                dve.wait_ge(steps.sem, steps.at(("nx", mark, CB - 1)))
                dve.tensor_tensor(dst[:, CB - 1, :], dst[:, CB - 1, :], src[:, CB - 1, :], ALU.add).then_inc(steps.sem, steps.step((mark, CB - 1)))

            add_normed(MX, GP, X, drt, "x")
            modulated("fp", X, GF, TQ, inh, inl, lambda kb: adac[:, 24 + kb, 0:1])
            dve.drain().then_inc(phase, 1)
            dve.wait_ge(phase, phase_done("dve"))
            dve.wait_ge(spill, 48)
            taps = vec[:, COLS["conv_w"]:COLS["conv_w"] + 176].rearrange("p (a b c) -> p a b c", a=4, b=2)
            row = lambda ap: ap.rearrange("p (r w) -> p r w", w=GRID)

            def gated(s):
                q, name, loop = s.q, s.name, s.loop
                if s.before is not None:
                    dve.wait_ge(dff.sem, prior(dff, "lo", s.before, 1))
                dve.tensor_copy(CWT[q][:], taps[:, :, :, s.blocks]).then_inc(dff.sem, dff.step(("cw", name, q)))
                dve.wait_ge(dff.sem, dff.at(("cw", name, q), loop))
                for j in range(2):
                    for step in range(2):
                        for hf in range(2):
                            m = 2 * j + hf
                            a, b = row(CV[m][:]), row(PB[4 * q + m][:])
                            if step == 0:
                                dve.wait_ge(affn.sem, affn.at(("cv", name, q, m), loop))
                                dve.scalar_tensor_tensor(a[:, :, 1:GRID], b[:, :, 0:GRID - 1], CWT[q][:, 0, hf, j:j + 1], a[:, :, 1:GRID], ALU.mult, ALU.add).then_inc(dff.sem, dff.step(("c1", name, q, m)))
                            else:
                                dve.wait_ge(dff.sem, dff.at(("c1", name, q, m), loop))
                                dve.scalar_tensor_tensor(a[:, :, 0:GRID - 1], b[:, :, 1:GRID], CWT[q][:, 2, hf, j:j + 1], a[:, :, 0:GRID - 1], ALU.mult, ALU.add).then_inc(dff.sem, dff.step(("cv", name, q, m)))
                for j in range(2):
                    dve.wait_ge(affn.sem, affn.at(("sg", name, q, j), loop))
                    dve.wait_ge(dff.sem, dff.at(("cv", name, q, 2 * j + 1), loop))
                    dve.tensor_tensor(HT[j][:], SG[j][:], CV[2 * j + 1][:], ALU.mult).then_inc(dff.sem, dff.step(("h", name, q, j)))
                for j in range(2):
                    dve.wait_ge(affn.sem, affn.at(("hh", name, q, j), loop))
                    dve.tensor_tensor(GL[:, s.at[j]], HT[j][:], GH[:, s.at[j]].bitcast(F32), ALU.subtract).then_inc(dff.sem, dff.step(("lo", name, q, j)))

            up_passes(dve, "dve", split_run, gated)
            split_run(UF + 44, NFB - 3)
            for m in (4, 5, 6, 7, 0, 1, 2, 3):
                dve.wait_ge(lin.sem, lin.at(("bank", "down", m)))
                dve.tensor_copy(FO[:, m, :], PB[m][:]).then_inc(dff.sem, dff.step(("fo", m)))
            dve.wait_ge(dn.sem, rstd("fo"))
            dve.wait_ge(fill, 48)
            add_normed(FO, GFP, X2, dff, "out")

        @block.tensor
        def _(pe):
            pn, pl = STEP["pe_norm"], STEP["pe_lora"]

            def sums(name, n=T):
                for kb in range(CB):
                    pe.wait_ge(STEP["act_norm"].sem, STEP["act_norm"].at(("sq", name, kb)))
                    pe.matmul(PB[0][:, :n], sq("ones"), SQT[kb % 2][:, :n], start=kb == 0, stop=kb == CB - 1).then_inc(pn.sem, pn.step(("sum", name, kb)))

            def product(o, u, wc, xh, xl_, start, stop):
                w, r = whi[u % SLOTS], wlo[u % SLOTS]
                pe.matmul(o, w[:, wc], xh, start=start, stop=False)
                pe.matmul(o, w[:, wc], xl_, start=False, stop=False)
                return pe.matmul(o, r[:, wc], xh, start=False, stop=stop)

            def token_product(o, u, wc, xh, xl_, start, stop):
                w, r = whi[u % SLOTS], wlo[u % SLOTS]
                pe.matmul(o, xh, w[:, wc], start=start, stop=False)
                pe.matmul(o, xl_, w[:, wc], start=False, stop=False)
                return pe.matmul(o, xh, r[:, wc], start=False, stop=stop)

            pe.wait_ge(in_c, 16 * 11)
            sums("n0")
            n = q = 0
            for j, (name, w1, width) in enumerate((("g", lg1, LORA_G), ("w", lw1, LORA_W), ("a", la1, LORA_A))):
                if j == 0:
                    pe.wait_ge(STEP["act_norm"].sem, STEP["act_norm"].at(("root", "n0")))
                else:
                    pe.wait_ge(STEP["act_lora"].sem, STEP["act_lora"].at(("hid", "gwa"[j - 1], 1 if j == 1 else 0)))
                for kb in range(CB):
                    pe.wait_ge(STEP["dve_lora"].sem, STEP["dve_lora"].at(("x", n)))
                    mm = pe.matmul(PB[0][0:min(width, P), :], w1[:, kb, 0:min(width, P)], xl[n % 4][:], start=kb == 0, stop=kb == CB - 1)
                    if width > P:
                        mm = pe.matmul(PB[1][0:width - P, :], w1[:, kb, P:width], xl[n % 4][:], start=kb == 0, stop=kb == CB - 1)
                    mm.then_inc(pl.sem, pl.step(("used", n), *([("hid", name)] if kb == CB - 1 else [])))
                    n += 1
                pe.wait_ge(STEP["act_lora"].sem, STEP["act_lora"].at(("hid", name, 1 if width > P else 0)))
                for m in range(CB):
                    if q >= 6:
                        pe.wait_ge(STEP["act_lora"].sem, STEP["act_lora"].at(("out", "gwa"[(q - 6) // 8], (q - 6) % 8)))
                    o = PB[2 + q % 6]
                    ms = slice(m * P, (m + 1) * P)
                    if name == "g":
                        pe.matmul(o[:], lg2a[:, ms], hid1[0][:], start=True, stop=False)
                        mm = pe.matmul(o[:], lg2b[0:LORA_G - P, ms], hid1[1][0:LORA_G - P, :], start=False, stop=True)
                    else:
                        w2 = lw2 if name == "w" else la2
                        mm = pe.matmul(o[:], w2[0:width, ms], hid1[0][0:width, :], start=True, stop=True)
                    mm.then_inc(pl.sem, pl.step(("out", name, m), *([("outs", name)] if m == CB - 1 else [])))
                    q += 1
            pe.drain().then_inc(phase, 1)
            pe.wait_ge(phase, phase_done("pe"))
            for u in range(24):
                p, kb = divmod(u, 8)
                pe.wait_ge(STEP["dve_mix"].sem, STEP["dve_mix"].at(("lo", u)))
                pe.wait_ge(w_lo, u + 1)
                for m in range(CB):
                    if kb == 0 and p > 0:
                        pe.wait_ge(STEP["dve_mix"].sem, STEP["dve_mix"].at(("taken", p - 1, m)))
                    product(PB[m][:], u, chunk(m), xmh[u % NR][:], xml[u % NR][:], kb == 0, kb == 7).then_inc(
                        lin.sem, lin.step(("bank", p, m), ("used", u)))
            pe.drain().then_inc(phase, 1)
            pe.wait_ge(phase, phase_done("pe"))

            pp, ps, pi, pt, pr, pg = (STEP["pe_" + n] for n in ("prep", "score", "inv", "tok", "rec", "gn"))
            for cb in range(CB):
                pe.wait_ge(STEP["act_prep"].sem, STEP["act_prep"].at(("ksq", cb)))
                pe.matmul(PB[0][0:HEADS, :], sel[:, cb, :], PREP["e1"][cb % 2][:], start=cb == 0, stop=cb == CB - 1).then_inc(pp.sem, pp.step(("ksum", cb)))
            pe.wait_ge(STEP["dve_prep"].sem, STEP["dve_prep"].at("kni"))
            for cb in range(CB + 1):
                if cb < CB:
                    if cb >= 2:
                        pe.wait_ge(STEP["dve_prep"].sem, STEP["dve_prep"].at(("kn", cb - 2)))
                    pe.matmul(PB[1 + cb % 2][:], selt[0:HEADS, chunk(cb)], KNI[0:HEADS, :], start=True, stop=True).then_inc(pp.sem, pp.step(("bc", cb)))
                if cb > 0:
                    pe.wait_ge(STEP["dve_prep"].sem, STEP["dve_prep"].at(("rk", cb - 1)))
                    pe.matmul(PB[3][0:HEADS, :], sel[:, cb - 1, :], PREP["rk"][(cb - 1) % 2][:], start=cb == 1, stop=cb == CB).then_inc(pp.sem, pp.step(("rks", cb - 1)))
            pe.drain().then_inc(phase, 1)
            pe.wait_ge(phase, phase_done("pe"))

            last_taken = {0: None, 1: None}

            def scores(c, half):
                for kind, (a, b) in enumerate(((AT, BT), (BT, AT), (KT, AT), (BT, RT), (KT, RT))):
                    for p in range(2):
                        if last_taken[p] is not None:
                            pe.wait_ge(last_taken[p][0].sem, last_taken[p][0].at(last_taken[p][1]))
                        rows = slice(64 * p, 64 * p + 64)
                        for s in range(4):
                            cb = 4 * half + s
                            mm = pe.matmul(PB[p][:, chunk(s)], a[rows, cb, chunk(c)], b[rows, cb, chunk(c)], start=True, stop=True)
                        mm.then_inc(ps.sem, ps.step((c, half, kind, p)))
                        last_taken[p] = (STEP["dve_score"], ("taken", c, half, kind, p))

            def inverse(c, half):
                for lv in range(LEVELS):
                    for p in range(2):
                        g = 2 * half + p
                        pe.wait_ge(STEP["pool_score"].sem, STEP["pool_score"].at(("lm", c, half, lv, p)))
                        if lv > 0:
                            pe.wait_ge(STEP["dve_inv"].sem, STEP["dve_inv"].at(("z", c, half, lv - 1, p)))
                        for s in range(4):
                            mm = pe.matmul(PB[2 + p][:, chunk(s)], LM[p][:, chunk(s)], ZI[:, g, chunk(s)], start=True, stop=True)
                        mm.then_inc(pi.sem, pi.step(("q", c, half, lv, p)))
                    for p in range(2):
                        g = 2 * half + p
                        pe.wait_ge(STEP["act_inv"].sem, STEP["act_inv"].at(("q", c, half, lv, p)))
                        for s in range(4):
                            if lv < LEVELS - 1:
                                pe.matmul(PB[4 + p][:, chunk(s)], QS[p][:, chunk(s)], TI[p][:, chunk(s)], start=True, stop=True)
                            mm = pe.matmul(PB[6 + p][:, chunk(s)], TI[p][:, chunk(s)], QS[p][:, chunk(s)], start=True, stop=True)
                        mm.then_inc(pi.sem, pi.step(("tz", c, half, lv, p)))

            def token_major(c):
                for which, src in (("v", V), ("k", KT), ("b", BT)):
                    for half in range(2):
                        pe.wait_ge(last_taken[half][0].sem, last_taken[half][0].at(last_taken[half][1]))
                        for s in range(4):
                            mm = pe.transpose(PB[half][:, chunk(s)], src[:, 4 * half + s, chunk(c)], sq("ident"))
                        mm.then_inc(pt.sem, pt.step(("tr", c, which, half)))
                        last_taken[half] = (STEP["act_tok"], ("tr", c, which, half))

            for c in range(TB):
                for half in range(2):
                    scores(c, half)
                    inverse(c, half)
                token_major(c)
                for h in range(2):
                    for p in range(2):
                        pe.wait_ge(STEP["dve_inv"].sem, STEP["dve_inv"].at(("z", c, h, LEVELS - 1, p)))
                for which in "vkb":
                    for h in range(2):
                        pe.wait_ge(STEP["act_tok"].sem, STEP["act_tok"].at(("tr", c, which, h)))
                for i in range(CB + 2):
                    if i < CB:
                        p, g, s = i % 2, 2 * (i // 4), i % 4
                        pe.wait_ge(STEP["dve_rec"].sem, STEP["dve_rec"].at(("sm", c, i)))
                        if i >= 2:
                            pe.wait_ge(STEP["act_rec"].sem, STEP["act_rec"].at(("w", c, i - 2)))
                        o = PB[2 + p]
                        pe.matmul(o[:, 0:P], AT[:, i, chunk(c)], SM[i % 4][:], start=True, stop=False)
                        for h in range(2):
                            mm = pe.matmul(o[:, 64 * h:64 * h + 64], MT[:, g + h, chunk(s)], VT[:, P * i + 64 * h:P * i + 64 * h + 64], start=False, stop=h == 1)
                        mm.then_inc(pr.sem, pr.step(("w", c, i)))
                    if 1 <= i <= CB:
                        cb = i - 1
                        p, g, s = cb % 2, 2 * (cb // 4), cb % 4
                        pe.wait_ge(STEP["act_rec"].sem, STEP["act_rec"].at(("w", c, cb)))
                        if cb >= 2:
                            pe.wait_ge(STEP["dve_rec"].sem, STEP["dve_rec"].at(("u", c, cb - 2)))
                        for h in range(2):
                            mm = pe.matmul(PB[4 + p][:, 64 * h:64 * h + 64], ZI[:, g + h, chunk(s)], WB[p][:, 64 * h:64 * h + 64], start=True, stop=True)
                        mm.then_inc(pr.sem, pr.step(("u", c, cb)))
                    if i >= 2:
                        cb = i - 2
                        p, g, s = cb % 2, 2 * (cb // 4), cb % 4
                        pe.wait_ge(STEP["dve_rec"].sem, STEP["dve_rec"].at(("u", c, cb)))
                        if cb >= 2:
                            pe.wait_ge(STEP["dve_rec"].sem, STEP["dve_rec"].at(("s", c, cb - 2)))
                            pe.wait_ge(STEP["act_rec"].sem, STEP["act_rec"].at(("y", c, cb - 2)))
                        pe.matmul(PB[6 + p][:, 0:P], BT[:, cb, chunk(c)], UB[p][:], start=True, stop=False)
                        mm = pe.matmul(PB[6 + p][:, 0:P], KT[:, cb, chunk(c)], VT[:, chunk(cb)], start=False, stop=True)
                        mm.then_inc(pr.sem, pr.step(("s", c, cb)))
                        pe.matmul(PB[p][:, 0:P], SM[cb % 4][:], RT[:, cb, chunk(c)], start=True, stop=False)
                        for h in range(2):
                            hs = slice(64 * h, 64 * h + 64)
                            pe.matmul(PB[p][hs, 0:P], UB[p][:, hs], GBm[:, g + h, chunk(s)], start=False, stop=False)
                            mm = pe.matmul(PB[p][hs, 0:P], VT[:, P * cb + 64 * h:P * cb + 64 * h + 64], GKm[:, g + h, chunk(s)], start=False, stop=True)
                        mm.then_inc(pr.sem, pr.step(("sy", c, cb)))
                last_taken[0] = (STEP["act_rec"], ("y", c, CB - 2))
                last_taken[1] = (STEP["act_rec"], ("y", c, CB - 1))
            pe.drain().then_inc(phase, 1)
            pe.wait_ge(phase, phase_done("pe"))
            for cb in range(CB):
                if cb >= 4:
                    pe.wait_ge(STEP["dve_gn"].sem, STEP["dve_gn"].at(("yc", cb - 4)))
                pe.matmul(PB[cb % 4][:], sq("blk64"), RT[:, cb, :], start=True, stop=True).then_inc(pg.sem, pg.step(("mean", cb)))
            for cb in range(CB):
                pe.wait_ge(STEP["act_gn"].sem, STEP["act_gn"].at(("sq", cb)))
                pe.matmul(PB[4][0:HEADS, :], sel[:, cb, :], SQT[cb % 2][:], start=cb == 0, stop=cb == CB - 1).then_inc(pg.sem, pg.step(("var", cb)))
            pe.wait_ge(STEP["dve_gn"].sem, STEP["dve_gn"].at("gni"))
            for cb in range(CB):
                if cb >= 2:
                    pe.wait_ge(STEP["dve_gn"].sem, STEP["dve_gn"].at(("t2", cb - 2)))
                pe.matmul(PB[5 + cb % 2][:], selt[0:HEADS, chunk(cb)], KNI[0:HEADS, :], start=True, stop=True).then_inc(pg.sem, pg.step(("bc1", cb)))
                pe.matmul(PB[cb % 2][:], selt[0:HEADS, chunk(cb)], RKS[0:HEADS, :], start=True, stop=True).then_inc(pg.sem, pg.step(("bc2", cb)))
            pe.drain().then_inc(phase, 1)
            pe.wait_ge(phase, phase_done("pe"))
            dmlp = STEP["dve_mlp"]

            def wide(u0, mh, ml, stage, loop=None, ready=None, free=None):
                for k in range(CB):
                    if ready is not None:
                        pe.wait_ge(ready[0].sem, ready[0].at((*ready[1], k), loop))
                    pe.wait_ge(w_lo, turn(u0 + k + 1, loop))
                    for m in range(CB):
                        if k == 0 and free is not None:
                            pe.wait_ge(free[0].sem, free[0].at((*free[1], m), loop, ago=free[2]))
                        product(PB[m][:], u0 + k, chunk(m), mh[:, k, :], ml[:, k, :], k == 0, k == CB - 1).then_inc(
                            lin.sem, lin.step(("bank", stage, m), ("used", u0 + k)))

            def x_sums(name, prev):
                pe.wait_ge(x_sum.sem, x_done(prev, 0))
                sums(name)

            def mlp(layer, u0, name, prev):
                x_sums(name, prev)
                pe.wait_ge(STEP["act_norm"].sem, STEP["act_norm"].at(("root", name)))
                for k in range(CB):
                    pe.wait_ge(STEP["dve_norm"].sem, STEP["dve_norm"].at(("lo", name, k)))
                with turns(pe, "pe", name, 4, 16) as lp:
                    lp.first = u0
                    wide(u0, inh, inl, name + "up", lp, free=(dmlp, ("x", name), 1))
                    wide(u0 + 8, hidh, hidl, name, lp, ready=(dmlp, ("hl", name)), free=(dmlp, ("r", name), 0))

            wide(UWO, inh, inl, "wo")
            mlp(0, UM0, "mlp0", "wo")
            pe.drain().then_inc(phase, 1)
            pe.wait_ge(phase, phase_done("pe"))
            pkv, dk = STEP["pe_kv"], STEP["dve_kv"]
            x_sums("kv", "mlp0")
            for j in range(4):
                pe.wait_ge(STEP["dve_norm"].sem, STEP["dve_norm"].at(("lo", "kv", 2 * j + 1)))
                pe.wait_ge(w_lo, UKV + j + 1)
                for a in range(2):
                    for m in range(2):
                        kb = 2 * j + a
                        product(PB[1 + m][:], UKV + j, slice(a * 256 + m * P, a * 256 + (m + 1) * P), inh[:, kb, :], inl[:, kb, :], kb == 0, kb == 7).then_inc(
                            lin.sem, lin.step(("bank", "kv", m), ("used", UKV + j)))
            pe.wait_ge(STEP["act_kv"].sem, STEP["act_kv"].at("ksq"))
            pe.matmul(PB[3][:], sq("blk64"), HS[2][:], start=True, stop=True).then_inc(pkv.sem, pkv.step("kmean"))
            pe.wait_ge(dk.sem, dk.at("vf"))
            for n in range(TB):
                mm = pe.transpose(PB[4][:, chunk(n)], VF[:, chunk(n)], sq("ident"))
            mm.then_inc(pkv.sem, pkv.step("vt"))
            pe.wait_ge(STEP["act_norm"].sem, STEP["act_norm"].at(("root", "kv")))
            pe.wait_ge(STEP["act_kv"].sem, STEP["act_kv"].at("kroot"))
            pe.wait_ge(STEP["act_kv"].sem, STEP["act_kv"].at("vk"))
            wide(UQ, hidh, hidl, "q", ready=(STEP["dve_norm"], ("lo", "q")))
            for cb in range(CB):
                pe.wait_ge(STEP["act_kv"].sem, STEP["act_kv"].at(("qsq", cb)))
                pe.matmul(PB[0][0:HEADS, :], sel[:, cb, :], SQT[cb % 2][:], start=cb == 0, stop=cb == CB - 1).then_inc(pkv.sem, pkv.step(("qsum", cb)))
            pe.wait_ge(dk.sem, dk.at("qni"))
            for cb in range(CB):
                if cb >= 2:
                    pe.wait_ge(dk.sem, dk.at(("qn", cb - 2)))
                pe.matmul(PB[1 + cb % 2][:], selt[0:HEADS, chunk(cb)], QNI[0:HEADS, :], start=True, stop=True).then_inc(pkv.sem, pkv.step(("qbc", cb)))
            pe.wait_ge(kdup, 64)
            pe.drain().then_inc(phase, 1)
            pe.wait_ge(phase, phase_done("pe"))
            pa, aat, da = STEP["pe_att"], STEP["act_att"], STEP["dve_att"]
            NT = 32
            for i in range(NT + 3):
                if i < NT:
                    cb, nn, par = i // 4, (i // 2) % 2, i % 2
                    kd = KD[cb // 4]
                    rows_ = slice(64 * par, 64 * par + 64)
                    if i >= 4:
                        pe.wait_ge(da.sem, da.at(("taken", i - 4)))
                    for b in range(2):
                        n = 2 * nn + b
                        o = PB[i % 4][:, b * 256:(b + 1) * 256]
                        if n == 0:
                            for z in range(2):
                                mm = pe.matmul(o[:, z * P:(z + 1) * P], QF[rows_, cb, chunk(0)], kd[rows_, chunk(0)], start=True, stop=True)
                        else:
                            mm = pe.matmul(o, QF[rows_, cb, chunk(n)], kd[rows_, (n - 1) * P:(n + 1) * P], start=True, stop=True)
                    mm.then_inc(pa.sem, pa.step(("s", i)))
                if 2 <= i < NT + 2:
                    k = i - 2
                    pe.wait_ge(da.sem, da.at(("den", k)))
                    if k >= 2:
                        pe.wait_ge(aat.sem, aat.at(("ptr", k - 2)))
                    for j in range(4):
                        mm = pe.transpose(PB[4 + k % 2][:, chunk(j)], S1[k % 3][:, chunk(j)], sq("ident"))
                    mm.then_inc(pa.sem, pa.step(("tr", k)))
                if i >= 3:
                    k = i - 3
                    cb, nn, par = k // 4, (k // 2) % 2, k % 2
                    pr_ = k // 2
                    pe.wait_ge(aat.sem, aat.at(("ptr", k)))
                    if pr_ >= 2 and par == 0:
                        pe.wait_ge(da.sem, da.at(("ol", pr_ - 2)))
                    vs = slice(64 * (cb // 4), 64 * (cb // 4) + 64)
                    for b in range(2):
                        n = 2 * nn + b
                        o = PB[6 + pr_ % 2][64 * par:64 * par + 64, chunk(b)]
                        if n > 0:
                            pe.matmul(o, VK[:, n - 1, vs], PTR[k % 3][:, chunk(2 * b)], start=True, stop=False)
                        mm = pe.matmul(o, VK[:, n, vs], PTR[k % 3][:, chunk(2 * b + 1)], start=n == 0, stop=True)
                    mm.then_inc(pa.sem, pa.step(("pv", k)))
            pe.drain().then_inc(phase, 1)
            pe.wait_ge(phase, phase_done("pe"))
            wide(UBO, inh, inl, "bo")
            mlp(1, UM1, "mlp1", "bo")
            pe.drain().then_inc(phase, 1)
            pe.wait_ge(phase, phase_done("pe"))
            pad, prt, pf = (STEP["pe_" + n] for n in ("ada", "ret", "four"))
            aad, art, af = (STEP["act_" + n] for n in ("ada", "ret", "four"))
            dad, drt, df, dff = (STEP["dve_" + n] for n in ("ada", "ret", "four", "ffn"))

            def turned(n):
                for hf in range(2):
                    pe.wait_ge(aad.sem, aad.at(("row", n, hf)))
                for m in range(CB):
                    mm = pe.matmul(PB[4][:, 2 * (8 * n + m):2 * (8 * n + m) + 2], AR[n % 2][0:4, chunk(m)], SUM2[0:4, :], start=True, stop=True)
                mm.then_inc(pad.sem, pad.step(("turned", n)))

            pe.wait_ge(in_a, 32)
            pe.wait_ge(aad.sem, aad.at("ch"))
            pe.wait_ge(dad.sem, dad.at("cl"))
            for n in range(6):
                for k in range(CB):
                    u = UADA + 8 * n + k
                    pe.wait_ge(w_lo, u + 1)
                    for hf in range(2):
                        if k == 0 and n >= 2:
                            pe.wait_ge(aad.sem, aad.at(("row", n - 2, hf)))
                        o, c = PB[2 * (n % 2) + hf][0:4, :], slice(512 * hf, 512 * hf + 512)
                        pe.matmul(o, CST[:, k, :], whi[u % SLOTS][:, c], start=k == 0, stop=False)
                        mm = pe.matmul(o, CST[:, k, :], wlo[u % SLOTS][:, c], start=False, stop=k == CB - 1)
                        mm.then_inc(lin.sem, lin.step(("row", n, hf), ("used", u)))
                    if k == 1 and n >= 1:
                        turned(n - 1)
            turned(5)
            pe.drain().then_inc(phase, 1)
            pe.wait_ge(phase, phase_done("pe"))
            sums("ctx", CTX)
            pe.wait_ge(STEP["act_norm"].sem, STEP["act_norm"].at(("root", "ctx")))
            for k in range(CB):
                pe.wait_ge(dad.sem, dad.at(("lo", "ctx", k)))
                pe.wait_ge(w_lo, UCTX + k + 1)
                for tb in range(2):
                    for hf in range(2):
                        token_product(PB[2 * tb + hf][:], UCTX + k, slice(512 * hf, 512 * hf + 512), chh[:, k, chunk(tb)], chl[:, k, chunk(tb)], k == 0, k == CB - 1).then_inc(
                            lin.sem, lin.step(("bank", "ctx", 2 * tb + hf), ("used", UCTX + k)))
            for tb in range(2):
                pe.wait_ge(art.sem, art.at(("kv", tb)))
            for d in range(2):
                for h in range(RH):
                    for tb in range(2):
                        mm = pe.matmul(PB[4 + d][:, chunk(h)], KW[d][tb][:, chunk(h)], VC[tb][:, chunk(h)], start=tb == 0, stop=tb == 1)
                mm.then_inc(prt.sem, prt.step(("state", d)))
            pe.drain().then_inc(phase, 1)
            pe.wait_ge(phase, phase_done("pe"))
            sums("lat")
            pe.wait_ge(STEP["act_norm"].sem, STEP["act_norm"].at(("root", "lat")))
            wide(UIN, inh, inl, "qk", ready=(dad, ("lo", "lat")))
            for k in range(CB):
                pe.wait_ge(w_lo, UIN + 8 + k + 1)
                for tb in range(TB):
                    if k == 0:
                        pe.wait_ge(drt.sem, drt.at(("qk", tb)))
                    token_product(PB[tb][:], UIN + 8 + k, slice(0, 512), inh[:, k, chunk(tb)], inl[:, k, chunk(tb)], k == 0, k == CB - 1).then_inc(
                        lin.sem, lin.step(("bank", "v", tb)))
                for m in range(RH):
                    if k == 0:
                        pe.wait_ge(drt.sem, drt.at(("qk", 4 + m)))
                    product(PB[4 + m][:], UIN + 8 + k, slice(512 + m * P, 512 + (m + 1) * P), inh[:, k, :], inl[:, k, :], k == 0, k == CB - 1).then_inc(
                        lin.sem, lin.step(("bank", "g", m), ("used", UIN + 8 + k)))
            for j in range(4):
                pe.wait_ge(w_lo, UIN + 16 + j + 1)
                for a in range(2):
                    for g in range(4):
                        kb = 2 * j + a
                        if kb == 0:
                            pe.wait_ge(drt.sem, drt.at(("vl", g)))
                        product(PB[g][:], UIN + 16 + j, slice(a * 512 + g * P, a * 512 + (g + 1) * P), inh[:, kb, :], inl[:, kb, :], kb == 0, kb == 7).then_inc(
                            lin.sem, lin.step(("bank", "f", g), ("used", UIN + 16 + j)))
            for m in range(CB):
                pe.wait_ge(drt.sem, drt.at(("g", m) if m < 4 else ("rope", m - 4)))
                pe.matmul(PB[4 + m % 4][:], sq("rot"), QK[:, m, :], start=True, stop=True).then_inc(prt.sem, prt.step(("rot", m)))
            pe.drain().then_inc(phase, 1)
            pe.wait_ge(phase, phase_done("pe"))
            pe.wait_ge(in_t, 112)
            for g in range(4):
                for tb in range(TB):
                    if g >= 1 and tb % 2 == 0:
                        pe.wait_ge(af.sem, af.at(("ab", g - 1, tb // 2)))
                    mm = pe.matmul(PB[tb // 2][:, 256 * (tb % 2):256 * (tb % 2) + 256], FQ[:, g, chunk(tb)], DFTC[:], start=True, stop=True)
                    if tb % 2:
                        mm.then_inc(pf.sem, pf.step(("ab", g, tb // 2)))
                if g >= 2:
                    pe.wait_ge(af.sem, af.at(("hi", g - 2)))
                    pe.wait_ge(df.sem, df.at(("lo", g - 2)))
                for tb in range(TB):
                    if tb % 2 == 0:
                        pe.wait_ge(af.sem, af.at(("ab", g, tb // 2)))
                    for part in range(2):
                        mm = pe.matmul(PB[2 + g % 2][:], FAB[:, tb, part * P:(part + 1) * P], DFTL[:, part, tb, :], start=tb + part == 0, stop=tb == 3 and part == 1)
                mm.then_inc(pf.sem, pf.step(("f", g)))
            pe.drain().then_inc(phase, 1)
            pe.wait_ge(phase, phase_done("pe"))

            def ret_scores(h):
                for sb in range(TB):
                    if h >= 1:
                        pe.wait_ge(drt.sem, drt.at(("p", h - 1, sb)))
                    pe.matmul(PB[sb][:], QK[:, 4 + h, chunk(sb)], QK[:, h, :], start=True, stop=True).then_inc(prt.sem, prt.step(("s", h, sb)))

            ret_scores(0)
            for h in range(RH):
                if h + 1 < RH:
                    ret_scores(h + 1)
                if h >= 2:
                    pe.wait_ge(art.sem, art.at(("o", h - 2)))
                o = PB[4 + h % 2][:]
                for d in range(2):
                    pe.wait_ge(drt.sem, drt.at(("qx", h, d)))
                    pe.matmul(o, SFB[:, 4 * d + h, :], QX[d][:], start=d == 0, stop=False)
                for sb in range(TB):
                    pe.wait_ge(drt.sem, drt.at(("p", h, sb)))
                    mm = pe.matmul(o, VL[:, sb, chunk(h)], PSC[sb][:], start=False, stop=sb == TB - 1)
                mm.then_inc(prt.sem, prt.step(("out", h)))
                if h >= 1:
                    pe.wait_ge(art.sem, art.at(("root", h - 1)))
                pe.wait_ge(art.sem, art.at(("sq", h)))
                pe.matmul(PB[6][:], sq("ones"), TQ[0][:], start=True, stop=True).then_inc(prt.sem, prt.step(("sum", h)))
            pe.drain().then_inc(phase, 1)
            pe.wait_ge(phase, phase_done("pe"))
            wide(UOUT, inh, inl, "mx")
            sums("mx")
            sums("fp")
            pe.drain().then_inc(phase, 1)
            pe.wait_ge(phase, phase_done("pe"))

            def up_pass(s):
                for k2 in range(4):
                    pe.wait_ge(w_lo, turn(s.u0 + k2 + 1, s.loop))
                    for a in range(2):
                        for m in range(4):
                            kb, c = 2 * k2 + a, a * 512 + (m % 2) * 256 + (m // 2) * P
                            if kb == 0 and s.freed is not None:
                                pe.wait_ge(dff.sem, prior(dff, "cv", s.freed, m))
                            product(PB[4 * s.q + m][:], s.u0 + k2, slice(c, c + P), inh[:, kb, :], inl[:, kb, :], kb == 0, kb == 7).then_inc(
                                lin.sem, lin.step(("bank", s.name, s.q, m), ("used", s.u0 + k2)))

            up_passes(pe, "pe", lambda *a: None, up_pass)
            order = (4, 5, 6, 7, 0, 1, 2, 3)
            for k in range(NFB):
                if k == 0:
                    pe.wait_ge(dff.sem, dff.at(("last", ("lo", "up", 1, 1))))
                if k >= NFB - 2:
                    pe.wait_ge(dff.sem, dff.at(("lo", "up1", 0, k - NFB + 2)))
                pe.wait_ge(w_lo, UF + 44 + k + 1)
                for m in order:
                    if k == 0:
                        pe.wait_ge(dff.sem, dff.at(("last", ("cv", "up", 1, m - 4)) if m >= 4 else ("cv", "up1", 0, m)))
                    product(PB[m][:], UF + 44 + k, chunk(m), GH[:, k * T:(k + 1) * T], GL[:, k * T:(k + 1) * T], k == 0, k == NFB - 1).then_inc(
                        lin.sem, lin.step(("bank", "down", m), ("used", UF + 44 + k)))
            sums("fo")

        @block.gpsimd
        def _(pool):
            pool.drain().then_inc(phase, 1)
            pool.wait_ge(phase, phase_done("pool"))
            pool.drain().then_inc(phase, 1)
            pool.wait_ge(phase, phase_done("pool"))
            po, pc = STEP["pool_prep"], STEP["pool_score"]
            for cb in range(CB):
                p = cb % 2
                pool.wait_ge(STEP["dve_prep"].sem, STEP["dve_prep"].at(("kn", cb)))
                if cb >= 2:
                    pool.wait_ge(po.sem, po.at(("done", cb - 2)))
                pool.tensor_tensor(PREP["t2"][p][:], PREP["kn"][p][:], AA[:, cb, :], ALU.mult).then_inc(po.sem, po.step())
                k = po.n
                pool.wait_ge(STEP["act_prep"].sem, STEP["act_prep"].at(("e1", cb)))
                pool.wait_ge(STEP["dve_prep"].sem, STEP["dve_prep"].at(("rk", cb)))
                pool.tensor_tensor(RT[:, cb, :], R[:, cb, :], PREP["e1"][p][:], ALU.mult).then_inc(po.sem, po.step())
                pool.wait_ge(po.sem, k)
                pool.tensor_tensor(BT[:, cb, :], PREP["t2"][p][:], PREP["e2"][p][:], ALU.mult).then_inc(po.sem, po.step(("done", cb)))
            pool.drain().then_inc(phase, 1)
            pool.wait_ge(phase, phase_done("pool"))
            for c in range(TB):
                for half in range(2):
                    for p in range(2):
                        g = 2 * half + p
                        pool.wait_ge(STEP["dve_score"].sem, STEP["dve_score"].at(("taken", c, half, 0, p)))
                        pool.tensor_tensor(quad(LM[p][:]), quad(LL[p][:]), four("lvl0"), ALU.mult).then_inc(pc.sem, pc.step())
                        pool.tensor_tensor(quad(TI[p][:]), quad(TI[p][:]), four("ident"), ALU.add).then_inc(pc.sem, pc.step())
                        pool.wait_ge(STEP["dve_score"].sem, STEP["dve_score"].at(("taken", c, half, 1, p)))
                        pool.tensor_tensor(quad(ZI[:, g, :]), quad(ZI[:, g, :]), four("ident"), ALU.add).then_inc(pc.sem, pc.step(("lm", c, half, 0, p)))
                    for lv in range(1, LEVELS):
                        for p in range(2):
                            pool.wait_ge(STEP["pe_inv"].sem, STEP["pe_inv"].at(("q", c, half, lv - 1, p)))
                            pool.tensor_tensor(quad(LM[p][:]), quad(LL[p][:]), four(f"lvl{lv}"), ALU.mult).then_inc(pc.sem, pc.step(("lm", c, half, lv, p)))
            pool.drain().then_inc(phase, 1)
            pool.wait_ge(phase, phase_done("pool"))
            pq = STEP["pool_gn"]
            pool.wait_ge(fill, 32)
            for cb in range(CB):
                pool.wait_ge(STEP["dve_gn"].sem, STEP["dve_gn"].at(("t3", cb)))
                pool.tensor_tensor(TV[cb % 2][:], TG[cb % 2][:], G2[:, cb, :], ALU.mult).then_inc(pq.sem, pq.step(("o", cb)))
            pool.drain().then_inc(phase, 1)
            pool.wait_ge(phase, phase_done("pool"))

            def mlp(name):
                with turns(pool, "pool", name, 4, 16) as lp:
                    for m in range(CB):
                        pool.wait_ge(STEP["dve_mlp"].sem, STEP["dve_mlp"].at(("r", name, m), lp))
                        if m >= 4:
                            pool.wait_ge(STEP["dve_mlp"].sem, STEP["dve_mlp"].at(("hl", name, m - 4), lp))
                        pool.tensor_tensor(HS[m % 4][:], HR[m % 4][:], HR[m % 4][:], ALU.mult).then_inc(STEP["pool_mlp"].sem, STEP["pool_mlp"].step(("hs", name, m)))

            mlp("mlp0")
            pool.drain().then_inc(phase, 1)
            pool.wait_ge(phase, phase_done("pool"))
            pool.drain().then_inc(phase, 1)
            pool.wait_ge(phase, phase_done("pool"))
            pool.drain().then_inc(phase, 1)
            pool.wait_ge(phase, phase_done("pool"))
            mlp("mlp1")
            pool.drain().then_inc(phase, 1)
            pool.wait_ge(phase, phase_done("pool"))
            for _ in ("modulation", "context", "input", "Fourier", "retention", "residual"):
                pool.drain().then_inc(phase, 1)
                pool.wait_ge(phase, phase_done("pool"))


INPUTS = ["a_w_rkv", "a_wo", "mlp_w1", "mlp_w2", "w_kv", "b_wq", "b_wo", "a_w1", "a_w2", "a_a1", "a_a2", "a_g1", "a_g2",
          "w_ada_2", "w_in_2", "w_out_2", "w_up_2", "w_down_2", "ctx"]


def layout(x, a):
    f = lambda v: np.asarray(v)
    arr = {}
    blocks = lambda v: f(v).reshape(-1, P).T
    arr["x"] = np.ascontiguousarray(f(x)[0].T.reshape(CB, P, T).transpose(1, 0, 2))
    arr["ctx"] = np.ascontiguousarray(f(a["ctx_2"])[0].T.reshape(CB, P, CTX).transpose(1, 0, 2))
    twice = lambda v: np.tile(f(v).reshape(-1), 2)[:, None]
    down = lambda v: np.broadcast_to(f(v).reshape(1, -1), (P, f(v).size))
    parts = {
        "ln_mix0": blocks(a["ln_mix"][0]), "ln_mix1": blocks(a["ln_mix"][1]), "ln_mlp0": blocks(a["ln_mlp"][0]),
        "ln_mlp1": blocks(a["ln_mlp"][1]), "mu": blocks(a["a_mu"][0]), "w0": blocks(a["a_w0"][0]), "a0": blocks(a["a_a0"][0]),
        "k_k": blocks(a["a_k_k"][0]), "k_a": blocks(a["a_k_a"][0]), "r_k": blocks(a["a_r_k"][0]), "gn_g": blocks(a["a_gn_g"][0]),
        "gn_b": blocks(a["a_gn_b"][0]), "kv_norm": blocks(a["kv_norm"]), "k_gain": twice(a["k_gain"]), "q_gain": twice(a["b_q_gain"][0]),
        "sinks": down(a["b_sinks"][0]), "c": blocks(a["c_2"][0]), "c_ctx": blocks(a["c_ctx_2"]), "b_ada": blocks(a["b_ada_2"][0]),
        "g_mix_pre": blocks(a["g_mix_pre_2"][0]), "g_mix_post": blocks(a["g_mix_post_2"][0]), "g_ffn_pre": blocks(a["g_ffn_pre_2"][0]),
        "g_ffn_post": blocks(a["g_ffn_post_2"][0]),
        "decay": np.concatenate([down(a["ret_decay_fwd_2"][0]), down(a["ret_decay_bwd_2"][0])], 1),
        "conv_w": blocks(a["conv_w_2"][0]), "conv_b": blocks(a["conv_b_2"][0]),
    }
    arr["vec"] = np.ascontiguousarray(np.concatenate([parts[n] for n in COLS], 1))
    assert arr["vec"].shape == (P, N_COLS)
    arr["a_w_rkv"] = f(a["a_w_rkv"])[0]
    for n in ("a_wo", "b_wq", "b_wo", "a_w1", "a_w2", "a_a1", "a_a2", "a_g1", "a_g2", "w_ada_2", "w_in_2", "w_out_2", "w_up_2", "w_down_2"):
        arr[n] = f(a[n])[0]
    up = arr["w_up_2"].reshape(CB // 2, 2, P, 2, NFB // 2, 256)
    arr["w_up_2"] = up.transpose(4, 0, 2, 1, 3, 5).reshape(-1, 1024)
    for n in ("mlp_w1", "mlp_w2", "w_kv"):
        arr[n] = f(a[n])
    arr.update(constants())
    return {n: np.ascontiguousarray(v) for n, v in arr.items()}


def declare(nc, arr):
    t = {n: nc.dram_tensor(f"in_{n}", v.shape, mybir.dt.from_np(v.dtype), kind="ExternalInput").ap() for n, v in arr.items()}
    out = nc.dram_tensor("out_0", (P, CB, T), F32, kind="ExternalOutput").ap()
    return t, out


def kernel(x, **a):
    import concourse.bacc as bacc
    from concourse.bass_utils import run_bass_kernel_spmd

    arr = layout(x, a)
    book = {}
    for _ in range(2):
        nc = bacc.Bacc("TRN2", target_bir_lowering=False, num_devices=1)
        t, out = declare(nc, arr)
        program(nc, t, out, book)
        book["built"] = True
    r = run_bass_kernel_spmd(nc, [{f"in_{n}": v for n, v in arr.items()}], core_ids=[0])
    y = r.results[0]["out_0"]
    return np.ascontiguousarray(y.transpose(1, 0, 2).reshape(C, T).T)[None]
```

```python
import math
from contextlib import ExitStack, contextmanager

import numpy as np
import concourse.bass as bass
from concourse import mybir

F32 = mybir.dt.float32
F32R = mybir.dt.float32r
ALU = mybir.AluOpType
ACT = mybir.ActivationFunctionType
AX = mybir.AxisListType

P = 128
C = 1024
CB = C // P
T = 512
TB = T // P
HEADS = 16
HD = 64
FF = 4 * C
DFF = 2816
NFB = DFF // P
CTX = 256
RH = 4
LORA_W, LORA_A, LORA_G = 64, 64, 160
LAM = math.exp(-0.5)
RMS_EPS = 1e-6
GN_EPS = 64e-5
GRID = 64
LEVELS = 6

COLS = {}


def _columns():
    at = 0
    for name, n in (
        ("ln_mix0", 8), ("ln_mix1", 8), ("ln_mlp0", 8), ("ln_mlp1", 8), ("mu", 48), ("w0", 8), ("a0", 8),
        ("k_k", 8), ("k_a", 8), ("r_k", 8), ("gn_g", 8), ("gn_b", 8), ("kv_norm", 8), ("k_gain", 1),
        ("q_gain", 1), ("sinks", 16), ("c", 8), ("c_ctx", 8), ("b_ada", 48), ("g_mix_pre", 8),
        ("g_mix_post", 8), ("g_ffn_pre", 8), ("g_ffn_post", 8), ("decay", 8), ("conv_w", 132),
        ("conv_b", 44),
    ):
        COLS[name] = at
        at += n
    return at


N_COLS = _columns()

SQUARES = ["ident", "ones", "blk", "blk64", "upper", "upper_in", "lower", "rot", "m0", "m0t"] + [
    f"lvl{i}" for i in range(LEVELS)]
SQ_AT = {n: i for i, n in enumerate(SQUARES)}
N_SQ = len(SQUARES)


def constants():
    i = np.arange(P)
    t, s = i[:, None], i[None, :]
    sq = {
        "ident": t == s, "ones": np.ones((P, P)), "blk": t // 64 == s // 64,
        "blk64": (t // 64 == s // 64) / 64.0,
        "upper": t < s, "upper_in": t <= s, "lower": t > s,
        "m0": (t // 2 == s // 2) & (t > s), "m0t": (t // 2 == s // 2) & (t < s),
        "rot": (t == s - 64) * 1.0 - (t == s + 64) * 1.0,
    }
    for n in range(LEVELS):
        b = 2 << n
        sq[f"lvl{n}"] = (t // (2 * b) == s // (2 * b)) & (t // b != s // b) & (t > s)
    squares = np.concatenate([np.asarray(sq[n], np.float32) for n in SQUARES], 1)
    sel = np.zeros((P, CB, HEADS), np.float32)
    for cb in range(CB):
        sel[i, cb, 2 * cb + i // 64] = 1.0
    selt = np.zeros((P, CB * P), np.float32)
    selt[:HEADS] = sel.transpose(2, 1, 0).reshape(HEADS, CB * P)
    d = t + P - np.arange(2 * P)[None, :]
    band = np.where((d >= 0) & (d < P), d, 1e32)
    first = np.where(np.arange(2 * P)[None, :] < P, 1e32, band)
    band = np.stack([first, band, band], 1)
    e = np.arange(896)[None, :] - 384 - i[:, None]
    after = np.maximum(e, 0).astype(np.float32)
    before = np.maximum(-e, 0).astype(np.float32)
    pos = np.arange(T, dtype=np.float64)
    n_freq = P // 4
    freqs = 10000.0 ** (-np.arange(n_freq, dtype=np.float32) / n_freq)
    ang = np.concatenate([(pos // GRID)[:, None] * freqs, (pos % GRID)[:, None] * freqs], 1)
    cos = np.tile(np.cos(ang).T, (2, 1)).astype(np.float32)
    sin = np.tile(np.sin(ang).T, (2, 1)).astype(np.float32)
    ramp = np.stack([np.broadcast_to(pos + 1, (P, T)), np.broadcast_to(T - pos, (P, T))], 1)
    cpos = np.stack([CTX - 1 - (i[:, None] + P * np.arange(2)[None, :]), i[:, None] + P * np.arange(2)[None, :]], 2)
    kd = 2 * np.pi * np.outer(i, i) / P
    dft_c = np.concatenate([np.cos(kd), np.sin(kd)], 1) / math.sqrt(P)
    kl = 2 * np.pi * (np.outer(pos, pos) % T) / T
    dl = np.stack([np.cos(kl), -np.sin(kl)]) / math.sqrt(T)
    dft_l = dl.reshape(2, TB, P, T).transpose(2, 0, 1, 3)
    f = lambda a: np.ascontiguousarray(a, np.float32)
    return {
        "k_sq": f(squares), "k_sel": f(sel.reshape(P, CB * HEADS)), "k_selt": f(selt), "k_band": f(band),
        "k_after": f(after), "k_before": f(before), "k_cos": f(cos), "k_sin": f(sin), "k_ramp": f(ramp),
        "k_cpos": f(cpos.reshape(P, 4)), "k_dftc": f(dft_c), "k_dftl": f(dft_l),
    }


class Steps:

    def __init__(self, sem, name, book):
        self.sem, self.name, self.book, self.n = sem, name, book, 0
        self.first, self.marks = 0, None

    def step(self, *marks):
        self.n += 1
        for m in marks:
            self.book[self.name, m] = self.n
            if self.marks is not None:
                self.marks.append(m)
        return 1

    def at(self, what, loop=None, ago=0):
        v = what if isinstance(what, int) else self.book[self.name, what] if "built" in self.book else self.book.get((self.name, what), 1)
        if loop is None:
            return v
        per = self.book.get((self.name, "per turn", loop.name), 1)
        return loop.i * per + (v - ago * per if (self.name, what) in self.book or isinstance(what, int) else 1)

    def begin(self):
        self.first, self.marks = self.n, []

    def end(self, name, turns, units):
        per = self.n - self.first
        self.book[self.name, "per turn", name] = per
        for m in self.marks:
            last = self.book[self.name, m] + per * (turns - 1)
            self.book[self.name, ("last", m)] = last
            if m[0] == "used":
                self.book[self.name, ("used", m[1] + units * (turns - 1))] = last
        self.n += per * (turns - 1)
        self.marks = None


class Loop:
    def __init__(self, name, i, units):
        self.name, self.i, self.units = name, i, units


def program(nc, t, out, book):
    ctx = ExitStack()
    with ctx:
        KB = 1024
        base = 16640

        def at(name, kb, shape, dt=F32):
            return nc.alloc_sbuf_tensor_at(name, [P] + list(shape), dt, offset=base + int(kb * KB))

        slab = ctx.enter_context(nc.sbuf_tensor("slab", [P, (229368 - base) // 4 - 8], F32))

        vec = at("vec", 0, [N_COLS])
        sqs = at("sqs", 2, [N_SQ * P])
        sel = at("sel", 10, [CB, HEADS])
        selt = at("selt", 10.5, [CB * P])
        adac = at("adac", 14.5, [48, 2])
        small = at("small", 14.875, [96])
        SLOTS = 4
        raw = [at(f"raw{s}", 16 + 4 * s, [1024]) for s in range(SLOTS)]
        whi = [at(f"whi{s}", 32 + 4 * s, [1024], F32R) for s in range(SLOTS)]
        wlo = [at(f"wlo{s}", 48 + 4 * s, [1024], F32R) for s in range(SLOTS)]
        A0 = 64

        def sq(name):
            return sqs[:, SQ_AT[name] * P:(SQ_AT[name] + 1) * P]

        def col(name, j=0):
            return vec[:, COLS[name] + j:COLS[name] + j + 1]

        PB = [ctx.enter_context(nc.psum_tensor(f"bank{i}", [P, 512], F32)) for i in range(8)]

        def sem(name):
            return ctx.enter_context(nc.semaphore(name))

        STEP = {}
        for owner, names in (
            ("pe", "pe_lin pe_norm pe_lora pe_prep pe_score pe_inv pe_tok pe_rec pe_gn pe_kv pe_att pe_ada pe_ret pe_four"),
            ("act", "act_bd act_norm act_mix act_lora act_prep act_inv act_tok act_rec act_gn act_mlp act_kv act_att act_ada act_ret act_four act_ffn"),
            ("dve", "dve_norm dve_mix dve_lora dve_prep dve_score dve_inv dve_rec dve_gn dve_mlp dve_kv dve_att dve_mod dve_ada dve_ret dve_four dve_ffn"),
            ("pool", "pool_prep pool_score pool_mlp pool_gn pool_ret"),
        ):
            for n in names.split():
                s = Steps(sem(n), n, book)
                s.owner = owner
                STEP[n] = s

        @contextmanager
        def turns(eng, owner, name, n, units):
            mine = [s for s in STEP.values() if s.owner == owner]
            for s in mine:
                s.begin()
            with eng.Fori(0, n) as i:
                yield Loop(name, i, units)
            for s in mine:
                s.end(name, n, units)

        w_raw = [sem(f"w_raw{s}") for s in range(SLOTS)]
        w_hi, w_lo = sem("w_hi"), sem("w_lo")
        phase = sem("phase")
        in_c, in_k, in_v = sem("in_c"), sem("in_k"), sem("in_v")
        in_x = [sem(f"in_x{q}") for q in range(4)]
        spill, fill = sem("spill"), sem("fill")
        stored = sem("stored")
        phases = {"pe": 0, "act": 0, "dve": 0, "pool": 0, "sp": 0}

        def phase_done(who):
            phases[who] += 1
            return 4 * phases[who]

        def turn(v, loop):
            return v if loop is None else loop.i * loop.units + v

        lin, x_sum = STEP["pe_lin"], STEP["dve_mlp"]

        def used(u, loop):
            if loop is not None and u < loop.first:
                return lin.at(("used", u + loop.units), loop, ago=1)
            return lin.at(("used", u), loop)

        def x_done(stage, m):
            key = ("x", stage, m)
            return x_sum.at(("last", key) if ("dve_mlp", ("last", key)) in book else key)

        kdup, in_a, in_t = sem("kdup"), sem("in_a"), sem("in_t")
        in_mod = [sem(f"in_mod{i}") for i in range(4)]

        UR, UWO, UM0 = 0, 24, 32
        UKV = UM0 + 64
        UQ = UKV + 4
        UBO = UQ + 8
        UM1 = UBO + 8
        UCTX = UM1 + 64
        UIN = UCTX + 8
        UOUT = UIN + 20
        UF = UOUT + 8
        UEND = UF + 66

        lambda8 = lambda n, kb, dt=F32: at(n, kb, [CB, T], dt)
        XT = lambda8("XT", 64)
        H = lambda8("H", 80)
        XX = lambda8("XX", 96)
        R, K_, V = lambda8("R", 112), lambda8("K", 128), lambda8("V", 144)
        SIG, AA = lambda8("SIG", 160), lambda8("AA", 176)
        NR = 3
        xmh = [at(f"xmh{i}", 192 + 2 * i, [T], F32R) for i in range(NR)]
        xml = [at(f"xml{i}", 192 + 6 + 2 * i, [T], F32R) for i in range(NR)]
        SQT = [at(f"sqt{i}", 192 + 2 * i, [T]) for i in range(2)]
        RS = at("RS", 204, [T])
        xt4 = [at(f"xt4_{i}", 64 + 2 * i, [T]) for i in range(4)]
        lw1 = at("lw1", 112, [CB, LORA_W])
        la1 = at("la1", 114, [CB, LORA_A])
        lg1 = at("lg1", 116, [CB, LORA_G])
        lw2 = at("lw2", 121, [C])
        la2 = at("la2", 125, [C])
        lg2a = at("lg2a", 129, [C])
        lg2b = at("lg2b", 133, [C])
        xl = [at(f"xl{i}", 137 + 2 * i, [T]) for i in range(4)]
        hid1 = [at(f"hid1_{i}", 145 + 2 * i, [T]) for i in range(2)]

        RT, KT, AT, BT = R, K_, SIG, AA
        PREP = {n: [at(f"prep_{n}{p}", 64 + 4 * j + 2 * p, [T]) for p in range(2)]
                for j, n in enumerate(("cs", "csn", "csx", "e1", "e2", "e3", "t1", "km", "rk", "kn", "t2"))}
        KNI, RKS = at("KNI", 108, [T]), at("RKS", 110, [T])
        VT = at("VT", 16, [CB, 3, HD])
        BD = [[at(f"BD{n}{i}", 24 + 12 * i + 4 * j, [4, 2, P]) for j, n in enumerate("ABR")] for i in range(2)]
        ZI, MT, GBm, GKm = (at(n, 68 + 8 * j, [4, 4 * P]) for j, n in enumerate(("ZI", "MT", "GB", "GK")))
        SS = at("SS", 100, [CB, P])
        WB = [at(f"WB{p}", 22 + 0.75 * p, [3, HD]) for p in range(2)]
        _, UB, TS, SM = ([at(f"{n}{p}", 104 + j + 0.5 * p, [P]) for p in range(2)] for j, n in enumerate(("W_", "UB", "TS", "SM")))
        SM += [at(f"SM{i}", 205 + 0.5 * i, [P]) for i in (2, 3)]
        LL = [at(f"LL{p}", 192 + 8 * p, [4 * P]) for p in range(2)]
        LM = [at(f"LM{p}", 194 + 8 * p, [4 * P]) for p in range(2)]
        QS = [at(f"QS{p}", 196 + 8 * p, [4 * P]) for p in range(2)]
        TI = [at("TI0", 198, [4 * P]), at("TI1", 108, [4 * P])]
        DMID = small[:, 2:2 + 32]
        DEND = small[:, 34:34 + 32]
        inh, inl = lambda8("inh", 64, F32R), lambda8("inl", 80, F32R)
        TG = [at(f"TG{p}", 96 + 2 * p, [T]) for p in range(2)]
        TV = [at(f"TV{p}", 100 + 2 * p, [T]) for p in range(2)]
        G2, X = lambda8("G2", 160), lambda8("X", 176)

        hidh, hidl = lambda8("hidh", 96, F32R), lambda8("hidl", 112, F32R)
        HR = [at(f"HR{i}", 128 + 2 * i, [T]) for i in range(4)]
        HS = [at(f"HS{i}", 136 + 2 * i, [T]) for i in range(4)]
        KF, VF, KN, RKN = (at(n, 128 + 2 * j, [T]) for j, n in enumerate(("KF", "VF", "KN", "RKN")))
        KD = [[at(f"KD{j}{par}", 166 + 4 * j + 2 * par, [T]) for par in range(2)] for j in range(2)]
        VK = at("VK", 200, [TB, P])
        QNI = at("QNI", 202, [T])
        QF = lambda8("QF", 144)
        BAND = at("BAND", 160, [3, 2 * P])
        S1 = [at(f"S1_{i}", 128 + 2 * i, [T]) for i in range(3)]
        PTR = [at(f"PTR{i}", 134 + 2 * i, [T]) for i in range(3)]

        AC = 6 * C // 4
        ADW = [at(f"ADW{i}", 144 + 6 * i, [AC]) for i in range(4)]
        AX_ = 2 * C // 4
        ADS = [at("ADS0", 168, [AC]), at("ADS1", 196, [AX_])]
        LG = at("LG", 15.4375, [8])
        WC = at("WC", 15.5, [2, 2, RH])
        CPOS = at("CPOS", 15.5625, [4])
        LT = [at(f"LT{i}", 15.625 + 0.0625 * i, [16]) for i in range(5)]
        GA, GAC, GP, GF, GFP = (small[:, 2 + 8 * i:10 + 8 * i] for i in range(5))
        CX = at("CX", 144, [CB, CTX])
        chh, chl = at("chh", 128, [CB, CTX], F32R), at("chl", 136, [CB, CTX], F32R)
        CT = [at(f"CT{i}", 152 + i, [CTX]) for i in range(2)]
        KW = [[at(f"KW{d}{tb}", 96 + 4 * d + 2 * tb, [T]) for tb in range(2)] for d in range(2)]
        VC = [at(f"VC{tb}", 104 + 2 * tb, [T]) for tb in range(2)]
        SFB = at("SFB", 196, [8, P])
        QK = lambda8("QK", 96)
        VL = at("VL", 112, [TB, 512])
        GS = at("GS", 120, [RH, T])
        FQ = at("FQ", 128, [RH, T])
        COS, SIN = at("COS", 136, [T]), at("SIN", 138, [T])
        RAMP = at("RAMP", 140, [2, T])
        AFT, BEF = at("AFT", 144, [896]), at("BEF", 147.5, [896])
        DM = [at(f"DM{i}", 151 + 3.5 * i, [896]) for i in range(2)]
        DFTC = at("DFTC", 158, [256])
        DFTL = at("DFTL", 160, [2, TB, T])
        FAB = at("FAB", 192, [TB, 256])
        PSC = [at(f"PSC{i}", 160 + 2 * i, [T]) for i in range(4)]
        RET = [at(f"RET{i}", 168 + 2 * i, [T]) for i in range(2)]
        RR = at("RR", 172, [T])
        HE = [at("HE0", 174, [T]), at("HE1", 204, [T])]
        QX = [at(f"QX{d}", 192 + 2 * d, [T]) for d in range(2)]
        TQ = [at(f"TQ{i}", 200 + 2 * i, [T]) for i in range(2)]
        MX = lambda8("MX", 96)
        GH, GL = at("GH", 96, [NFB * T], F32R), at("GL", 140, [NFB * T], F32R)
        CV = [at(f"CV{i}", 184 + 2 * i, [T]) for i in range(4)]
        SG = [at(f"SG{i}", 192 + 2 * i, [T]) for i in range(2)]
        HT = [at(f"HT{i}", 196 + 2 * i, [T]) for i in range(2)]
        CWT = [at(f"CWT{i}", 200 + 0.125 * i, [4, 2, 2]) for i in range(2)]
        FO, X2 = lambda8("FO", 64), lambda8("X2", 80)

        class Pass:

            def __init__(self, g, q, name, loop, before, freed):
                self.q, self.name, self.loop, self.before, self.freed = q, name, loop, before, freed
                self.u0 = UF + 4 * g
                self.at = [slice((2 * g + j) * T, (2 * g + j + 1) * T) if loop is None else bass.ds(loop.i * (4 * T) + (2 * g + j) * T, T) for j in range(2)]
                self.blocks = slice(2 * g, 2 * g + 2) if loop is None else bass.ds(loop.i * 4 + 2 * g, 2)

        def prior(steps, what, which, j):
            name, q, loop, ago = which
            key = (what, name, q, j)
            return steps.at(("last", key) if ago == "last" else key, loop, 0 if ago == "last" else ago)

        def up_passes(eng, owner, stream, work):
            stream(UF, 4)
            work(Pass(0, 0, "up0", None, None, None))
            stream(UF + 4, 4)
            work(Pass(1, 1, "up0", None, ("up0", 0, None, 0), None))
            with turns(eng, owner, "up", 4, 8) as lp:
                lp.first = UF + 8
                stream(UF + 8, 4, lp)
                work(Pass(2, 0, "up", lp, ("up", 1, lp, 1), ("up", 0, lp, 1)))
                stream(UF + 12, 4, lp)
                work(Pass(3, 1, "up", lp, ("up", 0, lp, 0), ("up", 1, lp, 1)))
            stream(UF + 40, 4)
            work(Pass(10, 0, "up1", None, ("up", 1, None, "last"), ("up", 0, None, "last")))

        def SM_at(c, cb):
            return SM[cb % 4][:]

        def four(name):
            return sq(name).unsqueeze(1).to_broadcast([P, 4, P])

        def quad(ap):
            return ap.rearrange("p (a b) -> p a b", a=4)

        def chunk(c):
            return slice(c * P, (c + 1) * P)

        xsp = nc.dram_tensor("x_spill", (P, CB * T), F32).ap()
        gsp = nc.dram_tensor("g_spill", (P, CB * T), F32).ap()

        block = ctx.enter_context(nc.Block())

        w_rkv = t["a_w_rkv"]

        @block.sync
        def _(sp):
            def load(u, src, dst=None, loop=None):
                if u >= SLOTS:
                    sp.wait_ge(w_lo, turn(u - SLOTS + 1, loop))
                sp.dma_start(raw[u % SLOTS][:, :] if dst is None else dst(raw[u % SLOTS]), src).then_inc(w_raw[u % SLOTS], 16)


            for q in range(4):
                sp.dma_start(XT[:, 2 * q:2 * q + 2, :], t["x"][:, 2 * q:2 * q + 2, :]).then_inc(in_x[q], 16)
                if q == 0:
                    sp.dma_start(sqs[:], t["k_sq"]).then_inc(in_k, 16)
                if q == 1:
                    sp.dma_start(vec[:], t["vec"]).then_inc(in_v, 16)
            sp.dma_start(sel[:], t["k_sel"].rearrange("p (a b) -> p a b", a=CB)).then_inc(in_c, 16)
            sp.dma_start(selt[:], t["k_selt"]).then_inc(in_c, 16)
            for dst, name in ((lg1, "a_g1"), (lw1, "a_w1"), (la1, "a_a1")):
                sp.dma_start(dst[:], t[name].rearrange("(a p) n -> p a n", p=P)).then_inc(in_c, 16)
            sp.dma_start(lg2a[:], t["a_g2"][0:P, :]).then_inc(in_c, 16)
            sp.dma_start(lg2b[0:LORA_G - P, :], t["a_g2"][P:LORA_G, :]).then_inc(in_c, 16)
            sp.dma_start(lw2[0:LORA_W, :], t["a_w2"]).then_inc(in_c, 16)
            sp.dma_start(la2[0:LORA_A, :], t["a_a2"]).then_inc(in_c, 16)
            rows = lambda w, k, n0=0: w[k * P:(k + 1) * P, n0:n0 + 1024]
            for u in range(4):
                load(u, rows(w_rkv[0], u))
            sp.wait_ge(STEP["dve_norm"].sem, STEP["dve_norm"].at("h0"))
            sp.dma_start(xsp, XT[:]).then_inc(spill, 16)
            sp.wait_ge(STEP["act_lora"].sem, STEP["act_lora"].at(("out", "g", CB - 1)))
            sp.dma_start(gsp, XT[:]).then_inc(spill, 16)
            for u in range(4, 24):
                load(u, rows(w_rkv[u // 8], u % 8))
            sp.wait_ge(phase, 4 * 4)
            for u in range(4):
                load(UWO + u, rows(t["a_wo"], u))
            sp.wait_ge(STEP["pe_rec"].sem, STEP["pe_rec"].at(("sy", TB - 1, CB - 1)))
            sp.dma_start(G2[:], gsp.rearrange("p (a b) -> p a b", a=CB)).then_inc(fill, 16)
            sp.dma_start(X[:], xsp.rearrange("p (a b) -> p a b", a=CB)).then_inc(fill, 16)
            for u in range(4, 8):
                load(UWO + u, rows(t["a_wo"], u))

            def load_modulation(k, lp):
                dmo = STEP["dve_mod"]
                if k >= 4:
                    sp.wait_ge(dmo.sem, dmo.at(("sum", k - 4), lp))
                else:
                    sp.wait_ge(dmo.sem, dmo.at(("sum", k + 4), lp, ago=1))
                sp.dma_start(ADW[k % 4][:], t["w_ada_2"][k * P:(k + 1) * P, bass.ds(lp.i * AC, AC)]).then_inc(in_mod[k % 4], 16)

            def load_mlp(layer, u0, name):
                with turns(sp, "sp", name, 4, 16) as lp:
                    lp.first = u0
                    for j in range(8):
                        load(u0 + j, t["mlp_w1"][layer, j * P:(j + 1) * P, bass.ds(lp.i * 1024, 1024)], loop=lp)
                        if layer == 1 and j >= 2:
                            load_modulation(j - 2, lp)
                    for j in range(8):
                        if layer == 1 and j < 2:
                            load_modulation(6 + j, lp)
                        load(u0 + 8 + j, t["mlp_w2"][layer, bass.ds(lp.i * 1024 + j * P, P), :], loop=lp)

            load_mlp(0, UM0, "mlp0")
            for j in range(4):
                load(UKV + j, t["w_kv"][2 * j * P:(2 * j + 2) * P, :].rearrange("(a p) n -> p a n", p=P),
                     dst=lambda r: r[:, 0:512].rearrange("p (a n) -> p a n", a=2))
            sp.dma_start(CPOS[:], t["k_cpos"]).then_inc(in_a, 16)
            sp.dma_start(BAND[:], t["k_band"]).then_inc(in_c, 16)
            for j in range(8):
                load(UQ + j, rows(t["b_wq"], j))
            for j in range(8):
                load(UBO + j, rows(t["b_wo"], j))
            load_mlp(1, UM1, "mlp1")
            for j in range(4):
                load(UCTX + j, rows(t["w_in_2"], j, 512))
            dmo = STEP["dve_mod"]
            sp.wait_ge(dmo.sem, dmo.at("mod"))
            sp.dma_start(CX[:], t["ctx"]).then_inc(in_a, 16)
            for j in range(4, 8):
                load(UCTX + j, rows(t["w_in_2"], j, 512))
            for j in range(6):
                load(UIN + j, rows(t["w_in_2"], j))
            sp.wait_ge(phase, 4 * 10)
            for dst, name in ((COS[:], "k_cos"), (SIN[:], "k_sin"), (RAMP[:], "k_ramp"), (AFT[:], "k_after"), (BEF[:], "k_before"),
                              (DFTC[:], "k_dftc"), (DFTL[:], "k_dftl")):
                sp.dma_start(dst, t[name]).then_inc(in_t, 16)
            for j in range(6, 16):
                load(UIN + j, rows(t["w_in_2"], j % 8, 1024 * (j // 8)))
            for j in range(4):
                load(UIN + 16 + j, t["w_in_2"][2 * j * P:(2 * j + 2) * P, 2048:2560].rearrange("(a p) n -> p a n", p=P),
                     dst=lambda r: r[:].rearrange("p (a n) -> p a n", a=2))
            for j in range(8):
                load(UOUT + j, rows(t["w_out_2"], j))
            for j in range(8):
                load(UF + j, t["w_up_2"][j * P:(j + 1) * P, :])
            with turns(sp, "sp", "up", 4, 8) as lp:
                for j in range(8):
                    load(UF + 8 + j, t["w_up_2"][bass.ds(lp.i * 1024 + (8 + j) * P, P), :], loop=lp)
            for j in range(40, 44):
                load(UF + j, t["w_up_2"][j * P:(j + 1) * P, :])
            for j in range(NFB):
                load(UF + 44 + j, rows(t["w_down_2"], j))
            for m in range(CB):
                sp.wait_ge(STEP["dve_ffn"].sem, STEP["dve_ffn"].at(("out", m)))
                sp.dma_start(out[:, m, :], X2[:, m, :]).then_inc(stored, 16)
            sp.wait_ge(stored, 16 * CB)

        @block.scalar
        def _(act):
            an, am, al = STEP["act_norm"], STEP["act_mix"], STEP["act_lora"]
            pn, pl = STEP["pe_norm"], STEP["pe_lora"]

            def split_hi(u, loop=None):
                act.wait_ge(w_raw[u % SLOTS], 16 * (u // SLOTS + 1) if loop is None else loop.i * (4 * loop.units) + 16 * (u // SLOTS + 1))
                if u >= SLOTS:
                    act.wait_ge(lin.sem, used(u - SLOTS, loop))
                act.activation(whi[u % SLOTS][:, :], raw[u % SLOTS][:, :], ACT.Copy).then_inc(w_hi, 1)

            def norm_stats(name, xb, n=T, ready=None):
                for kb in range(CB):
                    if ready is not None:
                        ready(kb)
                    if kb >= 2:
                        act.wait_ge(pn.sem, pn.at(("sum", name, kb - 2)))
                    act.activation(SQT[kb % 2][:, :n], xb(kb), ACT.Square).then_inc(an.sem, an.step(("sq", name, kb)))
                act.wait_ge(pn.sem, pn.at(("sum", name, CB - 1)))
                act.activation(RS[:, :n], PB[0][:, :n], ACT.Sqrt, scale=1.0 / C, bias=small[:, 0:1]).then_inc(an.sem, an.step(("root", name)))

            act.wait_ge(STEP["dve_norm"].sem, STEP["dve_norm"].at("eps"))
            norm_stats("n0", lambda kb: XT[:, kb, :], ready=lambda kb: act.wait_ge(in_x[kb // 2], 16))

            act.wait_ge(spill, 16)
            q = 0
            for j, (name, width) in enumerate((("g", LORA_G), ("w", LORA_W), ("a", LORA_A))):
                act.wait_ge(pl.sem, pl.at(("hid", name)))
                fn = {"g": ACT.Sigmoid, "w": ACT.Tanh, "a": ACT.Copy}[name]
                if j > 0:
                    act.wait_ge(pl.sem, pl.at(("outs", "gwa"[j - 1])))
                act.activation(hid1[0][0:min(width, P), :], PB[0][0:min(width, P), :], fn).then_inc(al.sem, al.step(("hid", name, 0)))
                if width > P:
                    act.activation(hid1[1][0:width - P, :], PB[1][0:width - P, :], fn).then_inc(al.sem, al.step(("hid", name, 1)))
                for m in range(CB):
                    act.wait_ge(pl.sem, pl.at(("out", name, m)))
                    b = PB[2 + q % 6]
                    if name == "g":
                        act.activation(XT[:, m, :], b[:], ACT.Copy).then_inc(al.sem, al.step(("out", name, m)))
                    elif name == "w":
                        act.activation(SIG[:, m, :], b[:], ACT.Sigmoid, bias=col("w0", m)).then_inc(al.sem, al.step(("out", name, m)))
                    else:
                        act.activation(AA[:, m, :], b[:], ACT.Sigmoid, bias=col("a0", m)).then_inc(al.sem, al.step(("out", name, m)))
                    q += 1
            for u in range(3):
                split_hi(u)
            act.drain().then_inc(phase, 1)
            act.wait_ge(phase, phase_done("act"))
            act.wait_ge(spill, 32)

            def mix_hi(u):
                act.wait_ge(STEP["dve_mix"].sem, STEP["dve_mix"].at(("mix", u)))
                if u >= NR:
                    act.wait_ge(lin.sem, lin.at(("used", u - NR)))
                act.activation(xmh[u % NR][:], xt4[u % 4][:], ACT.Copy).then_inc(am.sem, am.step(("hi", u)))

            for u in range(2):
                mix_hi(u)
            for u in range(24):
                if u + 3 < 24:
                    split_hi(u + 3)
                if u + 2 < 24:
                    mix_hi(u + 2)
            act.drain().then_inc(phase, 1)
            act.wait_ge(phase, phase_done("act"))

            ap_, ai, at_, ar, ag = (STEP["act_" + n] for n in ("prep", "inv", "tok", "rec", "gn"))
            pp, pr = STEP["pe_prep"], STEP["pe_rec"]
            dp = STEP["dve_prep"]
            for cb in range(CB):
                if cb >= 2:
                    act.wait_ge(pp.sem, pp.at(("ksum", cb - 2)))
                act.activation(PREP["e1"][cb % 2][:], K_[:, cb, :], ACT.Square, scale=col("k_k", cb)).then_inc(ap_.sem, ap_.step(("ksq", cb)))
            act.wait_ge(pp.sem, pp.at(("ksum", CB - 1)))
            act.wait_ge(dp.sem, dp.at("knz"))
            act.activation(KNI[0:HEADS, :], PB[0][0:HEADS, :], ACT.Sqrt).then_inc(ap_.sem, ap_.step("kroot"))
            for cb in range(CB):
                p = cb % 2
                if cb >= 2:
                    act.wait_ge(dp.sem, dp.at(("at", cb - 2)))
                    act.wait_ge(STEP["pool_prep"].sem, STEP["pool_prep"].at(("done", cb - 2)))
                act.wait_ge(dp.sem, dp.at(("csn", cb)))
                act.activation(PREP["e2"][p][:], PREP["csn"][p][:], ACT.Exp, scale=LAM).then_inc(ap_.sem, ap_.step(("e2", cb)))
                act.activation(PREP["e1"][p][:], PREP["csn"][p][:], ACT.Exp, scale=-LAM).then_inc(ap_.sem, ap_.step(("e1", cb)))
                act.wait_ge(dp.sem, dp.at(("csx", cb)))
                act.activation(PREP["e3"][p][:], PREP["csx"][p][:], ACT.Exp, scale=-LAM).then_inc(ap_.sem, ap_.step(("e3", cb)))
                act.activation(DMID[:, 4 * cb:4 * cb + 4].unsqueeze(2), quad(PREP["cs"][p][:])[:, :, 63:64], ACT.Exp, scale=-LAM).then_inc(ap_.sem, ap_.step())
                act.activation(DEND[:, 4 * cb:4 * cb + 4].unsqueeze(2), quad(PREP["csn"][p][:])[:, :, 127:128], ACT.Exp, scale=-LAM).then_inc(ap_.sem, ap_.step(("exps", cb)))
            act.drain().then_inc(phase, 1)
            act.wait_ge(phase, phase_done("act"))

            def inverse_copies(c, half):
                for lv in range(LEVELS):
                    for p in range(2):
                        if lv > 0:
                            act.wait_ge(STEP["pe_inv"].sem, STEP["pe_inv"].at(("tz", c, half, lv - 1, p)))
                        act.wait_ge(STEP["pe_inv"].sem, STEP["pe_inv"].at(("q", c, half, lv, p)))
                        act.activation(QS[p][:], PB[2 + p][:], ACT.Copy).then_inc(ai.sem, ai.step(("q", c, half, lv, p)))

            ab = STEP["act_bd"]

            def heads_apart(c, half):
                for r, src in ((1, BT), (0, AT), (2, RT)):
                    for h in range(2):
                        hs = slice(64 * h, 64 * h + 64)
                        act.activation(BD[half][r][hs, :, h, :], src[hs, 4 * half:4 * half + 4, chunk(c)], ACT.Copy).then_inc(ab.sem, ab.step((c, half, r)))

            for half in range(2):
                act.wait_ge(STEP["pool_score"].sem, STEP["pool_score"].at(("bd", half)))
                heads_apart(0, half)
            act.wait_ge(STEP["pool_score"].sem, STEP["pool_score"].at("gaps"))
            for c in range(TB):
                for half in range(2):
                    inverse_copies(c, half)
                    if c + 1 < TB:
                        act.wait_ge(STEP["pe_score"].sem, STEP["pe_score"].at((c, half, 4, 1)))
                        heads_apart(c + 1, half)
                if c > 0:
                    act.wait_ge(pr.sem, pr.at(("sy", c - 1, CB - 1)))
                for j, which in enumerate("vkb"):
                    for half in range(2):
                        act.wait_ge(STEP["pe_tok"].sem, STEP["pe_tok"].at(("tr", c, which, half)))
                        b = PB[half]
                        if which == "v":
                            dst = VT[:, 4 * half:4 * half + 4, 0:3:2, :]
                        else:
                            dst = (KT if which == "k" else BT)[:, 4 * half:4 * half + 4, chunk(c)]
                        src = b[:].rearrange("p (a c d) -> p a c d", a=4, c=2) if which == "v" else quad(b[:])
                        act.activation(dst, src, ACT.Copy).then_inc(at_.sem, at_.step(("tr", c, which, half)))
                for i in range(CB + 2):
                    if i < CB:
                        act.wait_ge(pr.sem, pr.at(("w", c, i)))
                        if i >= 2:
                            act.wait_ge(pr.sem, pr.at(("u", c, i - 2)))
                        act.activation(WB[i % 2][:, 0:3:2, :], PB[2 + i % 2][:, 0:P].rearrange("p (a b) -> p a b", a=2), ACT.Copy).then_inc(ar.sem, ar.step(("w", c, i)))
                    if i >= 2:
                        cb = i - 2
                        act.wait_ge(pr.sem, pr.at(("sy", c, cb)))
                        act.activation(RT[:, cb, chunk(c)], PB[cb % 2][:, 0:P], ACT.Copy).then_inc(ar.sem, ar.step(("y", c, cb)))
            act.drain().then_inc(phase, 1)
            act.wait_ge(phase, phase_done("act"))
            for u in range(UWO, UWO + 3):
                split_hi(u)
            dg, pg = STEP["dve_gn"], STEP["pe_gn"]
            for cb in range(CB):
                act.wait_ge(dg.sem, dg.at(("yc", cb)))
                if cb >= 2:
                    act.wait_ge(pg.sem, pg.at(("var", cb - 2)))
                act.activation(SQT[cb % 2][:], RT[:, cb, :], ACT.Square).then_inc(ag.sem, ag.step(("sq", cb)))
            act.wait_ge(pg.sem, pg.at(("var", CB - 1)))
            act.wait_ge(dg.sem, dg.at("knz"))
            act.activation(KNI[0:HEADS, :], PB[4][0:HEADS, :], ACT.Sqrt, scale=1.0 / HD, bias=small[0:HEADS, 1:2]).then_inc(ag.sem, ag.step("root"))
            for cb in range(CB):
                act.wait_ge(STEP["pool_gn"].sem, STEP["pool_gn"].at(("o", cb)))
                act.activation(inh[:, cb, :], TV[cb % 2][:], ACT.Copy).then_inc(ag.sem, ag.step(("hi", cb)))
            act.drain().then_inc(phase, 1)
            act.wait_ge(phase, phase_done("act"))
            amlp, akv, aat = STEP["act_mlp"], STEP["act_kv"], STEP["act_att"]
            dmlp = STEP["dve_mlp"]

            def split_run(u0, n, loop=None):
                for u in range(u0, u0 + n):
                    split_hi(u + 3, loop)

            def gained_hi(name, dst, gain, kb):
                act.activation(dst[:, kb, :], X[:, kb, :], ACT.Copy, scale=col(gain, kb)).then_inc(an.sem, an.step(("hi", name, kb)))

            def x_stats(name, prev, dst, gain, last_unit):
                for kb in range(CB):
                    act.wait_ge(x_sum.sem, x_done(prev, kb))
                    if kb >= 2:
                        act.wait_ge(pn.sem, pn.at(("sum", name, kb - 2)))
                    act.activation(SQT[kb % 2][:], X[:, kb, :], ACT.Square).then_inc(an.sem, an.step(("sq", name, kb)))
                    if kb == 4:
                        act.wait_ge(lin.sem, used(last_unit, None))
                    if kb >= 4:
                        gained_hi(name, dst, gain, kb - 4)
                gained_hi(name, dst, gain, 4)
                gained_hi(name, dst, gain, 5)
                act.wait_ge(pn.sem, pn.at(("sum", name, CB - 1)))
                act.activation(RS[:], PB[0][:], ACT.Sqrt, scale=1.0 / C, bias=small[:, 0:1]).then_inc(an.sem, an.step(("root", name)))
                gained_hi(name, dst, gain, 6)
                gained_hi(name, dst, gain, 7)

            def mlp(layer, u0, name, prev, last_unit):
                x_stats(name, prev, inh, f"ln_mlp{layer}", last_unit)
                with turns(act, "act", name, 4, 16) as lp:
                    lp.first = u0
                    split_run(u0, 8, lp)
                    for m in range(CB):
                        act.wait_ge(dmlp.sem, dmlp.at(("r", name, m), lp))
                        act.activation(hidh[:, m, :], HR[m % 4][:], ACT.Square).then_inc(amlp.sem, amlp.step(("hh", name, m)))
                    split_run(u0 + 8, 8, lp)

            split_run(UWO, 8)
            mlp(0, UM0, "mlp0", "wo", UWO + 7)
            act.drain().then_inc(phase, 1)
            act.wait_ge(phase, phase_done("act"))
            x_stats("kv", "mlp0", inh, "kv_norm", UM0 + 63)
            for kb in range(CB):
                gained_hi("q", hidh, "ln_mix1", kb)
            split_run(UKV, 4)
            dk = STEP["dve_kv"]
            act.wait_ge(dk.sem, dk.at("kf"))
            act.activation(HS[2][:], KF[:], ACT.Square).then_inc(akv.sem, akv.step("ksq"))
            act.wait_ge(STEP["pe_kv"].sem, STEP["pe_kv"].at("kmean"))
            act.activation(RKN[:], PB[3][:], ACT.Sqrt, bias=small[:, 0:1]).then_inc(akv.sem, akv.step("kroot"))
            act.wait_ge(STEP["pe_kv"].sem, STEP["pe_kv"].at("vt"))
            act.activation(VK[:].rearrange("p a b -> p (a b)"), PB[4][:], ACT.Copy).then_inc(akv.sem, akv.step("vk"))
            act.wait_ge(dk.sem, dk.at("kn"))
            act.wait_ge(STEP["pool_mlp"].sem, STEP["pool_mlp"].at("kd"))
            for j in range(2):
                for half in range(2):
                    act.dma_start(KD[j][half][64 * half:64 * half + 64, :], KN[64 * j:64 * j + 64, :]).then_inc(kdup, 16)
            split_run(UQ, 8)
            for cb in range(CB):
                act.wait_ge(dk.sem, dk.at(("q", cb)))
                if cb >= 2:
                    act.wait_ge(STEP["pe_kv"].sem, STEP["pe_kv"].at(("qsum", cb - 2)))
                act.activation(SQT[cb % 2][:], QF[:, cb, :], ACT.Square).then_inc(akv.sem, akv.step(("qsq", cb)))
            act.wait_ge(STEP["pe_kv"].sem, STEP["pe_kv"].at(("qsum", CB - 1)))
            act.wait_ge(dk.sem, dk.at("qnz"))
            act.activation(QNI[0:HEADS, :], PB[0][0:HEADS, :], ACT.Sqrt, bias=small[0:HEADS, 66:67]).then_inc(akv.sem, akv.step("qroot"))
            act.drain().then_inc(phase, 1)
            act.wait_ge(phase, phase_done("act"))
            pa, da = STEP["pe_att"], STEP["dve_att"]
            NT = 32
            for i in range(NT + 5):
                if i < NT:
                    act.wait_ge(da.sem, da.at(("nm", i)))
                    st = small[:, 2 + 16 * (i % 4):]
                    h = 2 * (i // 4) + i % 2
                    for b in range(2):
                        pb = S1[i % 3][:, b * 256:(b + 1) * 256]
                        act.activation(pb, pb, ACT.Exp, bias=st[:, b:b + 1], accum_out=st[:, 2 + b:3 + b]).then_inc(aat.sem, aat.step())
                    act.activation(st[:, 4:6], st[:, 0:2], ACT.Exp, bias=col("sinks", h)).then_inc(aat.sem, aat.step(("exp", i)))
                if 2 <= i < NT + 2:
                    k = i - 2
                    act.wait_ge(pa.sem, pa.at(("tr", k)))
                    if k >= 3:
                        act.wait_ge(pa.sem, pa.at(("pv", k - 3)))
                    act.activation(PTR[k % 3][:], PB[4 + k % 2][:], ACT.Copy).then_inc(aat.sem, aat.step(("ptr", k)))
                if i >= 4 and (i - 4) % 2 == 1 and i - 4 < NT:
                    k = i - 4
                    pr_ = k // 2
                    cb, nn = divmod(pr_, 2)
                    act.wait_ge(pa.sem, pa.at(("pv", k)))
                    act.activation(inh[:, cb, nn * 256:(nn + 1) * 256], PB[6 + pr_ % 2][:, 0:256], ACT.Copy).then_inc(aat.sem, aat.step(("oh", pr_)))
            act.drain().then_inc(phase, 1)
            act.wait_ge(phase, phase_done("act"))
            aad, art, af, affn = (STEP["act_" + n] for n in ("ada", "ret", "four", "ffn"))
            dad, drt, dff = (STEP["dve_" + n] for n in ("ada", "ret", "ffn"))
            dmo = STEP["dve_mod"]
            pad, prt, pf = (STEP["pe_" + n] for n in ("ada", "ret", "four"))
            act.activation(LT[0][:], vec[:, COLS["c"]:COLS["c"] + 16], ACT.Sigmoid).then_inc(aad.sem, aad.step("sig"))
            act.wait_ge(dmo.sem, dmo.at("abs"))
            act.activation(LT[1][:, 0:8], LT[1][:, 0:8], ACT.Exp, scale=-1.0).then_inc(aad.sem, aad.step("eabs"))
            split_run(UBO, 8)
            act.wait_ge(dmo.sem, dmo.at("cpos"))
            wc = WC[:].rearrange("p a b c -> p (a b c)")
            act.activation(wc, wc, ACT.Exp).then_inc(aad.sem, aad.step("wc"))
            mlp(1, UM1, "mlp1", "bo", UBO + 7)
            act.drain().then_inc(phase, 1)
            act.wait_ge(phase, phase_done("act"))
            def modulated_hi(name, dst, tmp, shift, n=T):
                for kb in range(CB):
                    act.wait_ge(dad.sem, dad.at(("t", name, kb)))
                    act.activation(dst[:, kb, :n], tmp[kb % 2][:, :n], ACT.Identity, bias=shift(kb)).then_inc(aad.sem, aad.step(("hi", name, kb)))

            def stats_of(name, block_, ready=None, n=T):
                for kb in range(CB):
                    if ready is not None:
                        ready(kb)
                    if kb >= 2:
                        act.wait_ge(pn.sem, pn.at(("sum", name, kb - 2)))
                    act.activation(SQT[kb % 2][:, :n], block_(kb), ACT.Square).then_inc(an.sem, an.step(("sq", name, kb)))
                act.wait_ge(pn.sem, pn.at(("sum", name, CB - 1)))
                act.activation(RS[:, :n], PB[0][:, :n], ACT.Sqrt, scale=1.0 / C, bias=small[:, 0:1]).then_inc(an.sem, an.step(("root", name)))

            act.wait_ge(in_a, 32)
            stats_of("ctx", lambda kb: CX[:, kb, :], n=CTX)
            modulated_hi("ctx", chh, CT, lambda kb: adac[:, kb, 1:2], CTX)
            split_run(UCTX, 8)
            for tb in range(2):
                act.wait_ge(lin.sem, lin.at(("bank", "ctx", 2 * tb + 1)))
                for d in range(2):
                    for h in range(RH):
                        act.activation(KW[d][tb][:, h * P:(h + 1) * P], PB[2 * tb][:, h * P:(h + 1) * P], ACT.Copy, scale=WC[:, tb, d, h:h + 1]).then_inc(art.sem, art.step())
                act.activation(VC[tb][:], PB[2 * tb + 1][:], ACT.Copy).then_inc(art.sem, art.step(("kv", tb)))
            for d in range(2):
                act.wait_ge(prt.sem, prt.at(("state", d)))
                act.activation(SFB[:, 4 * d:4 * d + 4, :].rearrange("p a b -> p (a b)"), PB[4 + d][:], ACT.Copy).then_inc(art.sem, art.step(("state", d)))
            act.drain().then_inc(phase, 1)
            act.wait_ge(phase, phase_done("act"))
            stats_of("lat", lambda kb: X[:, kb, :])
            modulated_hi("lat", inh, TQ, lambda kb: adac[:, kb, 0:1])
            split_run(UIN, 16)
            for m in range(RH):
                act.wait_ge(lin.sem, lin.at(("bank", "g", m)))
                if m >= 2:
                    act.wait_ge(drt.sem, drt.at(("g", m - 2)))
                act.activation(TQ[m % 2][:], PB[4 + m][:], ACT.Sigmoid).then_inc(art.sem, art.step(("sig", m)))
            split_run(UIN + 16, 4)
            act.drain().then_inc(phase, 1)
            act.wait_ge(phase, phase_done("act"))
            for g in range(4):
                for j in range(2):
                    act.wait_ge(pf.sem, pf.at(("ab", g, j)))
                    if g >= 1 and j == 0:
                        act.wait_ge(pf.sem, pf.at(("f", g - 1)))
                    act.activation(FAB[:, 2 * j:2 * j + 2, :].rearrange("p a b -> p (a b)"), PB[j][:], ACT.Copy).then_inc(af.sem, af.step(("ab", g, j)))
                act.wait_ge(pf.sem, pf.at(("f", g)))
                act.activation(inh[:, 4 + g, :], PB[2 + g % 2][:], ACT.Copy).then_inc(af.sem, af.step(("hi", g)))
            act.drain().then_inc(phase, 1)
            act.wait_ge(phase, phase_done("act"))
            act.wait_ge(in_t, 112)

            def decays(h):
                act.wait_ge(drt.sem, drt.at(("dm", h)))
                act.activation(DM[h % 2][:], DM[h % 2][:], ACT.Exp).then_inc(art.sem, art.step(("dm", h)))
                for d in range(2):
                    if h > 0:
                        act.wait_ge(drt.sem, drt.at(("qx", h - 1, d)))
                    act.activation(HE[d][:], RAMP[:, d, :], ACT.Exp, scale=LG[:, 4 * d + h:4 * d + h + 1]).then_inc(art.sem, art.step(("xi", h, d)))

            decays(0)
            for h in range(RH):
                if h + 1 < RH:
                    decays(h + 1)
                act.wait_ge(prt.sem, prt.at(("out", h)))
                if h >= 1:
                    act.wait_ge(prt.sem, prt.at(("sum", h - 1)))
                act.activation(TQ[0][:], PB[4 + h % 2][:], ACT.Square).then_inc(art.sem, art.step(("sq", h)))
                if h >= 2:
                    act.wait_ge(drt.sem, drt.at(("lo", h - 2)))
                act.activation(RET[h % 2][:], PB[4 + h % 2][:], ACT.Copy).then_inc(art.sem, art.step(("o", h)))
                act.wait_ge(prt.sem, prt.at(("sum", h)))
                if h >= 1:
                    act.wait_ge(drt.sem, drt.at(("n", h - 1)))
                act.activation(RR[:], PB[6][:], ACT.Sqrt, scale=1.0 / P, bias=small[:, 0:1]).then_inc(art.sem, art.step(("root", h)))
                act.wait_ge(drt.sem, drt.at(("ret", h)))
                act.activation(inh[:, h, :], RET[h % 2][:], ACT.Copy).then_inc(art.sem, art.step(("hi", h)))
            act.drain().then_inc(phase, 1)
            act.wait_ge(phase, phase_done("act"))
            split_run(UOUT, 8)
            stats_of("mx", lambda kb: MX[:, kb, :], lambda kb: act.wait_ge(drt.sem, drt.at(("mx", kb))))
            stats_of("fp", lambda kb: X[:, kb, :], lambda kb: act.wait_ge(drt.sem, drt.at(("x", kb))))
            act.wait_ge(fill, 32)
            act.dma_start(xsp, X[:]).then_inc(spill, 16)
            modulated_hi("fp", inh, TQ, lambda kb: adac[:, 24 + kb, 0:1])
            act.drain().then_inc(phase, 1)
            act.wait_ge(phase, phase_done("act"))
            act.wait_ge(spill, 48)

            def gated(s):
                q, name, loop = s.q, s.name, s.loop
                act.wait_ge(dff.sem, dff.at(("cw", name, q), loop))
                for j in range(2):
                    if s.before is not None:
                        act.wait_ge(dff.sem, prior(dff, "h", s.before, j))
                    for hf in range(2):
                        act.wait_ge(lin.sem, lin.at(("bank", name, q, 2 * j + hf), loop))
                        act.activation(CV[2 * j + hf][:], PB[4 * q + 2 * j + hf][:], ACT.Identity, scale=CWT[q][:, 1, hf, j:j + 1],
                                                bias=CWT[q][:, 3, hf, j:j + 1]).then_inc(affn.sem, affn.step(("cv", name, q, 2 * j + hf)))
                for j in range(2):
                    act.wait_ge(dff.sem, dff.at(("cv", name, q, 2 * j), loop))
                    act.activation(SG[j][:], CV[2 * j][:], ACT.Silu).then_inc(affn.sem, affn.step(("sg", name, q, j)))
                for j in range(2):
                    act.wait_ge(dff.sem, dff.at(("h", name, q, j), loop))
                    act.activation(GH[:, s.at[j]], HT[j][:], ACT.Copy).then_inc(affn.sem, affn.step(("hh", name, q, j)))

            up_passes(act, "act", split_run, gated)
            act.wait_ge(lin.sem, used(UF + 43, None))
            act.dma_start(X2[:], xsp.rearrange("p (a b) -> p a b", a=CB)).then_inc(fill, 16)
            split_run(UF + 44, NFB - 3)
            stats_of("fo", lambda kb: FO[:, kb, :], lambda kb: act.wait_ge(dff.sem, dff.at(("fo", kb))))
        @block.vector
        def _(dve):
            dn, dm, dl = STEP["dve_norm"], STEP["dve_mix"], STEP["dve_lora"]
            an = STEP["act_norm"]

            def split_lo(u, loop=None):
                dve.wait_ge(w_hi, turn(u + 1, loop))
                dve.tensor_tensor(wlo[u % SLOTS][:, :], raw[u % SLOTS][:, :], whi[u % SLOTS][:, :].bitcast(F32), ALU.subtract).then_inc(w_lo, 1)

            def rstd(name, n=T):
                dve.wait_ge(an.sem, an.at(("root", name)))
                dve.reciprocal(RS[:, :n], RS[:, :n]).then_inc(dn.sem, dn.step(("rstd", name)))
                return dn.n

            dve.memset(small[:, 0:1], RMS_EPS).then_inc(dn.sem, dn.step())
            dve.memset(small[:, 1:2], GN_EPS).then_inc(dn.sem, dn.step("eps"))
            dve.wait_ge(in_v, 16)
            r = rstd("n0")
            dve.wait_ge(dn.sem, r)
            for q in range(4):
                dve.wait_ge(in_x[q], 16)
            for kb in range(CB):
                dve.scalar_tensor_tensor(H[:, kb, :], XT[:, kb, :], col("ln_mix0", kb), RS[:, :], ALU.mult, ALU.mult).then_inc(dn.sem, dn.step(("h", kb), "h0"))
                dve.wait_ge(dn.sem, dn.n)
                dve.tensor_tensor(XX[:, kb, 1:T], H[:, kb, 0:T - 1], H[:, kb, 1:T], ALU.subtract).then_inc(dn.sem, dn.step())
                dve.tensor_scalar(XX[:, kb, 0:1], H[:, kb, 0:1], -1.0, None, ALU.mult).then_inc(dn.sem, dn.step())
                dve.wait_ge(dn.sem, dn.n)
                if kb >= 4:
                    dve.wait_ge(STEP["pe_lora"].sem, STEP["pe_lora"].at(("used", kb - 4)))
                dve.scalar_tensor_tensor(xl[kb % 4][:], XX[:, kb, :], col("mu", 8 * 5 + kb), H[:, kb, :], ALU.mult, ALU.add).then_inc(dl.sem, dl.step(("x", kb)))
            n = CB
            for name, mu in (("w", 3), ("a", 4)):
                for kb in range(CB):
                    if n >= 4:
                        dve.wait_ge(STEP["pe_lora"].sem, STEP["pe_lora"].at(("used", n - 4)))
                    dve.scalar_tensor_tensor(xl[n % 4][:], XX[:, kb, :], col("mu", 8 * mu + kb), H[:, kb, :], ALU.mult, ALU.add).then_inc(dl.sem, dl.step(("x", n)))
                    n += 1
            for u in range(3):
                split_lo(u)
            dve.drain().then_inc(phase, 1)
            dve.wait_ge(phase, phase_done("dve"))
            dve.wait_ge(spill, 32)

            def mix(u):
                if u >= 4:
                    dve.wait_ge(STEP["act_mix"].sem, STEP["act_mix"].at(("hi", u - 4)))
                    dve.wait_ge(dm.sem, dm.at(lo_at[u - 4]))
                dve.scalar_tensor_tensor(xt4[u % 4][:], XX[:, u % 8, :], col("mu", 8 * (u // 8) + u % 8), H[:, u % 8, :], ALU.mult, ALU.add).then_inc(dm.sem, dm.step(("mix", u)))

            lo_at = {}

            def mix_lo(u):
                dve.wait_ge(STEP["act_mix"].sem, STEP["act_mix"].at(("hi", u)))
                dve.tensor_tensor(xml[u % NR][:], xt4[u % 4][:], xmh[u % NR][:].bitcast(F32), ALU.subtract).then_inc(dm.sem, dm.step(("lo", u)))
                lo_at[u] = dm.n

            for u in range(3):
                mix(u)
            for u in range(2):
                mix_lo(u)
            for u in range(24):
                if u + 3 < 24:
                    split_lo(u + 3)
                if u + 3 < 24:
                    mix(u + 3)
                if u + 2 < 24:
                    mix_lo(u + 2)
                if u % 8 == 7:
                    dst = (R, K_, V)[u // 8]
                    for m in range(CB):
                        dve.wait_ge(lin.sem, lin.at(("bank", u // 8, m)))
                        dve.tensor_copy(dst[:, m, :], PB[m][:]).then_inc(dm.sem, dm.step(("taken", u // 8, m)))
            dve.drain().then_inc(phase, 1)
            dve.wait_ge(phase, phase_done("dve"))

            dp, ds, di, dr, dg = (STEP["dve_" + n] for n in ("prep", "score", "inv", "rec", "gn"))
            ap_, pp, pr = STEP["act_prep"], STEP["pe_prep"], STEP["pe_rec"]
            pre = PREP
            dve.memset(RKS[:], 0.0).then_inc(dp.sem, dp.step("rkz"))
            dve.memset(KNI[:], 0.0).then_inc(dp.sem, dp.step("knz"))
            dve.wait_ge(ap_.sem, ap_.at("kroot"))
            dve.tensor_scalar(KNI[0:HEADS, :], KNI[0:HEADS, :], 1e-12, None, ALU.max).then_inc(dp.sem, dp.step())
            k = dp.n
            dve.wait_ge(dp.sem, k)
            dve.reciprocal(KNI[0:HEADS, :], KNI[0:HEADS, :]).then_inc(dp.sem, dp.step("kni"))
            for cb in range(CB):
                p = cb % 2
                if cb >= 2:
                    dve.wait_ge(ap_.sem, ap_.at(("exps", cb - 2)))
                    dve.wait_ge(STEP["pool_prep"].sem, STEP["pool_prep"].at(("done", cb - 2)))
                    dve.wait_ge(pp.sem, pp.at(("rks", cb - 2)))
                    dve.wait_ge(dp.sem, dp.at(("at", cb - 2)))
                for c in range(TB):
                    dve.tensor_tensor_scan(pre["cs"][p][:, chunk(c)], sq("ones"), SIG[:, cb, chunk(c)], 0.0, ALU.mult, ALU.add).then_inc(dp.sem, dp.step())
                    k = dp.n
                dve.wait_ge(dp.sem, k)
                cs = quad(pre["cs"][p][:])
                dve.tensor_tensor(quad(pre["csn"][p][:]), cs, cs[:, :, 63:64].to_broadcast([P, 4, P]), ALU.subtract).then_inc(dp.sem, dp.step(("csn", cb)))
                k = dp.n
                dve.tensor_scalar(pre["t1"][p][:], AA[:, cb, :], 1.0, col("k_a", cb), ALU.subtract, ALU.mult).then_inc(dp.sem, dp.step(("t1", cb)))
                t1 = dp.n
                dve.wait_ge(dp.sem, k)
                dve.tensor_tensor(pre["csx"][p][:], pre["csn"][p][:], SIG[:, cb, :], ALU.subtract).then_inc(dp.sem, dp.step(("csx", cb)))
                dve.wait_ge(dp.sem, t1)
                dve.scalar_tensor_tensor(pre["km"][p][:], pre["t1"][p][:], 1.0, K_[:, cb, :], ALU.add, ALU.mult).then_inc(dp.sem, dp.step())
                km = dp.n
                dve.wait_ge(pp.sem, pp.at(("bc", cb)))
                dve.scalar_tensor_tensor(pre["kn"][p][:], K_[:, cb, :], col("k_k", cb), PB[1 + p][:], ALU.mult, ALU.mult).then_inc(dp.sem, dp.step(("kn", cb)))
                kn = dp.n
                dve.wait_ge(dp.sem, km)
                dve.scalar_tensor_tensor(pre["rk"][p][:], R[:, cb, :], col("r_k", cb), pre["km"][p][:], ALU.mult, ALU.mult).then_inc(dp.sem, dp.step(("rk", cb)))
                dve.wait_ge(dp.sem, kn)
                dve.wait_ge(ap_.sem, ap_.at(("e2", cb)))
                dve.tensor_tensor(KT[:, cb, :], pre["km"][p][:], pre["e2"][p][:], ALU.mult).then_inc(dp.sem, dp.step())
                dve.wait_ge(ap_.sem, ap_.at(("e3", cb)))
                dve.scalar_tensor_tensor(AT[:, cb, :], pre["kn"][p][:], -1.0, pre["e3"][p][:], ALU.mult, ALU.mult).then_inc(dp.sem, dp.step(("at", cb)))
            dve.wait_ge(pp.sem, pp.at(("rks", CB - 1)))
            dve.wait_ge(dp.sem, dp.at("rkz"))
            dve.tensor_copy(RKS[0:HEADS, :], PB[3][0:HEADS, :]).then_inc(dp.sem, dp.step())
            dve.drain().then_inc(phase, 1)
            dve.wait_ge(phase, phase_done("dve"))
            dve.memset(SS[:], 0.0).then_inc(dr.sem, dr.step("s0"))

            def score_masks(c, half):
                for kind in range(5):
                    for p in range(2):
                        g = 2 * half + p
                        dve.wait_ge(STEP["pe_score"].sem, STEP["pe_score"].at((c, half, kind, p)))
                        b = quad(PB[p][:])
                        if kind == 0:
                            dve.tensor_tensor(quad(TI[p][:]), b, four("m0"), ALU.mult).then_inc(ds.sem, ds.step(("ti", c, half, p)))
                            dve.tensor_tensor(quad(LL[p][:]), b, four("lower"), ALU.mult).then_inc(ds.sem, ds.step(("taken", c, half, kind, p)))
                        else:
                            dst, mask = {1: (ZI, "m0t"), 2: (MT, "upper"), 3: (GBm, "upper_in"), 4: (GKm, "upper_in")}[kind]
                            dve.tensor_tensor(quad(dst[:, g, :]), b, four(mask), ALU.mult).then_inc(ds.sem, ds.step(("taken", c, half, kind, p)))

            def inverse_sums(c, half):
                for lv in range(LEVELS):
                    for p in range(2):
                        g = 2 * half + p
                        dve.wait_ge(STEP["pe_inv"].sem, STEP["pe_inv"].at(("tz", c, half, lv, p)))
                        if lv < LEVELS - 1:
                            dve.tensor_tensor(TI[p][:], TI[p][:], PB[4 + p][:], ALU.add).then_inc(di.sem, di.step())
                        dve.tensor_tensor(ZI[:, g, :], ZI[:, g, :], PB[6 + p][:], ALU.add).then_inc(di.sem, di.step(("z", c, half, lv, p)))

            for c in range(TB):
                if c > 0:
                    dve.wait_ge(pr.sem, pr.at(("sy", c - 1, CB - 1)))
                for half in range(2):
                    score_masks(c, half)
                    inverse_sums(c, half)
                for i in range(CB + 2):
                    p = i % 2
                    if i < CB:
                        if i >= 4:
                            dve.wait_ge(pr.sem, pr.at(("sy", c, i - 4)))
                            dve.wait_ge(dr.sem, dr.at(("s", c, i - 4)))
                        if c == 0:
                            dve.wait_ge(dr.sem, dr.at("s0"))
                        else:
                            dve.wait_ge(dr.sem, dr.at(("s", c - 1, i)))
                        dve.tensor_scalar(SM[i % 4][:], SS[:, i, :], DMID[:, 4 * i + c:4 * i + c + 1], None, ALU.mult).then_inc(dr.sem, dr.step(("sm", c, i)))
                    if 1 <= i <= CB:
                        dve.wait_ge(pr.sem, pr.at(("u", c, i - 1)))
                        if i >= 3:
                            dve.wait_ge(pr.sem, pr.at(("sy", c, i - 3)))
                        dve.tensor_copy(UB[(i - 1) % 2][:], PB[4 + (i - 1) % 2][:, 0:P]).then_inc(dr.sem, dr.step(("u", c, i - 1)))
                    if i >= 2:
                        cb = i - 2
                        q = cb % 2
                        dve.wait_ge(pr.sem, pr.at(("s", c, cb)))
                        if c > 0 or cb >= 2:
                            dve.wait_ge(dr.sem, dr.at(("s", c, cb - 2) if cb >= 2 else ("s", c - 1, CB - 2 + cb)))
                        dve.tensor_tensor(TS[q][:], PB[6 + q][:, 0:P], sq("blk"), ALU.mult).then_inc(dr.sem, dr.step())
                        k = dr.n
                        dve.wait_ge(dr.sem, k)
                        dve.tensor_tensor(TS[q][:], TS[q][:], SM_at(c, cb), ALU.add).then_inc(dr.sem, dr.step())
                        k = dr.n
                        dve.wait_ge(dr.sem, k)
                        dve.tensor_scalar(SS[:, cb, :], TS[q][:], DEND[:, 4 * cb + c:4 * cb + c + 1], None, ALU.mult).then_inc(dr.sem, dr.step(("s", c, cb)))
            dve.drain().then_inc(phase, 1)
            dve.wait_ge(phase, phase_done("dve"))
            pg, ag = STEP["pe_gn"], STEP["act_gn"]
            dve.memset(KNI[:], 0.0).then_inc(dg.sem, dg.step("knz"))
            for cb in range(CB):
                dve.wait_ge(pg.sem, pg.at(("mean", cb)))
                dve.tensor_tensor(RT[:, cb, :], RT[:, cb, :], PB[cb % 4][:], ALU.subtract).then_inc(dg.sem, dg.step(("yc", cb)))
            for u in range(UWO, UWO + 3):
                split_lo(u)
            dve.wait_ge(ag.sem, ag.at("root"))
            dve.reciprocal(KNI[0:HEADS, :], KNI[0:HEADS, :]).then_inc(dg.sem, dg.step("gni"))
            dve.wait_ge(fill, 32)
            def gn_lo(cb):
                dve.wait_ge(ag.sem, ag.at(("hi", cb)))
                dve.tensor_tensor(inl[:, cb, :], TV[cb % 2][:], inh[:, cb, :].bitcast(F32), ALU.subtract).then_inc(dg.sem, dg.step(("lo", cb)))
            for cb in range(CB):
                p = cb % 2
                if cb >= 2:
                    dve.wait_ge(STEP["pool_gn"].sem, STEP["pool_gn"].at(("o", cb - 2)))
                    dve.wait_ge(dg.sem, dg.at(("lo", cb - 2)))
                dve.wait_ge(pg.sem, pg.at(("bc1", cb)))
                dve.scalar_tensor_tensor(TG[p][:], RT[:, cb, :], col("gn_g", cb), PB[5 + p][:], ALU.mult, ALU.mult).then_inc(dg.sem, dg.step(("t1", cb)))
                k = dg.n
                dve.wait_ge(pg.sem, pg.at(("bc2", cb)))
                dve.tensor_tensor(TV[p][:], V[:, cb, :], PB[p][:], ALU.mult).then_inc(dg.sem, dg.step(("t2", cb)))
                k = dg.n
                dve.wait_ge(dg.sem, k)
                dve.scalar_tensor_tensor(TG[p][:], TG[p][:], col("gn_b", cb), TV[p][:], ALU.add, ALU.add).then_inc(dg.sem, dg.step(("t3", cb)))
                if cb >= 1:
                    gn_lo(cb - 1)
            gn_lo(CB - 1)
            dve.drain().then_inc(phase, 1)
            dve.wait_ge(phase, phase_done("dve"))
            dmlp, dk, da = STEP["dve_mlp"], STEP["dve_kv"], STEP["dve_att"]
            amlp, akv, aat, pkv = STEP["act_mlp"], STEP["act_kv"], STEP["act_att"], STEP["pe_kv"]
            dve.memset(small[:, 66:67], 64 * RMS_EPS).then_inc(dn.sem, dn.step("eps64"))

            def split_run(u0, n, loop=None):
                for u in range(u0, u0 + n):
                    split_lo(u + 3, loop)

            def add_x(stage, loop=None):
                for m in range(CB):
                    dve.wait_ge(lin.sem, lin.at(("bank", stage, m), loop))
                    dve.tensor_tensor(X[:, m, :], X[:, m, :], PB[m][:], ALU.add).then_inc(dmlp.sem, dmlp.step(("x", stage, m)))

            def gained_lo(name, dst_h, dst_l, gain):
                for kb in range(CB):
                    dve.wait_ge(an.sem, an.at(("hi", name, kb)))
                    dve.scalar_tensor_tensor(dst_l[:, kb, :], X[:, kb, :], col(gain, kb), dst_h[:, kb, :].bitcast(F32), ALU.mult, ALU.subtract).then_inc(dn.sem, dn.step(("lo", name, kb)))

            def mlp(layer, u0, name):
                gained_lo(name, inh, inl, f"ln_mlp{layer}")
                k = rstd(name)
                dve.wait_ge(dn.sem, k)
                with turns(dve, "dve", name, 4, 16) as lp:
                    lp.first = u0

                    def hidden_lo(m):
                        dve.wait_ge(amlp.sem, amlp.at(("hh", name, m), lp))
                        dve.wait_ge(STEP["pool_mlp"].sem, STEP["pool_mlp"].at(("hs", name, m), lp))
                        dve.tensor_tensor(hidl[:, m, :], HS[m % 4][:], hidh[:, m, :].bitcast(F32), ALU.subtract).then_inc(dmlp.sem, dmlp.step(("hl", name, m)))

                    def modulation_sum(k):
                        dve.wait_ge(in_mod[k % 4], lp.i * 32 + 16 * (k // 4 + 1))
                        for v in range(2):
                            w, c_, acc = ADW[k % 4][:, 0:AX_ if v else AC], LT[0][:, 8 * v + k:8 * v + k + 1], ADS[v][:]
                            if k == 0:
                                dve.tensor_scalar(acc, w, c_, None, ALU.mult).then_inc(dmo.sem, dmo.step(("sum", v, k), ("sum", k)))
                            else:
                                dve.wait_ge(dmo.sem, dmo.at(("sum", v, k - 1), lp))
                                dve.scalar_tensor_tensor(acc, w, c_, acc, ALU.mult, ALU.add).then_inc(dmo.sem, dmo.step(("sum", v, k), ("sum", k)))

                    for k in range(CB):
                        split_run(u0 + k, 1, lp)
                        if layer == 1:
                            modulation_sum(k)
                    for m in range(CB):
                        dve.wait_ge(lin.sem, lin.at(("bank", name + "up", m), lp))
                        if m >= 4:
                            dve.wait_ge(amlp.sem, amlp.at(("hh", name, m - 4), lp))
                            dve.wait_ge(STEP["pool_mlp"].sem, STEP["pool_mlp"].at(("hs", name, m - 4), lp))
                        dve.scalar_tensor_tensor(HR[m % 4][:], PB[m][:], 0.0, RS[:], ALU.max, ALU.mult).then_inc(dmlp.sem, dmlp.step(("r", name, m)))
                        if layer == 1 and m == 3:
                            dve.wait_ge(pad.sem, pad.at("columns", lp))
                            cols = PB[0][:, 0:24].rearrange("p (a b) -> p a b", b=2)
                            dve.tensor_copy(adac[:, bass.ds(lp.i * 4, 4), :], cols[:, 0:4, :]).then_inc(dmo.sem, dmo.step())
                            dve.tensor_copy(adac[:, bass.ds(lp.i * 8 + 16, 8), 0:1], cols[:, 4:12, 0:1]).then_inc(dmo.sem, dmo.step("columns"))
                        if m >= 2:
                            hidden_lo(m - 2)
                    hidden_lo(6)
                    hidden_lo(7)
                    split_run(u0 + 8, 8, lp)
                    add_x(name, lp)

            split_run(UWO, 8)
            add_x("wo")
            mlp(0, UM0, "mlp0")
            dve.drain().then_inc(phase, 1)
            dve.wait_ge(phase, phase_done("dve"))
            dve.memset(QNI[:], 0.0).then_inc(dk.sem, dk.step("qnz"))
            gained_lo("kv", inh, inl, "kv_norm")
            k = rstd("kv")
            gained_lo("q", hidh, hidl, "ln_mix1")
            split_run(UKV, 4)
            dve.wait_ge(dn.sem, k)
            dve.wait_ge(lin.sem, lin.at(("bank", "kv", 0)))
            dve.tensor_tensor(KF[:], PB[1][:], RS[:], ALU.mult).then_inc(dk.sem, dk.step("kf"))
            dve.wait_ge(lin.sem, lin.at(("bank", "kv", 1)))
            dve.tensor_tensor(VF[:], PB[2][:], RS[:], ALU.mult).then_inc(dk.sem, dk.step("vf"))
            dve.wait_ge(akv.sem, akv.at("kroot"))
            dve.reciprocal(RKN[:], RKN[:]).then_inc(dk.sem, dk.step())
            k = dk.n
            dve.wait_ge(dk.sem, k)
            dve.scalar_tensor_tensor(KN[:], KF[:], col("k_gain"), RKN[:], ALU.mult, ALU.mult).then_inc(dk.sem, dk.step("kn"))
            split_run(UQ, 8)
            for m in range(CB):
                dve.wait_ge(lin.sem, lin.at(("bank", "q", m)))
                dve.tensor_tensor(QF[:, m, :], PB[m][:], RS[:], ALU.mult).then_inc(dk.sem, dk.step(("q", m)))
            dve.wait_ge(akv.sem, akv.at("qroot"))
            dve.reciprocal(QNI[0:HEADS, :], QNI[0:HEADS, :]).then_inc(dk.sem, dk.step("qni"))
            for cb in range(CB):
                dve.wait_ge(pkv.sem, pkv.at(("qbc", cb)))
                dve.scalar_tensor_tensor(QF[:, cb, :], QF[:, cb, :], col("q_gain"), PB[1 + cb % 2][:], ALU.mult, ALU.mult).then_inc(dk.sem, dk.step(("qn", cb)))
            dve.wait_ge(in_c, 16 * 10)
            dve.drain().then_inc(phase, 1)
            dve.wait_ge(phase, phase_done("dve"))
            pa = STEP["pe_att"]
            NT = 32
            for i in range(NT + 5):
                if i < NT:
                    h, nn = 2 * (i // 4) + i % 2, (i // 2) % 2
                    st = small[:, 2 + 16 * (i % 4):]
                    dve.wait_ge(pa.sem, pa.at(("s", i)))
                    if i >= 3:
                        dve.wait_ge(pa.sem, pa.at(("tr", i - 3)))
                    dve.scalar_tensor_tensor(S1[i % 3][:].rearrange("p (a b) -> p a b", a=2), BAND[:, nn:nn + 2, :],
                                                        -(2.0 ** (-8.0 * (h + 1) / HEADS)),
                                                        PB[i % 4][:].rearrange("p (a b) -> p a b", a=2), ALU.mult, ALU.add).then_inc(da.sem, da.step(("taken", i)))
                    k = da.n
                    dve.wait_ge(da.sem, k)
                    if i >= 4:
                        dve.wait_ge(da.sem, da.at(("den", i - 4)))
                    dve.tensor_reduce(st[:, 8:10], S1[i % 3][:].rearrange("p (a b) -> p a b", a=2), AX.X, ALU.max).then_inc(da.sem, da.step())
                    k = da.n
                    dve.wait_ge(da.sem, k)
                    dve.tensor_scalar(st[:, 0:2], st[:, 8:10], col("sinks", h), -1.0, ALU.max, ALU.mult).then_inc(da.sem, da.step(("nm", i)))
                if 1 <= i <= NT:
                    k = i - 1
                    st = small[:, 2 + 16 * (k % 4):]
                    dve.wait_ge(aat.sem, aat.at(("exp", k)))
                    dve.tensor_tensor(st[:, 6:8], st[:, 2:4], st[:, 4:6], ALU.add).then_inc(da.sem, da.step())
                    w = da.n
                    dve.wait_ge(da.sem, w)
                    dve.reciprocal(st[:, 6:8], st[:, 6:8]).then_inc(da.sem, da.step())
                    w = da.n
                    dve.wait_ge(da.sem, w)
                    for b in range(2):
                        pb = S1[k % 3][:, b * 256:(b + 1) * 256]
                        dve.tensor_scalar(pb, pb, st[:, 6 + b:7 + b], None, ALU.mult).then_inc(da.sem, da.step(*([("den", k)] if b else [])))
                        w = da.n
                if i >= 4 and (i - 4) % 2 == 1 and i - 4 < NT:
                    pr_ = (i - 4) // 2
                    cb, nn = divmod(pr_, 2)
                    dve.wait_ge(aat.sem, aat.at(("oh", pr_)))
                    cs = slice(nn * 256, (nn + 1) * 256)
                    dve.tensor_tensor(inl[:, cb, cs], PB[6 + pr_ % 2][:, 0:256], inh[:, cb, cs].bitcast(F32), ALU.subtract).then_inc(da.sem, da.step(("ol", pr_)))
            dve.drain().then_inc(phase, 1)
            dve.wait_ge(phase, phase_done("dve"))
            dad, drt, df, dff = (STEP["dve_" + n] for n in ("ada", "ret", "four", "ffn"))
            aad, art, af, affn = (STEP["act_" + n] for n in ("ada", "ret", "four", "ffn"))
            pad, prt, pf = (STEP["pe_" + n] for n in ("ada", "ret", "four"))
            dmo = STEP["dve_mod"]
            y = vec[:, COLS["decay"]:COLS["decay"] + 8]
            neg, e, s_, s2, low = LT[2][:, 0:8], LT[1][:, 0:8], LT[3][:, 0:8], LT[4][:, 0:8], LT[3][:, 8:16]

            dve.tensor_scalar(neg, y, -1.0, None, ALU.mult).then_inc(dmo.sem, dmo.step())
            dve.wait_ge(dmo.sem, dmo.n)
            dve.tensor_tensor(e, neg, y, ALU.max).then_inc(dmo.sem, dmo.step("abs"))
            dve.wait_ge(dmo.sem, dmo.n)
            dve.tensor_scalar(low, neg, 0.0, None, ALU.max).then_inc(dmo.sem, dmo.step())
            dve.wait_ge(dmo.sem, dmo.n)
            dve.wait_ge(aad.sem, aad.at("sig"))
            dve.tensor_tensor(LT[0][:], LT[0][:], vec[:, COLS["c"]:COLS["c"] + 16], ALU.mult).then_inc(dmo.sem, dmo.step("silu"))
            dve.wait_ge(dmo.sem, dmo.n)
            dve.wait_ge(aad.sem, aad.at("eabs"))
            dve.tensor_scalar(s_, e, 2.0, None, ALU.add).then_inc(dmo.sem, dmo.step())
            dve.wait_ge(dmo.sem, dmo.n)
            dve.reciprocal(s_, s_).then_inc(dmo.sem, dmo.step())
            dve.wait_ge(dmo.sem, dmo.n)
            dve.tensor_tensor(s_, s_, e, ALU.mult).then_inc(dmo.sem, dmo.step())
            dve.wait_ge(dmo.sem, dmo.n)
            dve.tensor_tensor(s2, s_, s_, ALU.mult).then_inc(dmo.sem, dmo.step())
            dve.wait_ge(dmo.sem, dmo.n)
            dve.tensor_scalar(e, s2, 1.0 / 19, None, ALU.mult).then_inc(dmo.sem, dmo.step())
            dve.wait_ge(dmo.sem, dmo.n)
            for n in range(8, 0, -1):
                dve.scalar_tensor_tensor(e, e, 1.0 / (2 * n + 1), s2, ALU.add, ALU.mult).then_inc(dmo.sem, dmo.step())
                dve.wait_ge(dmo.sem, dmo.n)
            dve.scalar_tensor_tensor(e, e, 1.0, s_, ALU.add, ALU.mult).then_inc(dmo.sem, dmo.step())
            dve.wait_ge(dmo.sem, dmo.n)
            dve.scalar_tensor_tensor(LG[:], e, -2.0, low, ALU.mult, ALU.subtract).then_inc(dmo.sem, dmo.step())
            dve.wait_ge(dmo.sem, dmo.n)
            dve.wait_ge(in_a, 16)
            for tb in range(2):
                for d in range(2):
                    dve.tensor_scalar(WC[:, tb, d, :], LG[:, 4 * d:4 * d + 4], CPOS[:, 2 * tb + d:2 * tb + d + 1], None, ALU.mult).then_inc(dmo.sem, dmo.step("cpos"))
                    dve.wait_ge(dmo.sem, dmo.n)
            split_run(UBO, 8)
            add_x("bo")
            mlp(1, UM1, "mlp1")
            b_ada = vec[:, COLS["b_ada"]:COLS["b_ada"] + 48]
            dve.wait_ge(dmo.sem, dmo.at(("last", "columns")))
            dve.tensor_tensor(adac[:, 0:16, :], adac[:, 0:16, :], b_ada[:, 0:16].unsqueeze(2).to_broadcast([P, 16, 2]), ALU.add).then_inc(dmo.sem, dmo.step())
            dve.tensor_tensor(adac[:, 16:48, 0], adac[:, 16:48, 0], b_ada[:, 16:48], ALU.add).then_inc(dmo.sem, dmo.step("mod"))
            dve.wait_ge(dmo.sem, dmo.n)
            dve.wait_ge(aad.sem, aad.at("wc"))
            dve.tensor_scalar(WC[:], WC[:], 1.0 / math.sqrt(P), None, ALU.mult).then_inc(dmo.sem, dmo.step("wcs"))
            gains = lambda name: vec[:, COLS[name]:COLS[name] + 8]
            dve.scalar_tensor_tensor(GA, adac[:, 8:16, 0], 1.0, gains("g_mix_pre"), ALU.add, ALU.mult).then_inc(dmo.sem, dmo.step())
            dve.scalar_tensor_tensor(GAC, adac[:, 8:16, 1], 1.0, gains("g_mix_pre"), ALU.add, ALU.mult).then_inc(dmo.sem, dmo.step())
            dve.tensor_tensor(GP, adac[:, 16:24, 0], gains("g_mix_post"), ALU.mult).then_inc(dmo.sem, dmo.step())
            dve.scalar_tensor_tensor(GF, adac[:, 32:40, 0], 1.0, gains("g_ffn_pre"), ALU.add, ALU.mult).then_inc(dmo.sem, dmo.step())
            dve.tensor_tensor(GFP, adac[:, 40:48, 0], gains("g_ffn_post"), ALU.mult).then_inc(dmo.sem, dmo.step())
            dve.drain().then_inc(phase, 1)
            dve.wait_ge(phase, phase_done("dve"))
            def modulated(name, src, gain, tmp, dst_h, dst_l, shift, n=T):
                dve.wait_ge(dn.sem, rstd(name, n))

                def lo(kb):
                    dve.wait_ge(aad.sem, aad.at(("hi", name, kb)))
                    dve.scalar_tensor_tensor(dst_l[:, kb, :n], tmp[kb % 2][:, :n], shift(kb), dst_h[:, kb, :n].bitcast(F32), ALU.add, ALU.subtract).then_inc(dad.sem, dad.step(("lo", name, kb)))

                for kb in range(CB):
                    if kb >= 2:
                        dve.wait_ge(dad.sem, dad.at(("lo", name, kb - 2)))
                    dve.scalar_tensor_tensor(tmp[kb % 2][:, :n], src[:, kb, :n], gain[:, kb:kb + 1], RS[:, :n], ALU.mult, ALU.mult).then_inc(dad.sem, dad.step(("t", name, kb)))
                    if kb >= 1:
                        lo(kb - 1)
                lo(CB - 1)

            dve.wait_ge(in_a, 32)
            modulated("ctx", CX, GAC, CT, chh, chl, lambda kb: adac[:, kb, 1:2], CTX)
            split_run(UCTX, 8)
            dve.drain().then_inc(phase, 1)
            dve.wait_ge(phase, phase_done("dve"))
            modulated("lat", X, GA, TQ, inh, inl, lambda kb: adac[:, kb, 0:1])
            split_run(UIN, 8)
            for m in range(CB):
                dve.wait_ge(lin.sem, lin.at(("bank", "qk", m)))
                dve.tensor_copy(QK[:, m, :], PB[m][:]).then_inc(drt.sem, drt.step(("qk", m)))
            split_run(UIN + 8, 8)
            for tb in range(TB):
                dve.wait_ge(lin.sem, lin.at(("bank", "v", tb)))
                dve.tensor_copy(VL[:, tb, :], PB[tb][:]).then_inc(drt.sem, drt.step(("vl", tb)))
            for m in range(RH):
                dve.wait_ge(art.sem, art.at(("sig", m)))
                dve.tensor_tensor(GS[:, m, :], TQ[m % 2][:], PB[4 + m][:], ALU.mult).then_inc(drt.sem, drt.step(("g", m)))
            split_run(UIN + 16, 4)
            for g in range(4):
                dve.wait_ge(lin.sem, lin.at(("bank", "f", g)))
                dve.tensor_copy(FQ[:, g, :], PB[g][:]).then_inc(drt.sem, drt.step(("fq", g)))
            dve.wait_ge(in_t, 112)
            for m in range(CB):
                dve.wait_ge(prt.sem, prt.at(("rot", m)))
                dve.wait_ge(drt.sem, drt.at(("rope", m - 2) if m >= 2 else ("g", RH - 1)))
                dve.tensor_tensor(TQ[m % 2][:], PB[4 + m % 4][:], SIN[:], ALU.mult).then_inc(drt.sem, drt.step())
                dve.tensor_tensor(QK[:, m, :], QK[:, m, :], COS[:], ALU.mult).then_inc(drt.sem, drt.step())
                k = drt.n
                dve.wait_ge(drt.sem, k)
                dve.tensor_tensor(QK[:, m, :], QK[:, m, :], TQ[m % 2][:], ALU.add).then_inc(drt.sem, drt.step(("rope", m)))
            dve.drain().then_inc(phase, 1)
            dve.wait_ge(phase, phase_done("dve"))
            for g in range(4):
                dve.wait_ge(af.sem, af.at(("hi", g)))
                dve.tensor_tensor(inl[:, 4 + g, :], PB[2 + g % 2][:], inh[:, 4 + g, :].bitcast(F32), ALU.subtract).then_inc(df.sem, df.step(("lo", g)))
            dve.drain().then_inc(phase, 1)
            dve.wait_ge(phase, phase_done("dve"))

            def distances(h):
                if h >= 2:
                    dve.wait_ge(drt.sem, drt.at(("p", h - 2, TB - 1)))
                dve.tensor_scalar(DM[h % 2][:], AFT[:], LG[:, h:h + 1], None, ALU.mult).then_inc(drt.sem, drt.step())
                k = drt.n
                dve.wait_ge(drt.sem, k)
                dve.scalar_tensor_tensor(DM[h % 2][:], BEF[:], LG[:, 4 + h:5 + h], DM[h % 2][:], ALU.mult, ALU.add).then_inc(drt.sem, drt.step(("dm", h)))

            def ret_norm(h):
                dve.wait_ge(art.sem, art.at(("root", h)))
                dve.reciprocal(RR[:], RR[:]).then_inc(drt.sem, drt.step())
                k = drt.n
                dve.wait_ge(drt.sem, k)
                dve.tensor_tensor(RET[h % 2][:], RET[h % 2][:], RR[:], ALU.mult).then_inc(drt.sem, drt.step(("n", h)))
                k = drt.n
                dve.wait_ge(drt.sem, k)
                dve.tensor_tensor(RET[h % 2][:], RET[h % 2][:], GS[:, h, :], ALU.mult).then_inc(drt.sem, drt.step(("ret", h)))
                dve.wait_ge(art.sem, art.at(("hi", h)))
                dve.tensor_tensor(inl[:, h, :], RET[h % 2][:], inh[:, h, :].bitcast(F32), ALU.subtract).then_inc(drt.sem, drt.step(("lo", h)))

            distances(0)
            distances(1)
            for h in range(RH):
                if h >= 1:
                    dve.wait_ge(prt.sem, prt.at(("out", h - 1)))
                for d in range(2):
                    dve.wait_ge(art.sem, art.at(("xi", h, d)))
                    dve.tensor_tensor(QX[d][:], QK[:, h, :], HE[d][:], ALU.mult).then_inc(drt.sem, drt.step(("qx", h, d)))
                dve.wait_ge(art.sem, art.at(("dm", h)))
                for sb in range(TB):
                    dve.wait_ge(prt.sem, prt.at(("s", h, sb)))
                    dve.scalar_tensor_tensor(PSC[sb][:], PB[sb][:], 1.0 / math.sqrt(P), DM[h % 2][:, 384 - P * sb:896 - P * sb], ALU.mult, ALU.mult).then_inc(drt.sem, drt.step(("p", h, sb)))
                if h + 2 < RH:
                    distances(h + 2)
                if h >= 1:
                    ret_norm(h - 1)
            ret_norm(RH - 1)
            dve.drain().then_inc(phase, 1)
            dve.wait_ge(phase, phase_done("dve"))
            split_run(UOUT, 8)
            for m in range(CB):
                dve.wait_ge(lin.sem, lin.at(("bank", "mx", m)))
                dve.tensor_copy(MX[:, m, :], PB[m][:]).then_inc(drt.sem, drt.step(("mx", m)))
            dve.wait_ge(dn.sem, rstd("mx"))

            def add_normed(src, gain, dst, steps, mark):
                for kb in range(CB):
                    dve.scalar_tensor_tensor(src[:, kb, :], src[:, kb, :], gain[:, kb:kb + 1], RS[:], ALU.mult, ALU.mult).then_inc(steps.sem, steps.step(("nx", mark, kb)))
                    if kb >= 1:
                        dve.wait_ge(steps.sem, steps.at(("nx", mark, kb - 1)))
                        dve.tensor_tensor(dst[:, kb - 1, :], dst[:, kb - 1, :], src[:, kb - 1, :], ALU.add).then_inc(steps.sem, steps.step((mark, kb - 1)))
                dve.wait_ge(steps.sem, steps.at(("nx", mark, CB - 1)))
                dve.tensor_tensor(dst[:, CB - 1, :], dst[:, CB - 1, :], src[:, CB - 1, :], ALU.add).then_inc(steps.sem, steps.step((mark, CB - 1)))

            add_normed(MX, GP, X, drt, "x")
            modulated("fp", X, GF, TQ, inh, inl, lambda kb: adac[:, 24 + kb, 0:1])
            dve.drain().then_inc(phase, 1)
            dve.wait_ge(phase, phase_done("dve"))
            dve.wait_ge(spill, 48)
            taps = vec[:, COLS["conv_w"]:COLS["conv_w"] + 176].rearrange("p (a b c) -> p a b c", a=4, b=2)
            row = lambda ap: ap.rearrange("p (r w) -> p r w", w=GRID)

            def gated(s):
                q, name, loop = s.q, s.name, s.loop
                if s.before is not None:
                    dve.wait_ge(dff.sem, prior(dff, "lo", s.before, 1))
                dve.tensor_copy(CWT[q][:], taps[:, :, :, s.blocks]).then_inc(dff.sem, dff.step(("cw", name, q)))
                dve.wait_ge(dff.sem, dff.at(("cw", name, q), loop))
                for j in range(2):
                    for step in range(2):
                        for hf in range(2):
                            m = 2 * j + hf
                            a, b = row(CV[m][:]), row(PB[4 * q + m][:])
                            if step == 0:
                                dve.wait_ge(affn.sem, affn.at(("cv", name, q, m), loop))
                                dve.scalar_tensor_tensor(a[:, :, 1:GRID], b[:, :, 0:GRID - 1], CWT[q][:, 0, hf, j:j + 1], a[:, :, 1:GRID], ALU.mult, ALU.add).then_inc(dff.sem, dff.step(("c1", name, q, m)))
                            else:
                                dve.wait_ge(dff.sem, dff.at(("c1", name, q, m), loop))
                                dve.scalar_tensor_tensor(a[:, :, 0:GRID - 1], b[:, :, 1:GRID], CWT[q][:, 2, hf, j:j + 1], a[:, :, 0:GRID - 1], ALU.mult, ALU.add).then_inc(dff.sem, dff.step(("cv", name, q, m)))
                for j in range(2):
                    dve.wait_ge(affn.sem, affn.at(("sg", name, q, j), loop))
                    dve.wait_ge(dff.sem, dff.at(("cv", name, q, 2 * j + 1), loop))
                    dve.tensor_tensor(HT[j][:], SG[j][:], CV[2 * j + 1][:], ALU.mult).then_inc(dff.sem, dff.step(("h", name, q, j)))
                for j in range(2):
                    dve.wait_ge(affn.sem, affn.at(("hh", name, q, j), loop))
                    dve.tensor_tensor(GL[:, s.at[j]], HT[j][:], GH[:, s.at[j]].bitcast(F32), ALU.subtract).then_inc(dff.sem, dff.step(("lo", name, q, j)))

            up_passes(dve, "dve", split_run, gated)
            split_run(UF + 44, NFB - 3)
            for m in (4, 5, 6, 7, 0, 1, 2, 3):
                dve.wait_ge(lin.sem, lin.at(("bank", "down", m)))
                dve.tensor_copy(FO[:, m, :], PB[m][:]).then_inc(dff.sem, dff.step(("fo", m)))
            dve.wait_ge(dn.sem, rstd("fo"))
            dve.wait_ge(fill, 48)
            add_normed(FO, GFP, X2, dff, "out")

        @block.tensor
        def _(pe):
            pn, pl = STEP["pe_norm"], STEP["pe_lora"]

            def sums(name, n=T):
                for kb in range(CB):
                    pe.wait_ge(STEP["act_norm"].sem, STEP["act_norm"].at(("sq", name, kb)))
                    pe.matmul(PB[0][:, :n], sq("ones"), SQT[kb % 2][:, :n], start=kb == 0, stop=kb == CB - 1).then_inc(pn.sem, pn.step(("sum", name, kb)))

            def product(o, u, wc, xh, xl_, start, stop):
                w, r = whi[u % SLOTS], wlo[u % SLOTS]
                pe.matmul(o, w[:, wc], xh, start=start, stop=False)
                pe.matmul(o, w[:, wc], xl_, start=False, stop=False)
                return pe.matmul(o, r[:, wc], xh, start=False, stop=stop)

            def token_product(o, u, wc, xh, xl_, start, stop):
                w, r = whi[u % SLOTS], wlo[u % SLOTS]
                pe.matmul(o, xh, w[:, wc], start=start, stop=False)
                pe.matmul(o, xl_, w[:, wc], start=False, stop=False)
                return pe.matmul(o, xh, r[:, wc], start=False, stop=stop)

            pe.wait_ge(in_k, 16)
            sums("n0")
            n = q = 0
            pe.wait_ge(in_c, 16 * 9)
            pe.wait_ge(STEP["pool_prep"].sem, STEP["pool_prep"].at("zero rows"))
            for j, (name, w1, width) in enumerate((("g", lg1, LORA_G), ("w", lw1, LORA_W), ("a", la1, LORA_A))):
                if j == 0:
                    pe.wait_ge(STEP["act_norm"].sem, STEP["act_norm"].at(("root", "n0")))
                else:
                    pe.wait_ge(STEP["act_lora"].sem, STEP["act_lora"].at(("hid", "gwa"[j - 1], 1 if j == 1 else 0)))
                for kb in range(CB):
                    pe.wait_ge(STEP["dve_lora"].sem, STEP["dve_lora"].at(("x", n)))
                    mm = pe.matmul(PB[0][0:min(width, P), :], w1[:, kb, 0:min(width, P)], xl[n % 4][:], start=kb == 0, stop=kb == CB - 1)
                    if width > P:
                        mm = pe.matmul(PB[1][0:width - P, :], w1[:, kb, P:width], xl[n % 4][:], start=kb == 0, stop=kb == CB - 1)
                    mm.then_inc(pl.sem, pl.step(("used", n), *([("hid", name)] if kb == CB - 1 else [])))
                    n += 1
                pe.wait_ge(STEP["act_lora"].sem, STEP["act_lora"].at(("hid", name, 1 if width > P else 0)))
                for m in range(CB):
                    if q >= 6:
                        pe.wait_ge(STEP["act_lora"].sem, STEP["act_lora"].at(("out", "gwa"[(q - 6) // 8], (q - 6) % 8)))
                    o = PB[2 + q % 6]
                    ms = slice(m * P, (m + 1) * P)
                    if name == "g":
                        pe.matmul(o[:], lg2a[:, ms], hid1[0][:], start=True, stop=False)
                        mm = pe.matmul(o[:], lg2b[:, ms], hid1[1][:], start=False, stop=True)
                    else:
                        w2 = lw2 if name == "w" else la2
                        mm = pe.matmul(o[:], w2[:, ms], hid1[0][:], start=True, stop=True)
                    mm.then_inc(pl.sem, pl.step(("out", name, m), *([("outs", name)] if m == CB - 1 else [])))
                    q += 1
            pe.drain().then_inc(phase, 1)
            pe.wait_ge(phase, phase_done("pe"))
            for u in range(24):
                p, kb = divmod(u, 8)
                pe.wait_ge(STEP["dve_mix"].sem, STEP["dve_mix"].at(("lo", u)))
                pe.wait_ge(w_lo, u + 1)
                for m in range(CB):
                    if kb == 0 and p > 0:
                        pe.wait_ge(STEP["dve_mix"].sem, STEP["dve_mix"].at(("taken", p - 1, m)))
                    product(PB[m][:], u, chunk(m), xmh[u % NR][:], xml[u % NR][:], kb == 0, kb == 7).then_inc(
                        lin.sem, lin.step(("bank", p, m), ("used", u)))
            pe.drain().then_inc(phase, 1)
            pe.wait_ge(phase, phase_done("pe"))

            pp, ps, pi, pt, pr, pg = (STEP["pe_" + n] for n in ("prep", "score", "inv", "tok", "rec", "gn"))
            for cb in range(CB):
                pe.wait_ge(STEP["act_prep"].sem, STEP["act_prep"].at(("ksq", cb)))
                pe.matmul(PB[0][0:HEADS, :], sel[:, cb, :], PREP["e1"][cb % 2][:], start=cb == 0, stop=cb == CB - 1).then_inc(pp.sem, pp.step(("ksum", cb)))
            pe.wait_ge(STEP["dve_prep"].sem, STEP["dve_prep"].at("kni"))
            for cb in range(CB + 1):
                if cb < CB:
                    if cb >= 2:
                        pe.wait_ge(STEP["dve_prep"].sem, STEP["dve_prep"].at(("kn", cb - 2)))
                    pe.matmul(PB[1 + cb % 2][:], selt[:, chunk(cb)], KNI[:], start=True, stop=True).then_inc(pp.sem, pp.step(("bc", cb)))
                if cb > 0:
                    pe.wait_ge(STEP["dve_prep"].sem, STEP["dve_prep"].at(("rk", cb - 1)))
                    pe.matmul(PB[3][0:HEADS, :], sel[:, cb - 1, :], PREP["rk"][(cb - 1) % 2][:], start=cb == 1, stop=cb == CB).then_inc(pp.sem, pp.step(("rks", cb - 1)))
            pe.drain().then_inc(phase, 1)
            pe.wait_ge(phase, phase_done("pe"))

            last_taken = {0: None, 1: None}

            def scores(c, half):
                b = BD[half]
                STEP_ = STEP["act_bd"]
                for kind, (a, r) in enumerate(((AT, 1), (BT, 0), (KT, 0), (BT, 2), (KT, 2))):
                    for z in range(2):
                        if last_taken[z] is not None:
                            pe.wait_ge(last_taken[z][0].sem, last_taken[z][0].at(last_taken[z][1]))
                        pe.wait_ge(STEP_.sem, STEP_.at((c, half, r)))
                        for s in range(2):
                            cb = 4 * half + 2 * z + s
                            mm = pe.matmul(PB[z][:, 256 * s:256 * s + 256], a[:, cb, chunk(c)], b[r][:, 2 * z + s, :, :], start=True, stop=True)
                        mm.then_inc(ps.sem, ps.step((c, half, kind, z)))
                        last_taken[z] = (STEP["dve_score"], ("taken", c, half, kind, z))

            def inverse(c, half):
                for lv in range(LEVELS):
                    for p in range(2):
                        g = 2 * half + p
                        pe.wait_ge(STEP["pool_score"].sem, STEP["pool_score"].at(("lm", c, half, lv, p)))
                        if lv > 0:
                            pe.wait_ge(STEP["dve_inv"].sem, STEP["dve_inv"].at(("z", c, half, lv - 1, p)))
                        for s in range(4):
                            mm = pe.matmul(PB[2 + p][:, chunk(s)], LM[p][:, chunk(s)], ZI[:, g, chunk(s)], start=True, stop=True)
                        mm.then_inc(pi.sem, pi.step(("q", c, half, lv, p)))
                    for p in range(2):
                        g = 2 * half + p
                        pe.wait_ge(STEP["act_inv"].sem, STEP["act_inv"].at(("q", c, half, lv, p)))
                        for s in range(4):
                            if lv < LEVELS - 1:
                                pe.matmul(PB[4 + p][:, chunk(s)], QS[p][:, chunk(s)], TI[p][:, chunk(s)], start=True, stop=True)
                            mm = pe.matmul(PB[6 + p][:, chunk(s)], TI[p][:, chunk(s)], QS[p][:, chunk(s)], start=True, stop=True)
                        mm.then_inc(pi.sem, pi.step(("tz", c, half, lv, p)))

            def token_major(c):
                for which, src in (("v", V), ("k", KT), ("b", BT)):
                    for half in range(2):
                        pe.wait_ge(last_taken[half][0].sem, last_taken[half][0].at(last_taken[half][1]))
                        for s in range(4):
                            mm = pe.transpose(PB[half][:, chunk(s)], src[:, 4 * half + s, chunk(c)], sq("ident"))
                        mm.then_inc(pt.sem, pt.step(("tr", c, which, half)))
                        last_taken[half] = (STEP["act_tok"], ("tr", c, which, half))

            for c in range(TB):
                for half in range(2):
                    scores(c, half)
                    inverse(c, half)
                token_major(c)
                for h in range(2):
                    for p in range(2):
                        pe.wait_ge(STEP["dve_inv"].sem, STEP["dve_inv"].at(("z", c, h, LEVELS - 1, p)))
                for which in "vkb":
                    for h in range(2):
                        pe.wait_ge(STEP["act_tok"].sem, STEP["act_tok"].at(("tr", c, which, h)))
                for i in range(CB + 2):
                    if i < CB:
                        p = i % 2
                        pe.wait_ge(STEP["dve_rec"].sem, STEP["dve_rec"].at(("sm", c, i)))
                        if i >= 2:
                            pe.wait_ge(STEP["act_rec"].sem, STEP["act_rec"].at(("w", c, i - 2)))
                        o = PB[2 + p]
                        pe.matmul(o[:, 0:P], AT[:, i, chunk(c)], SM[i % 4][:], start=True, stop=False)
                        for h in range(2):
                            mm = pe.matmul(o[:, 0:P], MT[:, i // 2, chunk(2 * (i % 2) + h)], VT[:, i, h:h + 2, :], start=False, stop=h == 1)
                        mm.then_inc(pr.sem, pr.step(("w", c, i)))
                    if 1 <= i <= CB:
                        cb = i - 1
                        p = cb % 2
                        pe.wait_ge(STEP["act_rec"].sem, STEP["act_rec"].at(("w", c, cb)))
                        if cb >= 2:
                            pe.wait_ge(STEP["dve_rec"].sem, STEP["dve_rec"].at(("u", c, cb - 2)))
                        for h in range(2):
                            mm = pe.matmul(PB[4 + p][:, 0:P], ZI[:, cb // 2, chunk(2 * (cb % 2) + h)], WB[p][:, h:h + 2, :], start=h == 0, stop=h == 1)
                        mm.then_inc(pr.sem, pr.step(("u", c, cb)))
                    if i >= 2:
                        cb = i - 2
                        p = cb % 2
                        pe.wait_ge(STEP["dve_rec"].sem, STEP["dve_rec"].at(("u", c, cb)))
                        if cb >= 2:
                            pe.wait_ge(STEP["dve_rec"].sem, STEP["dve_rec"].at(("s", c, cb - 2)))
                            pe.wait_ge(STEP["act_rec"].sem, STEP["act_rec"].at(("y", c, cb - 2)))
                        pe.matmul(PB[6 + p][:, 0:P], BT[:, cb, chunk(c)], UB[p][:], start=True, stop=False)
                        mm = pe.matmul(PB[6 + p][:, 0:P], KT[:, cb, chunk(c)], VT[:, cb, 0:3:2, :], start=False, stop=True)
                        mm.then_inc(pr.sem, pr.step(("s", c, cb)))
                        pe.matmul(PB[p][:, 0:P], SM[cb % 4][:], RT[:, cb, chunk(c)], start=True, stop=False)
                        for h in range(2):
                            hs = slice(64 * h, 64 * h + 64)
                            pe.matmul(PB[p][hs, 0:P], UB[p][:, hs], GBm[:, cb // 2, chunk(2 * (cb % 2) + h)], start=False, stop=False)
                            mm = pe.matmul(PB[p][hs, 0:P], VT[:, cb, 2 * h, :], GKm[:, cb // 2, chunk(2 * (cb % 2) + h)], start=False, stop=True)
                        mm.then_inc(pr.sem, pr.step(("sy", c, cb)))
                last_taken[0] = (STEP["act_rec"], ("y", c, CB - 2))
                last_taken[1] = (STEP["act_rec"], ("y", c, CB - 1))
            pe.drain().then_inc(phase, 1)
            pe.wait_ge(phase, phase_done("pe"))
            for cb in range(CB):
                if cb >= 4:
                    pe.wait_ge(STEP["dve_gn"].sem, STEP["dve_gn"].at(("yc", cb - 4)))
                pe.matmul(PB[cb % 4][:], sq("blk64"), RT[:, cb, :], start=True, stop=True).then_inc(pg.sem, pg.step(("mean", cb)))
            for cb in range(CB):
                pe.wait_ge(STEP["act_gn"].sem, STEP["act_gn"].at(("sq", cb)))
                pe.matmul(PB[4][0:HEADS, :], sel[:, cb, :], SQT[cb % 2][:], start=cb == 0, stop=cb == CB - 1).then_inc(pg.sem, pg.step(("var", cb)))
            pe.wait_ge(STEP["dve_gn"].sem, STEP["dve_gn"].at("gni"))
            for cb in range(CB):
                if cb >= 2:
                    pe.wait_ge(STEP["dve_gn"].sem, STEP["dve_gn"].at(("t2", cb - 2)))
                pe.matmul(PB[5 + cb % 2][:], selt[0:HEADS, chunk(cb)], KNI[0:HEADS, :], start=True, stop=True).then_inc(pg.sem, pg.step(("bc1", cb)))
                pe.matmul(PB[cb % 2][:], selt[:, chunk(cb)], RKS[:], start=True, stop=True).then_inc(pg.sem, pg.step(("bc2", cb)))
            pe.drain().then_inc(phase, 1)
            pe.wait_ge(phase, phase_done("pe"))
            dmlp = STEP["dve_mlp"]

            def wide(u0, mh, ml, stage, loop=None, ready=None, free=None, zero=None):
                for k in range(CB):
                    if ready is not None:
                        pe.wait_ge(ready[0].sem, ready[0].at((*ready[1], k), loop))
                    pe.wait_ge(w_lo, turn(u0 + k + 1, loop))
                    for m in (*range(1, CB), 0) if k == 0 and zero is not None else range(CB):
                        if k == 0 and free is not None:
                            pe.wait_ge(free[0].sem, free[0].at((*free[1], m), loop, ago=free[2]))
                        if k == 0 and m == 0 and zero is not None:
                            pe.wait_ge(zero[0].sem, zero[0].at(zero[1], loop))
                        product(PB[m][:], u0 + k, chunk(m), mh[:, k, :], ml[:, k, :], k == 0, k == CB - 1).then_inc(
                            lin.sem, lin.step(("bank", stage, m), ("used", u0 + k)))

            def x_sums(name, prev):
                pe.wait_ge(x_sum.sem, x_done(prev, 0))
                sums(name)

            pad, prt, pf = (STEP["pe_" + n] for n in ("ada", "ret", "four"))
            aad, art, af = (STEP["act_" + n] for n in ("ada", "ret", "four"))
            dad, drt, df, dff = (STEP["dve_" + n] for n in ("ada", "ret", "four", "ffn"))

            dmo = STEP["dve_mod"]

            def mlp(layer, u0, name, prev):
                x_sums(name, prev)
                pe.wait_ge(STEP["act_norm"].sem, STEP["act_norm"].at(("root", name)))
                for k in range(CB):
                    pe.wait_ge(STEP["dve_norm"].sem, STEP["dve_norm"].at(("lo", name, k)))
                with turns(pe, "pe", name, 4, 16) as lp:
                    lp.first = u0
                    wide(u0, inh, inl, name + "up", lp, free=(dmlp, ("x", name), 1))
                    if layer == 1:
                        pe.wait_ge(dmlp.sem, dmlp.at(("r", name, 0), lp))
                        pe.wait_ge(dmo.sem, dmo.at(("sum", CB - 1), lp))
                        for b in range(AC // P):
                            for v in range(2 if b < AX_ // P else 1):
                                mm = pe.matmul(PB[0][:, 2 * b + v:2 * b + v + 1], ADS[v][:, chunk(b)], sq("ones")[:, 0:1], start=True, stop=True)
                        mm.then_inc(pad.sem, pad.step("columns"))
                        wide(u0 + 8, hidh, hidl, name, lp, ready=(dmlp, ("hl", name)), free=(dmlp, ("r", name), 0), zero=(dmo, "columns"))
                    else:
                        wide(u0 + 8, hidh, hidl, name, lp, ready=(dmlp, ("hl", name)), free=(dmlp, ("r", name), 0))

            wide(UWO, inh, inl, "wo")
            mlp(0, UM0, "mlp0", "wo")
            pe.drain().then_inc(phase, 1)
            pe.wait_ge(phase, phase_done("pe"))
            pkv, dk = STEP["pe_kv"], STEP["dve_kv"]
            x_sums("kv", "mlp0")
            for j in range(4):
                pe.wait_ge(STEP["dve_norm"].sem, STEP["dve_norm"].at(("lo", "kv", 2 * j + 1)))
                pe.wait_ge(w_lo, UKV + j + 1)
                for a in range(2):
                    for m in range(2):
                        kb = 2 * j + a
                        product(PB[1 + m][:], UKV + j, slice(a * 256 + m * P, a * 256 + (m + 1) * P), inh[:, kb, :], inl[:, kb, :], kb == 0, kb == 7).then_inc(
                            lin.sem, lin.step(("bank", "kv", m), ("used", UKV + j)))
            pe.wait_ge(STEP["act_kv"].sem, STEP["act_kv"].at("ksq"))
            pe.matmul(PB[3][:], sq("blk64"), HS[2][:], start=True, stop=True).then_inc(pkv.sem, pkv.step("kmean"))
            pe.wait_ge(dk.sem, dk.at("vf"))
            for n in range(TB):
                mm = pe.transpose(PB[4][:, chunk(n)], VF[:, chunk(n)], sq("ident"))
            mm.then_inc(pkv.sem, pkv.step("vt"))
            pe.wait_ge(STEP["act_norm"].sem, STEP["act_norm"].at(("root", "kv")))
            pe.wait_ge(STEP["act_kv"].sem, STEP["act_kv"].at("kroot"))
            pe.wait_ge(STEP["act_kv"].sem, STEP["act_kv"].at("vk"))
            wide(UQ, hidh, hidl, "q", ready=(STEP["dve_norm"], ("lo", "q")))
            for cb in range(CB):
                pe.wait_ge(STEP["act_kv"].sem, STEP["act_kv"].at(("qsq", cb)))
                pe.matmul(PB[0][0:HEADS, :], sel[:, cb, :], SQT[cb % 2][:], start=cb == 0, stop=cb == CB - 1).then_inc(pkv.sem, pkv.step(("qsum", cb)))
            pe.wait_ge(dk.sem, dk.at("qni"))
            for cb in range(CB):
                if cb >= 2:
                    pe.wait_ge(dk.sem, dk.at(("qn", cb - 2)))
                pe.matmul(PB[1 + cb % 2][:], selt[:, chunk(cb)], QNI[:], start=True, stop=True).then_inc(pkv.sem, pkv.step(("qbc", cb)))
            pe.wait_ge(kdup, 64)
            pe.drain().then_inc(phase, 1)
            pe.wait_ge(phase, phase_done("pe"))
            pa, aat, da = STEP["pe_att"], STEP["act_att"], STEP["dve_att"]
            NT = 32
            for i in range(NT + 3):
                if i < NT:
                    cb, nn, par = i // 4, (i // 2) % 2, i % 2
                    kd = KD[cb // 4][par]
                    if i >= 4:
                        pe.wait_ge(da.sem, da.at(("taken", i - 4)))
                    for b in range(2):
                        n = 2 * nn + b
                        o = PB[i % 4][:, b * 256:(b + 1) * 256]
                        if n == 0:
                            for z in range(2):
                                mm = pe.matmul(o[:, z * P:(z + 1) * P], QF[:, cb, chunk(0)], kd[:, chunk(0)], start=True, stop=True)
                        else:
                            mm = pe.matmul(o, QF[:, cb, chunk(n)], kd[:, (n - 1) * P:(n + 1) * P], start=True, stop=True)
                    mm.then_inc(pa.sem, pa.step(("s", i)))
                if 2 <= i < NT + 2:
                    k = i - 2
                    pe.wait_ge(da.sem, da.at(("den", k)))
                    if k >= 2:
                        pe.wait_ge(aat.sem, aat.at(("ptr", k - 2)))
                    for j in range(4):
                        mm = pe.transpose(PB[4 + k % 2][:, chunk(j)], S1[k % 3][:, chunk(j)], sq("ident"))
                    mm.then_inc(pa.sem, pa.step(("tr", k)))
                if i >= 3:
                    k = i - 3
                    cb, nn, par = k // 4, (k // 2) % 2, k % 2
                    pr_ = k // 2
                    pe.wait_ge(aat.sem, aat.at(("ptr", k)))
                    if pr_ >= 2 and par == 0:
                        pe.wait_ge(da.sem, da.at(("ol", pr_ - 2)))
                    vs = slice(64 * (cb // 4), 64 * (cb // 4) + 64)
                    for b in range(2):
                        n = 2 * nn + b
                        o = PB[6 + pr_ % 2][64 * par:64 * par + 64, chunk(b)]
                        if n > 0:
                            pe.matmul(o, VK[:, n - 1, vs], PTR[k % 3][:, chunk(2 * b)], start=True, stop=False)
                        mm = pe.matmul(o, VK[:, n, vs], PTR[k % 3][:, chunk(2 * b + 1)], start=n == 0, stop=True)
                    mm.then_inc(pa.sem, pa.step(("pv", k)))
            pe.drain().then_inc(phase, 1)
            pe.wait_ge(phase, phase_done("pe"))
            wide(UBO, inh, inl, "bo")
            mlp(1, UM1, "mlp1", "bo")
            pe.drain().then_inc(phase, 1)
            pe.wait_ge(phase, phase_done("pe"))
            sums("ctx", CTX)
            pe.wait_ge(STEP["act_norm"].sem, STEP["act_norm"].at(("root", "ctx")))
            for k in range(CB):
                pe.wait_ge(dad.sem, dad.at(("lo", "ctx", k)))
                pe.wait_ge(w_lo, UCTX + k + 1)
                for tb in range(2):
                    for hf in range(2):
                        token_product(PB[2 * tb + hf][:], UCTX + k, slice(512 * hf, 512 * hf + 512), chh[:, k, chunk(tb)], chl[:, k, chunk(tb)], k == 0, k == CB - 1).then_inc(
                            lin.sem, lin.step(("bank", "ctx", 2 * tb + hf), ("used", UCTX + k)))
            for tb in range(2):
                pe.wait_ge(art.sem, art.at(("kv", tb)))
            for d in range(2):
                for h in range(RH):
                    for tb in range(2):
                        mm = pe.matmul(PB[4 + d][:, chunk(h)], KW[d][tb][:, chunk(h)], VC[tb][:, chunk(h)], start=tb == 0, stop=tb == 1)
                mm.then_inc(prt.sem, prt.step(("state", d)))
            pe.drain().then_inc(phase, 1)
            pe.wait_ge(phase, phase_done("pe"))
            sums("lat")
            pe.wait_ge(STEP["act_norm"].sem, STEP["act_norm"].at(("root", "lat")))
            wide(UIN, inh, inl, "qk", ready=(dad, ("lo", "lat")))
            for k in range(CB):
                pe.wait_ge(w_lo, UIN + 8 + k + 1)
                for tb in range(TB):
                    if k == 0:
                        pe.wait_ge(drt.sem, drt.at(("qk", tb)))
                    token_product(PB[tb][:], UIN + 8 + k, slice(0, 512), inh[:, k, chunk(tb)], inl[:, k, chunk(tb)], k == 0, k == CB - 1).then_inc(
                        lin.sem, lin.step(("bank", "v", tb)))
                for m in range(RH):
                    if k == 0:
                        pe.wait_ge(drt.sem, drt.at(("qk", 4 + m)))
                    product(PB[4 + m][:], UIN + 8 + k, slice(512 + m * P, 512 + (m + 1) * P), inh[:, k, :], inl[:, k, :], k == 0, k == CB - 1).then_inc(
                        lin.sem, lin.step(("bank", "g", m), ("used", UIN + 8 + k)))
            for j in range(4):
                pe.wait_ge(w_lo, UIN + 16 + j + 1)
                for a in range(2):
                    for g in range(4):
                        kb = 2 * j + a
                        if kb == 0:
                            pe.wait_ge(drt.sem, drt.at(("vl", g)))
                        product(PB[g][:], UIN + 16 + j, slice(a * 512 + g * P, a * 512 + (g + 1) * P), inh[:, kb, :], inl[:, kb, :], kb == 0, kb == 7).then_inc(
                            lin.sem, lin.step(("bank", "f", g), ("used", UIN + 16 + j)))
            for m in range(CB):
                pe.wait_ge(drt.sem, drt.at(("g", m) if m < 4 else ("rope", m - 4)))
                pe.matmul(PB[4 + m % 4][:], sq("rot"), QK[:, m, :], start=True, stop=True).then_inc(prt.sem, prt.step(("rot", m)))
            pe.drain().then_inc(phase, 1)
            pe.wait_ge(phase, phase_done("pe"))
            pe.wait_ge(in_t, 112)
            for g in range(4):
                for tb in range(TB):
                    if g >= 1 and tb % 2 == 0:
                        pe.wait_ge(af.sem, af.at(("ab", g - 1, tb // 2)))
                    mm = pe.matmul(PB[tb // 2][:, 256 * (tb % 2):256 * (tb % 2) + 256], FQ[:, g, chunk(tb)], DFTC[:], start=True, stop=True)
                    if tb % 2:
                        mm.then_inc(pf.sem, pf.step(("ab", g, tb // 2)))
                if g >= 2:
                    pe.wait_ge(af.sem, af.at(("hi", g - 2)))
                    pe.wait_ge(df.sem, df.at(("lo", g - 2)))
                for tb in range(TB):
                    if tb % 2 == 0:
                        pe.wait_ge(af.sem, af.at(("ab", g, tb // 2)))
                    for part in range(2):
                        mm = pe.matmul(PB[2 + g % 2][:], FAB[:, tb, part * P:(part + 1) * P], DFTL[:, part, tb, :], start=tb + part == 0, stop=tb == 3 and part == 1)
                mm.then_inc(pf.sem, pf.step(("f", g)))
            pe.drain().then_inc(phase, 1)
            pe.wait_ge(phase, phase_done("pe"))

            def ret_scores(h):
                for sb in range(TB):
                    if h >= 1:
                        pe.wait_ge(drt.sem, drt.at(("p", h - 1, sb)))
                    pe.matmul(PB[sb][:], QK[:, 4 + h, chunk(sb)], QK[:, h, :], start=True, stop=True).then_inc(prt.sem, prt.step(("s", h, sb)))

            ret_scores(0)
            for h in range(RH):
                if h + 1 < RH:
                    ret_scores(h + 1)
                if h >= 2:
                    pe.wait_ge(art.sem, art.at(("o", h - 2)))
                o = PB[4 + h % 2][:]
                for d in range(2):
                    pe.wait_ge(drt.sem, drt.at(("qx", h, d)))
                    pe.matmul(o, SFB[:, 4 * d + h, :], QX[d][:], start=d == 0, stop=False)
                for sb in range(TB):
                    pe.wait_ge(drt.sem, drt.at(("p", h, sb)))
                    mm = pe.matmul(o, VL[:, sb, chunk(h)], PSC[sb][:], start=False, stop=sb == TB - 1)
                mm.then_inc(prt.sem, prt.step(("out", h)))
                if h >= 1:
                    pe.wait_ge(art.sem, art.at(("root", h - 1)))
                pe.wait_ge(art.sem, art.at(("sq", h)))
                pe.matmul(PB[6][:], sq("ones"), TQ[0][:], start=True, stop=True).then_inc(prt.sem, prt.step(("sum", h)))
            pe.drain().then_inc(phase, 1)
            pe.wait_ge(phase, phase_done("pe"))
            wide(UOUT, inh, inl, "mx")
            sums("mx")
            sums("fp")
            pe.drain().then_inc(phase, 1)
            pe.wait_ge(phase, phase_done("pe"))

            def up_pass(s):
                for k2 in range(4):
                    pe.wait_ge(w_lo, turn(s.u0 + k2 + 1, s.loop))
                    for a in range(2):
                        for m in range(4):
                            kb, c = 2 * k2 + a, a * 512 + (m % 2) * 256 + (m // 2) * P
                            if kb == 0 and s.freed is not None:
                                pe.wait_ge(dff.sem, prior(dff, "cv", s.freed, m))
                            product(PB[4 * s.q + m][:], s.u0 + k2, slice(c, c + P), inh[:, kb, :], inl[:, kb, :], kb == 0, kb == 7).then_inc(
                                lin.sem, lin.step(("bank", s.name, s.q, m), ("used", s.u0 + k2)))

            up_passes(pe, "pe", lambda *a: None, up_pass)
            order = (4, 5, 6, 7, 0, 1, 2, 3)
            for k in range(NFB):
                if k == 0:
                    pe.wait_ge(dff.sem, dff.at(("last", ("lo", "up", 1, 1))))
                if k >= NFB - 2:
                    pe.wait_ge(dff.sem, dff.at(("lo", "up1", 0, k - NFB + 2)))
                pe.wait_ge(w_lo, UF + 44 + k + 1)
                for m in order:
                    if k == 0:
                        pe.wait_ge(dff.sem, dff.at(("last", ("cv", "up", 1, m - 4)) if m >= 4 else ("cv", "up1", 0, m)))
                    product(PB[m][:], UF + 44 + k, chunk(m), GH[:, k * T:(k + 1) * T], GL[:, k * T:(k + 1) * T], k == 0, k == NFB - 1).then_inc(
                        lin.sem, lin.step(("bank", "down", m), ("used", UF + 44 + k)))
            sums("fo")

        @block.gpsimd
        def _(pool):
            pz = STEP["pool_prep"]
            for w, r0 in ((lw2, 64), (la2, 64), (lg2b, 64), (hid1[1], 64)):
                pool.memset(w[r0:P, :], 0.0).then_inc(pz.sem, pz.step())
            pool.memset(lg2b[32:64, :], 0.0).then_inc(pz.sem, pz.step())
            pool.memset(hid1[1][32:64, :], 0.0).then_inc(pz.sem, pz.step("zero rows"))
            pool.drain().then_inc(phase, 1)
            pool.wait_ge(phase, phase_done("pool"))
            pool.drain().then_inc(phase, 1)
            pool.wait_ge(phase, phase_done("pool"))
            po, pc = STEP["pool_prep"], STEP["pool_score"]
            for cb in range(CB):
                p = cb % 2
                pool.wait_ge(STEP["dve_prep"].sem, STEP["dve_prep"].at(("kn", cb)))
                if cb >= 2:
                    pool.wait_ge(po.sem, po.at(("done", cb - 2)))
                pool.tensor_tensor(PREP["t2"][p][:], PREP["kn"][p][:], AA[:, cb, :], ALU.mult).then_inc(po.sem, po.step())
                k = po.n
                pool.wait_ge(STEP["act_prep"].sem, STEP["act_prep"].at(("e1", cb)))
                pool.wait_ge(STEP["dve_prep"].sem, STEP["dve_prep"].at(("rk", cb)))
                pool.tensor_tensor(RT[:, cb, :], R[:, cb, :], PREP["e1"][p][:], ALU.mult).then_inc(po.sem, po.step())
                pool.wait_ge(po.sem, k)
                pool.tensor_tensor(BT[:, cb, :], PREP["t2"][p][:], PREP["e2"][p][:], ALU.mult).then_inc(po.sem, po.step(("done", cb)))
            pool.drain().then_inc(phase, 1)
            pool.wait_ge(phase, phase_done("pool"))
            for half in range(2):
                for r in range(3):
                    pool.memset(BD[half][r][:], 0.0).then_inc(pc.sem, pc.step(("bd", half)))
            for z in (VT, WB[0], WB[1]):
                pool.memset(z[:], 0.0).then_inc(pc.sem, pc.step("gaps"))
            for c in range(TB):
                for half in range(2):
                    for p in range(2):
                        g = 2 * half + p
                        pool.wait_ge(STEP["dve_score"].sem, STEP["dve_score"].at(("taken", c, half, 0, p)))
                        pool.tensor_tensor(quad(LM[p][:]), quad(LL[p][:]), four("lvl0"), ALU.mult).then_inc(pc.sem, pc.step())
                        pool.tensor_tensor(quad(TI[p][:]), quad(TI[p][:]), four("ident"), ALU.add).then_inc(pc.sem, pc.step())
                        pool.wait_ge(STEP["dve_score"].sem, STEP["dve_score"].at(("taken", c, half, 1, p)))
                        pool.tensor_tensor(quad(ZI[:, g, :]), quad(ZI[:, g, :]), four("ident"), ALU.add).then_inc(pc.sem, pc.step(("lm", c, half, 0, p)))
                    for lv in range(1, LEVELS):
                        for p in range(2):
                            pool.wait_ge(STEP["pe_inv"].sem, STEP["pe_inv"].at(("q", c, half, lv - 1, p)))
                            pool.tensor_tensor(quad(LM[p][:]), quad(LL[p][:]), four(f"lvl{lv}"), ALU.mult).then_inc(pc.sem, pc.step(("lm", c, half, lv, p)))
            pool.drain().then_inc(phase, 1)
            pool.wait_ge(phase, phase_done("pool"))
            pq = STEP["pool_gn"]
            pool.wait_ge(fill, 32)
            for cb in range(CB):
                pool.wait_ge(STEP["dve_gn"].sem, STEP["dve_gn"].at(("t3", cb)))
                pool.tensor_tensor(TV[cb % 2][:], TG[cb % 2][:], G2[:, cb, :], ALU.mult).then_inc(pq.sem, pq.step(("o", cb)))
            pool.drain().then_inc(phase, 1)
            pool.wait_ge(phase, phase_done("pool"))

            def mlp(name):
                with turns(pool, "pool", name, 4, 16) as lp:
                    for m in range(CB):
                        pool.wait_ge(STEP["dve_mlp"].sem, STEP["dve_mlp"].at(("r", name, m), lp))
                        if m >= 4:
                            pool.wait_ge(STEP["dve_mlp"].sem, STEP["dve_mlp"].at(("hl", name, m - 4), lp))
                        pool.tensor_tensor(HS[m % 4][:], HR[m % 4][:], HR[m % 4][:], ALU.mult).then_inc(STEP["pool_mlp"].sem, STEP["pool_mlp"].step(("hs", name, m)))

            mlp("mlp0")
            pool.drain().then_inc(phase, 1)
            pool.wait_ge(phase, phase_done("pool"))
            for j in range(2):
                for par in range(2):
                    pool.memset(KD[j][par][:], 0.0).then_inc(STEP["pool_mlp"].sem, STEP["pool_mlp"].step("kd"))
            pool.drain().then_inc(phase, 1)
            pool.wait_ge(phase, phase_done("pool"))
            pool.drain().then_inc(phase, 1)
            pool.wait_ge(phase, phase_done("pool"))
            mlp("mlp1")
            pool.drain().then_inc(phase, 1)
            pool.wait_ge(phase, phase_done("pool"))
            for _ in ("context", "input", "Fourier", "retention", "residual"):
                pool.drain().then_inc(phase, 1)
                pool.wait_ge(phase, phase_done("pool"))


INPUTS = ["a_w_rkv", "a_wo", "mlp_w1", "mlp_w2", "w_kv", "b_wq", "b_wo", "a_w1", "a_w2", "a_a1", "a_a2", "a_g1", "a_g2",
          "w_ada_2", "w_in_2", "w_out_2", "w_up_2", "w_down_2", "ctx"]


def layout(x, a):
    f = lambda v: np.asarray(v)
    arr = {}
    blocks = lambda v: f(v).reshape(-1, P).T
    arr["x"] = np.ascontiguousarray(f(x)[0].T.reshape(CB, P, T).transpose(1, 0, 2))
    arr["ctx"] = np.ascontiguousarray(f(a["ctx_2"])[0].T.reshape(CB, P, CTX).transpose(1, 0, 2))
    twice = lambda v: np.tile(f(v).reshape(-1), 2)[:, None]
    down = lambda v: np.broadcast_to(f(v).reshape(1, -1), (P, f(v).size))
    parts = {
        "ln_mix0": blocks(a["ln_mix"][0]), "ln_mix1": blocks(a["ln_mix"][1]), "ln_mlp0": blocks(a["ln_mlp"][0]),
        "ln_mlp1": blocks(a["ln_mlp"][1]), "mu": blocks(a["a_mu"][0]), "w0": blocks(a["a_w0"][0]), "a0": blocks(a["a_a0"][0]),
        "k_k": blocks(a["a_k_k"][0]), "k_a": blocks(a["a_k_a"][0]), "r_k": blocks(a["a_r_k"][0]), "gn_g": blocks(a["a_gn_g"][0]),
        "gn_b": blocks(a["a_gn_b"][0]), "kv_norm": blocks(a["kv_norm"]), "k_gain": twice(a["k_gain"]), "q_gain": twice(a["b_q_gain"][0]),
        "sinks": down(a["b_sinks"][0]), "c": blocks(a["c_2"][0]), "c_ctx": blocks(a["c_ctx_2"]), "b_ada": blocks(a["b_ada_2"][0]),
        "g_mix_pre": blocks(a["g_mix_pre_2"][0]), "g_mix_post": blocks(a["g_mix_post_2"][0]), "g_ffn_pre": blocks(a["g_ffn_pre_2"][0]),
        "g_ffn_post": blocks(a["g_ffn_post_2"][0]),
        "decay": np.concatenate([down(a["ret_decay_fwd_2"][0]), down(a["ret_decay_bwd_2"][0])], 1),
        "conv_w": blocks(a["conv_w_2"][0]), "conv_b": blocks(a["conv_b_2"][0]),
    }
    arr["vec"] = np.ascontiguousarray(np.concatenate([parts[n] for n in COLS], 1))
    assert arr["vec"].shape == (P, N_COLS)
    arr["a_w_rkv"] = f(a["a_w_rkv"])[0]
    for n in ("a_wo", "b_wq", "b_wo", "a_w1", "a_w2", "a_a1", "a_a2", "a_g1", "a_g2", "w_ada_2", "w_in_2", "w_out_2", "w_up_2", "w_down_2"):
        arr[n] = f(a[n])[0]
    up = arr["w_up_2"].reshape(CB // 2, 2, P, 2, NFB // 2, 256)
    arr["w_up_2"] = up.transpose(4, 0, 2, 1, 3, 5).reshape(-1, 1024)
    ada = arr["w_ada_2"]
    arr["w_ada_2"] = np.concatenate([ada[:, c0 + i * n:c0 + (i + 1) * n] for i in range(4) for c0, n in ((0, C // 2), (2 * C, C))], 1)
    for n in ("mlp_w1", "mlp_w2", "w_kv"):
        arr[n] = f(a[n])
    arr.update(constants())
    return {n: np.ascontiguousarray(v) for n, v in arr.items()}


def declare(nc, arr):
    t = {n: nc.dram_tensor(f"in_{n}", v.shape, mybir.dt.from_np(v.dtype), kind="ExternalInput").ap() for n, v in arr.items()}
    out = nc.dram_tensor("out_0", (P, CB, T), F32, kind="ExternalOutput").ap()
    return t, out


def kernel(x, **a):
    import concourse.bacc as bacc
    from concourse.bass_utils import run_bass_kernel_spmd

    arr = layout(x, a)
    book = {}
    for _ in range(2):
        nc = bacc.Bacc("TRN2", target_bir_lowering=False, num_devices=1)
        t, out = declare(nc, arr)
        program(nc, t, out, book)
        book["built"] = True
    r = run_bass_kernel_spmd(nc, [{f"in_{n}": v for n, v in arr.items()}], core_ids=[0])
    y = r.results[0]["out_0"]
    return np.ascontiguousarray(y.transpose(1, 0, 2).reshape(C, T).T)[None]
```
